# Optimizing a Trainium2 kernel written in Bass

```python
import math
import jax, jax.numpy as jnp
from jax import lax
import numpy as np

D_MODEL = 1024
BATCH = 1
SEQ = 2048
DEPTH = 1

MIX_WIDTH = D_MODEL
RG_WIDTH = MIX_WIDTH // 2
RG_BLOCKS = 8
RG_BLOCK = RG_WIDTH // RG_BLOCKS
CONV_WIDTH = 4
C_RG = 8.0
GLA_HEADS = 4
GLA_VAL = MIX_WIDTH - RG_WIDTH
GLA_KEY = GLA_VAL // 2
GLA_DK = GLA_KEY // GLA_HEADS
GLA_DV = GLA_VAL // GLA_HEADS
GATE_RANK = 16
GATE_NORM = 16.0
CHUNK = 64
IN_WIDTH = 2 * RG_WIDTH + 2 * GLA_KEY + 2 * GLA_VAL + GATE_RANK
N_GROUPS = 4
EXPERTS_PER_GROUP = 8
N_EXPERTS = N_GROUPS * EXPERTS_PER_GROUP
TOP_K = 2
D_EXPERT = D_MODEL
EXPERT_BLOCK = 128
EPS = 1e-6

kernel_name = "hymba_rglru_gla_hmoe_layer"

def rmsnorm(x, g):
    xf = x.astype(jnp.float32)
    y = xf * lax.rsqrt(jnp.mean(xf * xf, axis=-1, keepdims=True) + EPS)
    return (y * g.astype(jnp.float32)).astype(x.dtype)

def causal_depthwise_conv(x, w, b):
    c = x.shape[-1]
    y = lax.conv_general_dilated(
        x, w[:, None, :].astype(x.dtype), window_strides=(1,),
        padding=[(CONV_WIDTH - 1, 0)], dimension_numbers=("NWC", "WIO", "NWC"),
        feature_group_count=c)
    return y + b.astype(x.dtype)

def rg_lru(xc, w_a, b_a, w_x, b_x, lam):
    bsz, s, _ = xc.shape
    xf = xc.astype(jnp.float32)
    xh = xf.reshape(bsz, s, RG_BLOCKS, RG_BLOCK)
    r = jax.nn.sigmoid(jnp.einsum('bshi,hij->bshj', xh, w_a.astype(jnp.float32)) + b_a.astype(jnp.float32))
    i = jax.nn.sigmoid(jnp.einsum('bshi,hij->bshj', xh, w_x.astype(jnp.float32)) + b_x.astype(jnp.float32))
    r = r.reshape(bsz, s, RG_WIDTH)
    i = i.reshape(bsz, s, RG_WIDTH)
    log_a = -C_RG * r * jax.nn.softplus(-lam.astype(jnp.float32))
    a = jnp.exp(log_a)
    u = jnp.sqrt(-jnp.expm1(2.0 * log_a)) * (i * xf)

    def combine(e1, e2):
        a1, b1 = e1
        a2, b2 = e2
        return a1 * a2, a2 * b1 + b2

    _, h = lax.associative_scan(combine, (a, u), axis=1)
    return h

def gla_chunked(q, k, v, log_alpha):
    bsz, s, h, dk = q.shape
    dv = v.shape[-1]
    n = s // CHUNK

    def to_chunks(t):
        return t.reshape(bsz, n, CHUNK, h, t.shape[-1]).transpose(1, 0, 3, 2, 4)

    q, k, v, la = to_chunks(q * (dk ** -0.5)), to_chunks(k), to_chunks(v), to_chunks(log_alpha)
    b = jnp.cumsum(la, axis=3)
    b_last = b[:, :, :, -1:, :]
    q_s = q * jnp.exp(b)
    k_s = k * jnp.exp(-b)
    k_end = k * jnp.exp(b_last - b)
    decay = jnp.exp(b_last[:, :, :, 0, :])

    mask = jnp.tril(jnp.ones((CHUNK, CHUNK), dtype=bool))
    att = jnp.einsum('nbhid,nbhjd->nbhij', q_s, k_s)
    att = jnp.where(mask, att, 0.0)
    o_intra = jnp.einsum('nbhij,nbhje->nbhie', att, v)

    def step(state, inp):
        qc, kc, vc, dc = inp
        o = jnp.einsum('bhcd,bhde->bhce', qc, state)
        state = dc[..., None] * state + jnp.einsum('bhcd,bhce->bhde', kc, vc)
        return state, o

    s0 = jnp.zeros((bsz, h, dk, dv), jnp.float32)
    _, o_inter = lax.scan(step, s0, (q_s, k_end, v, decay))
    o = o_intra + o_inter
    return o.transpose(1, 0, 3, 2, 4).reshape(bsz, s, h, dv)

def mixer(hn, w_in, conv_w, conv_b, w_rg_a, b_rg_a, w_rg_x, b_rg_x, rg_lambda, rg_norm,
          w_alpha_up, b_alpha, gla_norm, w_out):
    bsz, s, _ = hn.shape
    proj = hn @ w_in.astype(hn.dtype)
    cuts = np.cumsum([RG_WIDTH, RG_WIDTH, GLA_KEY, GLA_KEY, GLA_VAL, GLA_VAL]).tolist()
    xr, yr, q, k, v, g, a_low = jnp.split(proj, cuts, axis=-1)

    xc = causal_depthwise_conv(xr, conv_w, conv_b)
    h_rg = rg_lru(xc, w_rg_a, b_rg_a, w_rg_x, b_rg_x, rg_lambda)
    y_rg = h_rg * jax.nn.gelu(yr.astype(jnp.float32))
    y_rg = rmsnorm(y_rg, rg_norm)

    gate_logits = a_low.astype(jnp.float32) @ w_alpha_up.astype(jnp.float32) + b_alpha.astype(jnp.float32)
    log_alpha = jax.nn.log_sigmoid(gate_logits) / GATE_NORM
    qh = q.astype(jnp.float32).reshape(bsz, s, GLA_HEADS, GLA_DK)
    kh = k.astype(jnp.float32).reshape(bsz, s, GLA_HEADS, GLA_DK)
    vh = v.astype(jnp.float32).reshape(bsz, s, GLA_HEADS, GLA_DV)
    lah = log_alpha.reshape(bsz, s, GLA_HEADS, GLA_DK)
    o = gla_chunked(qh, kh, vh, lah)
    o = rmsnorm(o, gla_norm) * jax.nn.silu(g.astype(jnp.float32).reshape(bsz, s, GLA_HEADS, GLA_DV))
    y_gla = o.reshape(bsz, s, GLA_VAL)

    y = jnp.concatenate([y_rg, y_gla], axis=-1).astype(hn.dtype)
    return y @ w_out.astype(hn.dtype)

def hierarchical_moe(hn, w_router_group, b_router_group, w_router_expert, b_router_expert,
                     w_exp_gate, w_exp_up, w_exp_down):
    bsz, s, d = hn.shape
    t = bsz * s
    xt = hn.reshape(t, d)
    pg = jax.nn.softmax((xt @ w_router_group.astype(xt.dtype)).astype(jnp.float32)
                        + b_router_group.astype(jnp.float32), axis=-1)
    g_idx = jnp.argmax(pg, axis=-1)
    g_w = jnp.max(pg, axis=-1)
    le = ((xt @ w_router_expert.astype(xt.dtype)).astype(jnp.float32)
          + b_router_expert.astype(jnp.float32)).reshape(t, N_GROUPS, EXPERTS_PER_GROUP)
    le = jnp.take_along_axis(le, g_idx[:, None, None], axis=1)[:, 0]
    pe = jax.nn.softmax(le, axis=-1)
    top_p, top_i = lax.top_k(pe, TOP_K)
    top_p = top_p / jnp.sum(top_p, axis=-1, keepdims=True)
    weights = g_w[:, None] * top_p
    experts = g_idx[:, None] * EXPERTS_PER_GROUP + top_i

    n_assign = t * TOP_K
    e_flat = experts.reshape(n_assign).astype(jnp.int32)
    w_flat = weights.reshape(n_assign)
    tok_flat = jnp.repeat(jnp.arange(t, dtype=jnp.int32), TOP_K)
    order = jnp.argsort(e_flat, stable=True)
    sorted_e = e_flat[order]
    counts = jnp.bincount(e_flat, length=N_EXPERTS).astype(jnp.int32)
    starts = jnp.cumsum(counts) - counts
    padded = ((counts + EXPERT_BLOCK - 1) // EXPERT_BLOCK) * EXPERT_BLOCK
    pends = jnp.cumsum(padded)
    pstarts = pends - padded
    rank = jnp.arange(n_assign, dtype=jnp.int32) - starts[sorted_e]
    dest = pstarts[sorted_e] + rank
    n_blocks = (n_assign + N_EXPERTS * (EXPERT_BLOCK - 1) + EXPERT_BLOCK - 1) // EXPERT_BLOCK
    cap = n_blocks * EXPERT_BLOCK
    slot_tok = jnp.zeros((cap,), jnp.int32).at[dest].set(tok_flat[order])
    slot_w = jnp.zeros((cap,), jnp.float32).at[dest].set(w_flat[order])
    block_start = jnp.arange(n_blocks, dtype=jnp.int32) * EXPERT_BLOCK
    block_e = jnp.clip(jnp.searchsorted(pends, block_start, side='right'), 0, N_EXPERTS - 1)

    xb = xt[slot_tok].reshape(n_blocks, EXPERT_BLOCK, d)

    def expert_block(args):
        xblk, e = args
        wg = w_exp_gate[e].astype(xblk.dtype)
        wu = w_exp_up[e].astype(xblk.dtype)
        wd = w_exp_down[e].astype(xblk.dtype)
        return (jax.nn.gelu(xblk @ wg) * (xblk @ wu)) @ wd

    yb = lax.map(expert_block, (xb, block_e)).reshape(cap, d)
    out = jnp.zeros((t, d), jnp.float32).at[slot_tok].add(yb.astype(jnp.float32) * slot_w[:, None])
    return out.astype(hn.dtype).reshape(bsz, s, d)

def setup_inputs(seed: int = 0) -> dict:
    key = jax.random.key(seed)
    ks = jax.random.split(key, 24)
    f32 = jnp.float32
    nrm = lambda k, shape, scale: jax.random.normal(k, shape, f32) * scale
    u = jax.random.uniform(ks[9], (DEPTH, RG_WIDTH), f32, minval=0.9, maxval=0.999)
    a0 = u ** (1.0 / C_RG)
    rg_lambda = jnp.log(a0) - jnp.log1p(-a0)
    return {
        "x": jax.random.normal(ks[0], (BATCH, SEQ, D_MODEL), f32),
        "norm_mix": 1.0 + nrm(ks[1], (DEPTH, D_MODEL), 0.02),
        "w_in": nrm(ks[2], (DEPTH, D_MODEL, IN_WIDTH), D_MODEL ** -0.5),
        "conv_w": nrm(ks[3], (DEPTH, CONV_WIDTH, RG_WIDTH), CONV_WIDTH ** -0.5),
        "conv_b": nrm(ks[4], (DEPTH, RG_WIDTH), 0.01),
        "w_rg_a": nrm(ks[5], (DEPTH, RG_BLOCKS, RG_BLOCK, RG_BLOCK), RG_BLOCK ** -0.5),
        "b_rg_a": nrm(ks[6], (DEPTH, RG_BLOCKS, RG_BLOCK), 0.01),
        "w_rg_x": nrm(ks[7], (DEPTH, RG_BLOCKS, RG_BLOCK, RG_BLOCK), RG_BLOCK ** -0.5),
        "b_rg_x": nrm(ks[8], (DEPTH, RG_BLOCKS, RG_BLOCK), 0.01),
        "rg_lambda": rg_lambda,
        "rg_norm": 1.0 + nrm(ks[10], (DEPTH, RG_WIDTH), 0.02),
        "w_alpha_up": nrm(ks[11], (DEPTH, GATE_RANK, GLA_KEY), GATE_RANK ** -0.5),
        "b_alpha": nrm(ks[12], (DEPTH, GLA_KEY), 0.01),
        "gla_norm": 1.0 + nrm(ks[13], (DEPTH, GLA_DV), 0.02),
        "w_out": nrm(ks[14], (DEPTH, MIX_WIDTH, D_MODEL), MIX_WIDTH ** -0.5),
        "norm_ffn": 1.0 + nrm(ks[15], (DEPTH, D_MODEL), 0.02),
        "w_router_group": nrm(ks[16], (DEPTH, D_MODEL, N_GROUPS), D_MODEL ** -0.5),
        "b_router_group": nrm(ks[17], (DEPTH, N_GROUPS), 0.01),
        "w_router_expert": nrm(ks[18], (DEPTH, D_MODEL, N_EXPERTS), D_MODEL ** -0.5),
        "b_router_expert": nrm(ks[19], (DEPTH, N_EXPERTS), 0.01),
        "w_exp_gate": nrm(ks[20], (DEPTH, N_EXPERTS, D_MODEL, D_EXPERT), D_MODEL ** -0.5),
        "w_exp_up": nrm(ks[21], (DEPTH, N_EXPERTS, D_MODEL, D_EXPERT), D_MODEL ** -0.5),
        "w_exp_down": nrm(ks[22], (DEPTH, N_EXPERTS, D_EXPERT, D_MODEL), D_EXPERT ** -0.5),
        "norm_final": 1.0 + nrm(ks[23], (D_MODEL,), 0.02),
    }

def reference(x, norm_mix, w_in, conv_w, conv_b, w_rg_a, b_rg_a, w_rg_x, b_rg_x, rg_lambda,
              rg_norm, w_alpha_up, b_alpha, gla_norm, w_out, norm_ffn, w_router_group,
              b_router_group, w_router_expert, b_router_expert, w_exp_gate, w_exp_up,
              w_exp_down, norm_final):
    h = x
    for l in range(DEPTH):
        hn = rmsnorm(h, norm_mix[l])
        h = h + mixer(hn, w_in[l], conv_w[l], conv_b[l], w_rg_a[l], b_rg_a[l], w_rg_x[l],
                      b_rg_x[l], rg_lambda[l], rg_norm[l], w_alpha_up[l], b_alpha[l],
                      gla_norm[l], w_out[l])
        hn = rmsnorm(h, norm_ffn[l])
        h = h + hierarchical_moe(hn, w_router_group[l], b_router_group[l], w_router_expert[l],
                                 b_router_expert[l], w_exp_gate[l], w_exp_up[l], w_exp_down[l])
    return rmsnorm(h, norm_final)


_drawn_inputs = setup_inputs


def setup_inputs(seed=0):
    import zlib

    import numpy as np

    out = dict(_drawn_inputs(seed))
    spreads = {}
    factors = {'b_rg_a': 33.571,
     'b_rg_x': 30.403,
     'b_alpha': 8.0,
     'gla_norm': 3.811,
     'b_router_group': 21.077,
     'b_router_expert': 12.573,
     'norm_final': 8.463,
     'rg_norm': 4.533,
     'norm_ffn': 3.444}
    for name, (base, spread) in spreads.items():
        noise = np.random.default_rng([zlib.crc32(name.encode()), seed]).standard_normal(out[name].shape)
        drawn = base * np.exp(spread * noise) if base else spread * noise
        out[name] = __import__('jax').numpy.asarray(drawn.astype(out[name].dtype))
    for name, factor in factors.items():
        out[name] = (out[name] * factor).astype(out[name].dtype)
    return out
```

```python
from contextlib import ExitStack

import concourse.bass as bass
from concourse import mybir

F32 = mybir.dt.float32
F32R = mybir.dt.float32r
I32 = mybir.dt.int32
U32 = mybir.dt.uint32
ALU = mybir.AluOpType
ACT = mybir.ActivationFunctionType
AX = mybir.AxisListType.X

P = 128
D = 1024
SEQ = 2048
KT = D // P
RG = 512
CT = RG // P
CONV = 4
HEADS = 4
DK = 64
DV = 128
HP = HEADS * DK // P
RANK = 16
CHUNK = 64
GT = 512
GROUPS = SEQ // GT
TT = GT // P
TILES = SEQ // P
NCH = GT // CHUNK
NG = 4
EPG = 8
NE = NG * EPG
NR = NG + NE
EPS = 1e-6
BLOCKS = (SEQ * 2 + NE * (P - 1) + P - 1) // P
SLOTS = (BLOCKS + 1) * P
GATE_NORM = 16.0
C_RG = 8.0

COL_X, COL_Y, COL_Q, COL_K, COL_V, COL_G, COL_A = 0, 512, 1024, 1280, 1536, 2048, 2560
IN_W = 2576


class Steps:

    def __init__(self, sem, known):
        self.sem, self.known = sem, known
        self.n, self.base, self.per, self.g = 0, 0, None, None
        self.marks = {}

    def begin_loop(self, g):
        self.base, self.n, self.g = self.n, 0, g
        self.ahead, self.marks = self.marks, {}

    def tick(self, name=None):
        self.n += 1
        if name is not None:
            assert name not in self.marks, name
            self.marks[name] = self.n
        return self.sem, 1

    def now(self):
        if self.g is None:
            return self.sem, self.n
        return self.sem, self.base + self.known.get("per", 1) * self.g + self.n

    def at(self, name, g):
        return self.sem, self.known.get("base", 0) + self.known.get("per", 1) * g + self.known.get(name, 1)

    def before(self, name):
        return self.sem, self.known.get("ahead", {}).get(name, 1)

    def table(self):
        return {**self.marks, "base": self.base, "per": self.n, "ahead": self.ahead}


RESULTS = ([(f"T{k}", "AV"[k % 2]) for k in range(KT)]
           + [(f"X{c}", "A") for c in range(CT)] + [("AL", "A")]
           + [(f"V{t}", "A") for t in range(TT)] + [("L0", "V"), ("L1", "V")]
           + [("GA0", "A"), ("GX0", "A")] + [(n, "V") for n in ("Q0", "Q1", "K0", "K1")]
           + [("GA1", "A"), ("GX1", "A")] + [(f"Y{c}", "A") for c in range(CT)]
           + [("GA2", "A"), ("GX2", "A"), ("G0", "V"), ("G1", "V")]
           + [("GA3", "A"), ("GX3", "A"), ("G2", "V"), ("G3", "V"), ("KE0", "V"), ("KE1", "V"), ("SS", "V")]
           + [(f"YT{t}", "A") for t in range(TT)]
           + [r for t in range(TT) for r in
              ([(f"O{t}{n}{h}", "V") for n in range(2) for h in "rg"]
               + ([(f"H{t-1}{q}", "AV"[q]) for q in range(2)] + [(f"R{t-1}", "V")] if t else []))]
           + [(f"H{TT-1}{q}", "AV"[q]) for q in range(2)] + [(f"R{TT-1}", "V")])
ORDER = [r for r, _ in RESULTS]
EMPTIED_BY = dict(RESULTS)


def build(nc, T, known):
    tables = {}
    x_rows = T["x"].rearrange("b s d -> (b s) d")
    out_rows = T["out"].rearrange("b s d -> (b s) d")
    w_in = T["w_in"][0].rearrange("(k p) n -> p k n", p=P)
    h_dram = nc.dram_tensor("h_rows", (SEQ, D), F32, kind="Internal").ap()
    hn_dram = nc.dram_tensor("hn_rows", (SEQ, D), F32, kind="Internal").ap()
    slot_dram = nc.dram_tensor("slot_rows", (SLOTS, 2), I32, kind="Internal").ap()
    y_dram = nc.dram_tensor("y_rows", (2 * SEQ + SLOTS, D), F32, kind="Internal").ap()

    with ExitStack() as ctx:
        def keep_sb(name, shape, dt=F32):
            return ctx.enter_context(nc.sbuf_tensor(name, shape, dt))

        def sem(name):
            return ctx.enter_context(nc.semaphore(name))

        ident = keep_sb("ident", [P, P])
        ones = keep_sb("ones", [P, P])
        logits = keep_sb("logits", [P, TILES, NR])
        mixer(nc, T, known, tables, x_rows, w_in, h_dram, hn_dram, ident, ones, logits, sem)
        dest = keep_sb("dest", [P, TILES, 2], I32)
        wts = keep_sb("wts", [P, TILES, 2])
        btab = keep_sb("btab", [P, 2 * (BLOCKS + 1) + 1], I32)
        route(nc, slot_dram, ident, ones, logits, dest, wts, btab, sem)
        experts(nc, T, slot_dram, hn_dram, y_dram, ident, btab, sem)
        combine(nc, T, h_dram, y_dram, out_rows, wts, sem)
    return tables


def mixer(nc, T, known, tables, x_rows, w_in, h_dram, hn_dram, ident, ones, logits, sem):
    with ExitStack() as ctx:
        def sb(name, shape, dt=F32):
            return ctx.enter_context(nc.sbuf_tensor(name, shape, dt))

        def ps(name, shape, dt=F32):
            return ctx.enter_context(nc.psum_tensor(name, shape, dt))

        wout = sb("wout", [P, KT, D])
        wal = sb("wal", [P, KT, RANK])
        wup = sb("wup", [RANK, HP * P])
        wrt = sb("wrt", [P, KT, NR])
        bd = sb("bd", [P, 2, CT, P])
        nmix = sb("nmix", [P, KT])
        nffn = sb("nffn", [P, D])
        cw = sb("cw", [P, CT, CONV])
        cb = sb("cb", [P, CT])
        gb = sb("gb", [P, 2, CT])
        lam = sb("lam", [P, CT])
        sp = sb("sp", [P, 4, CT])
        rgn = sb("rgn", [P, CT])
        glan = sb("glan", [P, 1])
        bal = sb("bal", [P, HP])
        rbias = sb("rbias", [P, NR])
        keepm = sb("keepm", [P, HEADS * P], U32)
        restart = sb("restart", [P, GT])
        ring = sb("ring", [P, 4, KT, P])
        wvg = sb("wvg", [P, KT, RG])
        xs = sb("xs", [P, TT, D])
        hnT = sb("hnT", [P, KT, GT])
        xr = sb("xr", [P, CT, GT + CONV - 1])
        xc = sb("xc", [P, CT, GT])
        yr = sb("yr", [P, CT, GT])
        rg_tmp = sb("rg_tmp", [P, 5, GT])
        rt, it, at_, th, uu = (rg_tmp[:, i] for i in range(5))
        junk = rg_tmp[:, 0:2].rearrange("p a b -> p (a b)")
        hcar = sb("hcar", [P, CT])
        alow = uu[0:RANK]
        qk = sb("qk", [P, 4, GT])
        ks = sb("ks", [P, HP, GT])
        z1 = sb("z1", [P, HP, GT])
        attmask = z1[:, 0]
        z2 = sb("z2", [P, HP, GT])
        bb = sb("bb", [P, HP, GT])
        dc = sb("dc", [P, HP, NCH])
        keT = sb("keT", [P, TT, HP * P])
        vt = sb("vt", [P, TT, RG])
        sg = sb("sg", [P, TT, RG])
        att = sb("att", [P, 2, HEADS * P])
        st = sb("st", [P, 2, HP, DV])
        ot = sb("ot", [P, TT, RG])
        hres = [hnT[:, 6:8, :].rearrange("p a b -> p (a b)"), bb[:].rearrange("p a b -> p (a b)")]
        stat = sb("stat", [P, 96])
        hn2 = [hnT[:, 2 + 2 * i:4 + 2 * i, :].rearrange("p a b -> p (a b)") for i in range(2)]
        hn2T = hnT[:, 0:2, :].rearrange("p a (b t) -> p (a b) t", t=P)
        big = [ps(f"big{i}", [P, 512]) for i in range(4)]
        attp = [ps(f"attp{i}", [P, HEADS * P]) for i in range(2)]
        kvp = ps("kvp", [P, 2, HP, DV])
        op = ps("op", [P, HEADS * DV])

        consts_in = sem("m_consts_in")
        wout_in = sem("m_wout_in")
        consts_made = sem("m_consts_made")
        wout_scaled = sem("m_wout_scaled")
        wring_in = [sem(f"m_wring_in{i}") for i in range(4)]
        wvg_in = sem("m_wvg_in")
        x_in = sem("m_x_in")
        hres_in = [sem(f"m_hres_in{i}") for i in range(2)]
        h_out = [sem(f"m_h_out{i}") for i in range(2)]
        hn_ready = sem("m_hn_ready")
        hn_stat = sem("m_hn_stat")
        hn_rs = sem("m_hn_rs")
        group_done = sem("m_group_done")
        prep = sem("m_prep")
        passed_p = sem("m_passed_p")
        passed_s = sem("m_passed_s")
        passed_v = sem("m_passed_v")
        S = {k: Steps(sem(f"m_steps_{k}"), known.get(k, {})) for k in "PAV"}
        PE_, A_, V_ = S["P"], S["A"], S["V"]

        def now_in(E, g):
            return E.now()

        block = ctx.enter_context(nc.Block())
        tile_cols = ([COL_X + c * P for c in range(CT)] + [COL_Q + c * P for c in range(HP)]
                     + [COL_K + c * P for c in range(HP)] + [COL_Y + c * P for c in range(CT)])
        tile_names = [f"X{c}" for c in range(CT)] + ["Q0", "Q1", "K0", "K1"] + [f"Y{c}" for c in range(CT)]

        N_CONST = 15 + CONV + 4

        @block.sync
        def _(sync):
            def ring_load(i):
                c = tile_cols[i % 12]
                sync.dma_start(ring[:, i % 4], w_in[:, :, c:c + P]).then_inc(wring_in[i % 4], 16)

            def const(dst, src):
                sync.dma_start(dst, src, allow_slow_non_contiguous=True).then_inc(consts_in, 16)

            sync.dma_start(xs[:], x_rows[0:GT].rearrange("(t p) d -> p t d", p=P)).then_inc(x_in, 16)
            for i in range(4):
                ring_load(i)
            sync.dma_start(wvg[:], w_in[:, :, COL_V:COL_V + RG]).then_inc(wvg_in, 16)
            const(nmix[:], T["norm_mix"][0].rearrange("(k p) -> p k", p=P))
            const(nffn[:], T["norm_ffn"].partition_broadcast(P))
            const(wal[:], w_in[:, :, COL_A:COL_A + RANK])
            const(wup[:], T["w_alpha_up"][0])
            const(cb[:], T["conv_b"][0].rearrange("(c p) -> p c", p=P))
            const(gb[:, 0], T["b_rg_a"][0].rearrange("(c b) i -> (b i) c", b=2))
            const(gb[:, 1], T["b_rg_x"][0].rearrange("(c b) i -> (b i) c", b=2))
            const(lam[:], T["rg_lambda"][0].rearrange("(c p) -> p c", p=P))
            const(rgn[:], T["rg_norm"][0].rearrange("(c p) -> p c", p=P))
            const(glan[:], T["gla_norm"][0].rearrange("(p a) -> p a", a=1))
            const(bal[:], T["b_alpha"][0].rearrange("(c p) -> p c", p=P))
            const(wrt[:, :, 0:NG], T["w_router_group"][0].rearrange("(k p) n -> p k n", p=P))
            const(wrt[:, :, NG:NR], T["w_router_expert"][0].rearrange("(k p) n -> p k n", p=P))
            const(rbias[:, 0:NG], T["b_router_group"].partition_broadcast(P))
            const(rbias[:, NG:NR], T["b_router_expert"].partition_broadcast(P))
            for j in range(CONV):
                sync.dma_start(cw[:, :, j], T["conv_w"][0, j].rearrange("(c p) -> p c", p=P),
                               allow_slow_non_contiguous=True).then_inc(consts_in, 16)
            sync.wait_ge(prep, 1)
            for i, w in enumerate(("w_rg_a", "w_rg_x")):
                for b in range(2):
                    src = T[w][0].rearrange("(c b) i j -> b i c j", b=2)[b]
                    const(bd[b * 64:(b + 1) * 64, i, :, b * 64:(b + 1) * 64], src)
            sync.dma_start(wout[:], T["w_out"][0].rearrange("(k p) n -> p k n", p=P)).then_inc(wout_in, 16)

            with sync.Fori(0, GROUPS) as g:
                sync.wait_ge(*PE_.at("T7", g))
                nx = ((g + 1) % GROUPS) * GT
                sync.dma_start(xs[:], x_rows[bass.ds(nx, GT), :].rearrange("(t p) d -> p t d", p=P)).then_inc(x_in, 16)
                for i in range(4):
                    sync.wait_ge(*PE_.at(tile_names[i], g))
                    ring_load(i + 4)
                sync.wait_ge(*PE_.at("V3", g))
                sync.dma_start(wvg[:], w_in[:, :, COL_G:COL_G + RG]).then_inc(wvg_in, 16)
                for i in range(4, 12):
                    sync.wait_ge(*PE_.at(tile_names[i], g))
                    ring_load(i + 4)
                sync.wait_ge(*PE_.at("G3", g))
                sync.dma_start(wvg[:], w_in[:, :, COL_V:COL_V + RG]).then_inc(wvg_in, 16)
                sync.wait_ge(*V_.at("ke", g))
                for t in range(2):
                    sync.dma_start(hres[t], x_rows[bass.ds(g * GT + t * P, P), :]).then_inc(hres_in[t], 16)
                for t in range(TT):
                    sync.wait_ge(*V_.at(f"h{t}", g))
                    sync.dma_start(h_dram[bass.ds(g * GT + t * P, P), :], hres[t % 2]).then_inc(h_out[t % 2], 16)
                    sync.wait_ge(*V_.at(f"hn{t}", g))
                    sync.dma_start(hn_dram[bass.ds(g * GT + t * P, P), :], hn2[t % 2]).then_inc(h_out[t % 2], 16)
                    if t + 2 < TT:
                        sync.wait_ge(h_out[t % 2], 64 * g + 32)
                        sync.dma_start(hres[t % 2], x_rows[bass.ds(g * GT + (t + 2) * P, P), :]).then_inc(hres_in[t % 2], 16)
                for i in range(2):
                    sync.wait_ge(h_out[i], 64 * (g + 1))
                sync.sem_inc(passed_s, 1)
            sync.wait_ge(x_in, 16 * (GROUPS + 1))
            sync.wait_ge(wvg_in, 16 * (2 * GROUPS + 1))
            for i in range(4):
                sync.wait_ge(wring_in[i], 16 * (3 * GROUPS + 1))

        @block.gpsimd
        def _(pool):
            nc.gpsimd.memset(bd[:], 0.0).then_inc(prep, 1)
            nc.gpsimd.memset(ident[:], 0.0).then_inc(consts_made, 1)
            nc.gpsimd.memset(ones[:], 1.0).then_inc(consts_made, 1)
            nc.gpsimd.memset(attmask, 1.0).then_inc(consts_made, 1)
            nc.gpsimd.memset(restart[:], 1.0).then_inc(consts_made, 1)
            pool.wait_ge(consts_made, 4)
            nc.gpsimd.memset(restart[:].rearrange("p (n c) -> p n c", c=CHUNK)[:, :, 0:1], 0.0).then_inc(consts_made, 1)
            nc.gpsimd.affine_select(out=ident[:], in_=ident[:], compare_op=ALU.not_equal, fill=1.0, base=0,
                                    pattern=[[-1, P]], channel_multiplier=1).then_inc(consts_made, 1)
            am = attmask.rearrange("p (h i) -> p h i", h=HEADS)
            nc.gpsimd.affine_select(out=am, in_=am, compare_op=ALU.is_ge, fill=0.0, base=0,
                                    pattern=[[0, HEADS], [1, P]], channel_multiplier=-1).then_inc(consts_made, 1)
            pool.wait_ge(consts_made, 7)
            nc.gpsimd.memset(am[0:CHUNK, :, CHUNK:P], 0.0).then_inc(consts_made, 1)
            pool.wait_ge(consts_in, 16 * N_CONST)
            pool.wait_ge(wout_in, 16)
            for k in range(KT):
                s = rgn[:, k:k + 1] if k < CT else glan[:]
                nc.gpsimd.tensor_scalar(wout[:, k], wout[:, k], s, None, ALU.mult).then_inc(wout_scaled, 1)

        @block.scalar
        def _(act):
            A = A_

            def own():
                act.wait_ge(*A.now())

            act.wait_ge(consts_in, 16 * N_CONST)
            nc.scalar.activation(sp[:, 0], lam[:], ACT.Abs).then_inc(*A.tick("p0"))
            own()
            nc.scalar.activation(sp[:, 1], sp[:, 0], ACT.Exp, scale=-1.0).then_inc(*A.tick("p1"))
            own()
            nc.scalar.activation(sp[:, 2], sp[:, 1], ACT.Ln, bias=1.0).then_inc(*A.tick("p2"))

            def norm_stats(n):
                act.wait_ge(x_in, 16 * (n + 1))
                for t in range(TT):
                    if t:
                        act.wait_ge(hn_stat, (TT + 1) * n + t)
                    nc.scalar.activation(junk, xs[:, t], ACT.Square, accum_out=stat[:, t:t + 1]).then_inc(hn_stat, 1)
                act.wait_ge(hn_rs, 2 * n + 1)
                nc.scalar.activation(stat[:, 8:12], stat[:, 4:8], ACT.Sqrt).then_inc(hn_stat, 1)

            norm_stats(0)

            act.wait_ge(*V_.before("sp"))
            with act.Fori(0, GROUPS) as g:
                A.begin_loop(g)

                def empty(name, dst, **kw):
                    i = ORDER.index(name)
                    func = kw.pop("func", ACT.Copy)
                    act.wait_ge(*PE_.at(name, g))
                    own()
                    nc.scalar.activation(dst, kw.pop("src", big[i % 4][:]), func, **kw).then_inc(*A.tick(kw_name(name)))

                def kw_name(name):
                    return "e:" + name if EMPTIED_BY[name] == "A" else "a:" + name

                for k in range(0, KT, 2):
                    empty(f"T{k}", hnT[:, k], scale=nmix[:, k:k + 1])
                for c in range(CT):
                    empty(f"X{c}", xr[:, c, CONV - 1:])
                empty("AL", alow, src=big[ORDER.index("AL") % 4][0:RANK, :])
                for t in range(TT):
                    empty(f"V{t}", vt[:, t])
                for c in range(HP):
                    empty(f"L{c}", z1[:, c], func=ACT.Abs, bias=bal[:, c:c + 1])
                own()
                nc.scalar.activation(z1[:], z1[:], ACT.Exp, scale=-1.0).then_inc(*A.tick())
                own()
                nc.scalar.activation(z1[:], z1[:], ACT.Ln, bias=1.0).then_inc(*A.tick("ln"))

                def gates(c):
                    if c:
                        act.wait_ge(*V_.at(f"scan{c-1}", g))
                    empty(f"GA{c}", rt, func=ACT.Sigmoid, bias=gb[:, 0, c:c + 1])
                    empty(f"GX{c}", it, func=ACT.Sigmoid, bias=gb[:, 1, c:c + 1])
                    own()
                    nc.scalar.activation(at_, rt, ACT.Exp, scale=sp[:, 0, c:c + 1]).then_inc(*A.tick())
                    nc.scalar.activation(th, rt, ACT.Tanh, scale=sp[:, 3, c:c + 1]).then_inc(*A.tick(f"th{c}"))
                    act.wait_ge(*V_.at(f"oma{c}", g))
                    own()
                    nc.scalar.activation(th, th, ACT.Sqrt).then_inc(*A.tick(f"sq{c}"))

                gates(0)
                act.wait_ge(*V_.at("b", g))
                own()
                nc.scalar.activation(z1[:], bb[:], ACT.Exp, scale=1.0 / GATE_NORM).then_inc(*A.tick("eb"))
                nc.scalar.activation(z2[:], bb[:], ACT.Exp, scale=-1.0 / GATE_NORM).then_inc(*A.tick("enb"))
                last = bb[:].rearrange("p a (n c) -> p a n c", c=CHUNK)[:, :, :, CHUNK - 1]
                nc.scalar.activation(dc[:], last, ACT.Exp, scale=1.0 / GATE_NORM).then_inc(*A.tick("dc"))
                gates(1)
                act.wait_ge(*V_.at("bend", g))
                own()
                nc.scalar.activation(z1[:], z1[:], ACT.Exp, scale=1.0 / GATE_NORM).then_inc(*A.tick("eend"))
                for c in range(CT):
                    empty(f"Y{c}", yr[:, c], func=ACT.Gelu_apprx_tanh)
                gates(2)
                for t in range(2):
                    empty(f"G{t}", sg[:, t], func=ACT.Sigmoid)
                gates(3)
                for t in range(2, TT):
                    empty(f"G{t}", sg[:, t], func=ACT.Sigmoid)
                act.wait_ge(*V_.at(f"scan{CT-1}", g))
                norm_stats(g + 1)
                for c in range(CT):
                    act.wait_ge(*V_.at(f"y{c}", g))
                    own()
                    nc.scalar.activation(xc[:, c], yr[:, c], ACT.Square).then_inc(*A.tick(f"ysq{c}"))
                for t in range(TT):
                    act.wait_ge(*PE_.at(f"o{t}", g))
                    nc.scalar.activation(ot[:, t], op[:], ACT.Copy).then_inc(*A.tick(f"o{t}"))
                    own()
                    for h in range(HEADS):
                        j = 32 + t * HEADS + h
                        nc.scalar.activation(junk[:, 0:DV] if h % 2 else junk[:, DV:2 * DV], ot[:, t, h * DV:(h + 1) * DV],
                                             ACT.Square, accum_out=stat[:, j:j + 1]).then_inc(*A.tick(f"os{t}{h}"))
                        own()
                act.wait_ge(*V_.at("oms", g))
                own()
                nc.scalar.activation(stat[:, 64:84], stat[:, 64:84], ACT.Sqrt).then_inc(*A.tick("ort"))
                for t in range(TT):
                    empty(f"YT{t}", qk[:, :, t * P:(t + 1) * P], src=big[ORDER.index(f"YT{t}") % 4][:].rearrange("p (h t) -> p h t", h=HEADS))
                for t in range(TT + 1):
                    if t < TT:
                        act.wait_ge(*V_.at(f"h{t}", g))
                        own()
                        nc.scalar.activation(junk, hres[t % 2], ACT.Square, accum_out=stat[:, 16 + t:17 + t]).then_inc(*A.tick(f"hsq{t}"))
                        act.wait_ge(*V_.at(f"hms{t}", g))
                        own()
                        nc.scalar.activation(stat[:, 20 + t:21 + t], stat[:, 20 + t:21 + t], ACT.Sqrt).then_inc(*A.tick(f"hrt{t}"))
                    if t:
                        i = ORDER.index(f"H{t-1}0")
                        act.wait_ge(*PE_.at(f"H{t-1}0", g))
                        own()
                        nc.scalar.activation(hn2T[:, 0:4], big[i % 4][:].rearrange("p (k t) -> p k t", k=4), ACT.Copy).then_inc(*A.tick(f"e:H{t-1}0"))
                for i in range(2):
                    act.wait_ge(h_out[i], 64 * (g + 1))
                tables["A"] = A.table()

        @block.vector
        def _(dve):
            V = V_

            def own():
                dve.wait_ge(*V.now())

            def op1(name, fn, *a, **k):
                own()
                fn(*a, **k).then_inc(*V.tick(name))

            nc.vector.memset(xr[:, :, 0:CONV - 1], 0.0).then_inc(*V.tick())
            nc.vector.memset(hcar[:], 0.0).then_inc(*V.tick())
            nc.vector.memset(att[:], 0.0).then_inc(*V.tick())
            nc.vector.memset(st[:], 0.0).then_inc(*V.tick("zeroed"))
            dve.wait_ge(consts_made, 8)
            nc.vector.tensor_copy(keepm[:], attmask).then_inc(*V.tick())
            dve.wait_ge(*A_.before("p2"))
            nc.vector.tensor_scalar(sp[:, 1], lam[:], -1.0, 0.0, ALU.mult, ALU.max).then_inc(*V.tick())
            own()
            nc.vector.tensor_tensor(sp[:, 1], sp[:, 1], sp[:, 2], ALU.add).then_inc(*V.tick())
            own()
            nc.vector.tensor_scalar(sp[:, 0], sp[:, 1], -C_RG, None, ALU.mult).then_inc(*V.tick())
            nc.vector.tensor_scalar(sp[:, 3], sp[:, 1], C_RG, None, ALU.mult).then_inc(*V.tick("sp"))

            def norm_rows(n):
                dve.wait_ge(hn_stat, (TT + 1) * n + TT)
                if not isinstance(n, int):
                    dve.wait_ge(hn_ready, TT * n)
                nc.vector.tensor_scalar(stat[:, 4:8], stat[:, 0:4], 1.0 / D, EPS, ALU.mult, ALU.add).then_inc(hn_rs, 1)
                dve.wait_ge(hn_stat, (TT + 1) * (n + 1))
                nc.vector.reciprocal(stat[:, 12:16], stat[:, 8:12]).then_inc(hn_rs, 1)
                dve.wait_ge(hn_rs, 2 * n + 2)
                for t in range(TT):
                    nc.vector.tensor_scalar(xs[:, t], xs[:, t], stat[:, 12 + t:13 + t], None, ALU.mult).then_inc(hn_ready, 1)

            norm_rows(0)
            dve.sem_inc(group_done, 1)
            with dve.Fori(0, GROUPS) as g:
                V.begin_loop(g)

                def result(name):
                    dve.wait_ge(*PE_.at(name, g))
                    own()
                    return big[ORDER.index(name) % 4]

                for k in range(1, KT, 2):
                    b = result(f"T{k}")
                    nc.vector.tensor_scalar(hnT[:, k], b[:], nmix[:, k:k + 1], None, ALU.mult).then_inc(*V.tick(f"e:T{k}"))
                for c in range(CT):
                    dve.wait_ge(*A_.at(f"e:X{c}", g))
                    own()
                    nc.vector.tensor_scalar(xc[:, c], xr[:, c, 0:GT], cw[:, c, 0:1], cb[:, c:c + 1], ALU.mult, ALU.add).then_inc(*V.tick())
                    for j in range(1, CONV):
                        own()
                        nc.vector.scalar_tensor_tensor(xc[:, c], xr[:, c, j:j + GT], cw[:, c, j:j + 1], xc[:, c],
                                                       ALU.mult, ALU.add).then_inc(*V.tick(f"xc{c}" if j == CONV - 1 else None))
                own()
                nc.vector.tensor_copy(xr[:, :, 0:CONV - 1], xr[:, :, GT:GT + CONV - 1]).then_inc(*V.tick("halo"))
                for c in range(HP):
                    b = result(f"L{c}")
                    dve.wait_ge(*A_.at(f"a:L{c}", g))
                    nc.vector.tensor_scalar(z2[:, c], b[:], bal[:, c:c + 1], 0.0, ALU.add, ALU.min).then_inc(*V.tick(f"e:L{c}"))
                dve.wait_ge(*A_.at("ln", g))
                own()
                nc.vector.tensor_tensor(z2[:], z2[:], z1[:], ALU.subtract).then_inc(*V.tick())
                for c in range(HP):
                    own()
                    nc.vector.tensor_tensor_scan(bb[:, c], restart[:], z2[:, c], 0.0, ALU.mult, ALU.add).then_inc(*V.tick("b" if c == HP - 1 else None))

                def rg(c):
                    dve.wait_ge(*A_.at(f"th{c}", g))
                    own()
                    nc.vector.tensor_scalar(uu, th, 1.0, None, ALU.add).then_inc(*V.tick())
                    own()
                    nc.vector.reciprocal(uu, uu).then_inc(*V.tick())
                    own()
                    nc.vector.scalar_tensor_tensor(th, th, 2.0, uu, ALU.mult, ALU.mult).then_inc(*V.tick(f"oma{c}"))
                    own()
                    nc.vector.tensor_tensor(it, it, xc[:, c], ALU.mult).then_inc(*V.tick())
                    dve.wait_ge(*A_.at(f"sq{c}", g))
                    own()
                    nc.vector.tensor_tensor(uu, th, it, ALU.mult).then_inc(*V.tick())
                    own()
                    nc.vector.tensor_tensor_scan(xc[:, c], at_, uu, hcar[:, c:c + 1], ALU.mult, ALU.add).then_inc(*V.tick(f"scan{c}"))
                    own()
                    nc.vector.tensor_copy(hcar[:, c:c + 1], xc[:, c, GT - 1:GT]).then_inc(*V.tick())

                rg(0)
                for i, n in enumerate(("Q0", "Q1", "K0", "K1")):
                    b = result(n)
                    nc.vector.tensor_copy(qk[:, i], b[:]).then_inc(*V.tick("e:" + n))
                dve.wait_ge(*A_.at("enb", g))
                own()
                nc.vector.scalar_tensor_tensor(qk[:, 0:HP], qk[:, 0:HP], DK ** -0.5, z1[:], ALU.mult, ALU.mult).then_inc(*V.tick("qs"))
                nc.vector.tensor_tensor(ks[:], qk[:, HP:], z2[:], ALU.mult).then_inc(*V.tick("ks"))
                own()
                for c in range(HP):
                    bc = bb[:, c].rearrange("p (n c) -> p n c", c=CHUNK)
                    nc.vector.tensor_tensor(z1[:, c].rearrange("p (n c) -> p n c", c=CHUNK),
                                            bc[:, :, CHUNK - 1:CHUNK].to_broadcast([P, NCH, CHUNK]), bc,
                                            ALU.subtract).then_inc(*V.tick("bend" if c else None))
                rg(1)
                dve.wait_ge(*A_.at("eend", g))
                own()
                nc.vector.tensor_tensor(qk[:, HP:], qk[:, HP:], z1[:], ALU.mult).then_inc(*V.tick("ke"))
                rg(2)
                for t in range(2):
                    b = result(f"G{t}")
                    dve.wait_ge(*A_.at(f"a:G{t}", g))
                    nc.vector.tensor_tensor(sg[:, t], b[:], sg[:, t], ALU.mult).then_inc(*V.tick(f"e:G{t}"))
                rg(3)
                for t in range(2, TT):
                    b = result(f"G{t}")
                    dve.wait_ge(*A_.at(f"a:G{t}", g))
                    nc.vector.tensor_tensor(sg[:, t], b[:], sg[:, t], ALU.mult).then_inc(*V.tick(f"e:G{t}"))
                for c in range(CT):
                    dve.wait_ge(*A_.at(f"e:Y{c}", g))
                    own()
                    nc.vector.tensor_tensor(yr[:, c], xc[:, c], yr[:, c], ALU.mult).then_inc(*V.tick(f"y{c}"))
                norm_rows(g + 1)
                for q in range(2):
                    b = result(f"KE{q}")
                    nc.vector.tensor_copy(keT[:, 2 * q:2 * q + 2], b[:].rearrange("p (t c) -> p t c", t=2)).then_inc(*V.tick(f"e:KE{q}"))

                def keep(t):
                    dve.wait_ge(*PE_.at(f"att{t}", g))
                    if t >= 2:
                        dve.wait_ge(*PE_.at(f"o{t-2}", g))
                    own()
                    dve.sem_inc(passed_v, 1)
                    nc.vector.copy_predicated(att[:, t % 2], keepm[:], attp[t % 2][:]).then_inc(*V.tick(f"keep{t}"))

                keep(0)
                for t in range(TT):
                    for ch in range(2):
                        j = 2 * t + ch
                        if ch == 0:
                            dve.wait_ge(*PE_.at(f"kv{t}", g))
                            if t:
                                dve.wait_ge(*PE_.at(f"o{t-1}", g))
                        if ch == 1:
                            dve.wait_ge(*PE_.at(f"oc{t}", g))
                            own()
                        else:
                            own()
                        for c in range(HP):
                            nc.vector.scalar_tensor_tensor(st[:, (j + 1) % 2, c], st[:, j % 2, c], dc[:, c, j:j + 1],
                                                           kvp[:, ch, c], ALU.mult, ALU.add).then_inc(*V.tick(f"st{j+1}" if c else None))
                        if ch == 0 and t + 1 < TT:
                            keep(t + 1)
                b = result("SS")
                nc.vector.tensor_scalar(stat[:, 80:84], b[:, 0:TT], 1.0 / RG, EPS, ALU.mult, ALU.add).then_inc(*V.tick("e:SS"))
                dve.wait_ge(*A_.at(f"os{TT-1}{HEADS-1}", g))
                own()
                nc.vector.tensor_scalar(stat[:, 64:80], stat[:, 32:48], 1.0 / DV, EPS, ALU.mult, ALU.add).then_inc(*V.tick("oms"))
                dve.wait_ge(*A_.at("ort", g))
                nc.vector.reciprocal(stat[:, 64:84], stat[:, 64:84]).then_inc(*V.tick("rs"))
                own()
                for t in range(TT):
                    for h in range(HEADS):
                        cs = slice(h * DV, (h + 1) * DV)
                        j = 64 + t * HEADS + h
                        nc.vector.scalar_tensor_tensor(ot[:, t, cs], ot[:, t, cs], stat[:, j:j + 1], sg[:, t, cs],
                                                       ALU.mult, ALU.mult).then_inc(*V.tick(f"on{t}" if h == HEADS - 1 else None))
                for t in range(TT + 1):
                    if t < TT:
                        for n in range(2):
                            hs = hres[t % 2][:, n * 512:(n + 1) * 512]
                            b = result(f"O{t}{n}r")
                            dve.wait_ge(hres_in[t % 2], 32 * g + 16 * (t // 2 + 1))
                            nc.vector.scalar_tensor_tensor(hs, b[:], stat[:, 80 + t:81 + t], hs, ALU.mult, ALU.add).then_inc(*V.tick(f"e:O{t}{n}r"))
                            b = result(f"O{t}{n}g")
                            nc.vector.tensor_tensor(hs, b[:], hs, ALU.add).then_inc(*V.tick(f"e:O{t}{n}g"))
                            if n:
                                V.marks[f"h{t}"] = V.n
                        dve.wait_ge(*A_.at(f"hsq{t}", g))
                        nc.vector.tensor_scalar(stat[:, 20 + t:21 + t], stat[:, 16 + t:17 + t], 1.0 / D, EPS, ALU.mult, ALU.add).then_inc(*V.tick(f"hms{t}"))
                        dve.wait_ge(*A_.at(f"hrt{t}", g))
                        nc.vector.reciprocal(stat[:, 24 + t:25 + t], stat[:, 20 + t:21 + t]).then_inc(*V.tick())
                        own()
                        if t >= 2:
                            dve.wait_ge(h_out[t % 2], 64 * g + 32)
                            dve.wait_ge(*PE_.at(f"H{t-2}1", g))
                        nc.vector.scalar_tensor_tensor(hn2[t % 2], hres[t % 2], stat[:, 24 + t:25 + t], nffn[:], ALU.mult, ALU.mult).then_inc(*V.tick(f"hn{t}"))
                    if t:
                        b = result(f"H{t-1}1")
                        nc.vector.tensor_copy(hn2T[:, 4:8], b[:].rearrange("p (k t) -> p k t", k=4)).then_inc(*V.tick(f"e:H{t-1}1"))
                        b = result(f"R{t-1}")
                        if t < TT:
                            nc.vector.tensor_tensor(logits[:, bass.ds(g * TT + t - 1, 1), :], b[:, 0:NR].rearrange("p (a n) -> p a n", a=1),
                                                    rbias[:].rearrange("p (a n) -> p a n", a=1), ALU.add).then_inc(*V.tick(f"e:R{t-1}"))
                        else:
                            nc.vector.tensor_tensor(logits[:, bass.ds(g * TT + t - 1, 1), :], b[:, 0:NR].rearrange("p (a n) -> p a n", a=1),
                                                    rbias[:].rearrange("p (a n) -> p a n", a=1), ALU.add).then_inc(group_done, 1)
                for i in range(2):
                    dve.wait_ge(h_out[i], 64 * (g + 1))
                tables["V"] = V.table()

        @block.tensor
        def _(pe):
            pe.wait_ge(consts_made, 8)
            pe.wait_ge(consts_in, 16 * N_CONST)
            with pe.Fori(0, GROUPS) as g:
                PE_.begin_loop(g)

                def bank(name):
                    i = ORDER.index(name)
                    if i >= 4:
                        E = A_ if EMPTIED_BY[ORDER[i - 4]] == "A" else V_
                        pe.wait_ge(*E.at("e:" + ORDER[i - 4], g))
                    return big[i % 4]

                pe.wait_ge(group_done, g + 1)
                pe.wait_ge(hn_ready, TT * (g + 1))
                for k in range(KT):
                    b = bank(f"T{k}")
                    for t in range(TT):
                        m = nc.tensor.transpose(b[:, t * P:(t + 1) * P], xs[:, t, k * P:(k + 1) * P], ident[:])
                    m.then_inc(*PE_.tick(f"T{k}"))
                pe.wait_ge(*A_.at(f"e:T{KT-2}", g))
                pe.wait_ge(*V_.at(f"e:T{KT-1}", g))

                def channels(i):
                    n = tile_names[i]
                    b = bank(n)
                    pe.wait_ge(wring_in[i % 4], 48 * g + 16 * (i // 4 + 1))
                    for k in range(KT):
                        m = nc.tensor.matmul(b[:], ring[:, i % 4, k], hnT[:, k], start=(k == 0), stop=(k == KT - 1))
                    m.then_inc(*PE_.tick(n))

                def tokens(n, t):
                    b = bank(f"{n}{t}")
                    pe.wait_ge(wvg_in, 32 * g + (16 if n == "V" else 32))
                    for k in range(KT):
                        m = nc.tensor.matmul(b[:], hnT[:, k, t * P:(t + 1) * P], wvg[:, k], start=(k == 0), stop=(k == KT - 1))
                    m.then_inc(*PE_.tick(f"{n}{t}"))

                def gates(c):
                    for i, n in enumerate((f"GA{c}", f"GX{c}")):
                        b = bank(n)
                        pe.wait_ge(*V_.at(f"xc{c}", g))
                        nc.tensor.matmul(b[:], bd[:, i, c], xc[:, c], start=True, stop=True).then_inc(*PE_.tick(n))

                for i in range(4):
                    channels(i)
                b = bank("AL")
                for k in range(KT):
                    m = nc.tensor.matmul(b[0:RANK, :], wal[:, k], hnT[:, k], start=(k == 0), stop=(k == KT - 1))
                m.then_inc(*PE_.tick("AL"))
                for t in range(TT):
                    tokens("V", t)
                for c in range(HP):
                    b = bank(f"L{c}")
                    pe.wait_ge(*A_.at("e:AL", g))
                    nc.tensor.matmul(b[:], wup[:, c * P:(c + 1) * P], alow, start=True, stop=True).then_inc(*PE_.tick(f"L{c}"))
                gates(0)
                for i in range(4, 8):
                    channels(i)
                gates(1)
                for i in range(8, 12):
                    channels(i)
                gates(2)
                tokens("G", 0)
                tokens("G", 1)
                gates(3)
                tokens("G", 2)
                tokens("G", 3)
                for q in range(2):
                    b = bank(f"KE{q}")
                    pe.wait_ge(*V_.at("ke", g))
                    for t in range(2):
                        for c in range(HP):
                            tt = 2 * q + t
                            m = nc.tensor.transpose(b[:, (t * HP + c) * P:(t * HP + c + 1) * P],
                                                    qk[:, HP + c, tt * P:(tt + 1) * P], ident[:])
                    m.then_inc(*PE_.tick(f"KE{q}"))

                by_rows = [h for r in range(2) for h in range(r, HEADS, 2)]

                def rows_apart():
                    pe.wait_ge(*PE_.now())
                    pe.sem_inc(passed_p, 1)

                def scores(t):
                    if t >= 2:
                        pe.wait_ge(*V_.at(f"keep{t-2}", g))
                    else:
                        pe.wait_ge(*V_.at("ks", g))
                    for i, h in enumerate(by_rows):
                        if i == HP:
                            m.then_inc(*PE_.tick())
                            rows_apart()
                        r, c = slice(DK * (h % 2), DK * (h % 2) + DK), h // 2
                        m = nc.tensor.matmul(attp[t % 2][:, h * P:(h + 1) * P], ks[r, c, t * P:(t + 1) * P],
                                             qk[r, c, t * P:(t + 1) * P], start=True, stop=True)
                    m.then_inc(*PE_.tick(f"att{t}"))

                def outer(t):
                    pe.wait_ge(*V_.at(f"e:KE{t//2}", g))
                    if t:
                        pe.wait_ge(*V_.at(f"st{2*t}", g))
                    for ch in range(2):
                        for h in range(HEADS):
                            r, c = slice(DK * (h % 2), DK * (h % 2) + DK), h // 2
                            tk = slice(CHUNK * ch, CHUNK * ch + CHUNK)
                            if h == 0:
                                if ch:
                                    m.then_inc(*PE_.tick())
                                rows_apart()
                            m = nc.tensor.matmul(kvp[r, ch, c], keT[tk, t, h * DK:(h + 1) * DK], vt[tk, t, h * DV:(h + 1) * DV],
                                                 start=True, stop=True, skip_group_check=True)
                    m.then_inc(*PE_.tick(f"kv{t}"))

                def attend(t):
                    pe.wait_ge(*V_.at(f"keep{t}", g))
                    if t:
                        pe.wait_ge(*A_.at(f"o{t-1}", g))
                    for h in range(HEADS):
                        cs = slice(h * DV, (h + 1) * DV)
                        m = nc.tensor.matmul(op[:, cs], att[:, t % 2, h * P:(h + 1) * P], vt[:, t, cs],
                                             start=(h == 0), stop=False, skip_group_check=True)
                    for ch in range(2):
                        j = 2 * t + ch
                        if j:
                            pe.wait_ge(*V_.at(f"st{j}", g))
                        m.then_inc(*PE_.tick())
                        rows_apart()
                        for i, h in enumerate(by_rows):
                            if i == HP:
                                m.then_inc(*PE_.tick())
                                rows_apart()
                            r, c = slice(DK * (h % 2), DK * (h % 2) + DK), h // 2
                            tk = slice(CHUNK * ch, CHUNK * ch + CHUNK)
                            m = nc.tensor.matmul(op[tk, h * DV:(h + 1) * DV], qk[r, c, t * P + CHUNK * ch:t * P + CHUNK * (ch + 1)],
                                                 st[r, j % 2, c], start=False, stop=(ch == 1), skip_group_check=True)
                        PE_.marks[f"oc{t}" if ch == 0 else f"o{t}"] = PE_.n + 1
                        if ch == 1:
                            m.then_inc(*PE_.tick())

                scores(0)
                outer(0)
                for t in range(TT):
                    if t + 1 < TT:
                        scores(t + 1)
                    attend(t)
                    if t + 1 < TT:
                        outer(t + 1)
                b = bank("SS")
                pe.wait_ge(*A_.at(f"ysq{CT-1}", g))
                for t in range(TT):
                    for c in range(CT):
                        m = nc.tensor.matmul(b[:, t:t + 1], xc[:, c, t * P:(t + 1) * P], ones[:, 0:1],
                                             start=(c == 0), stop=(c == CT - 1))
                m.then_inc(*PE_.tick("SS"))
                for t in range(TT):
                    b = bank(f"YT{t}")
                    pe.wait_ge(*V_.at(f"on{t}", g))
                    for h in range(HEADS):
                        m = nc.tensor.transpose(b[:, h * P:(h + 1) * P], ot[:, t, h * DV:(h + 1) * DV], ident[:])
                    m.then_inc(*PE_.tick(f"YT{t}"))

                def out(t):
                    for n in range(2):
                        ns = slice(n * 512, (n + 1) * 512)
                        b = bank(f"O{t}{n}r")
                        for k in range(CT):
                            m = nc.tensor.matmul(b[:], yr[:, k, t * P:(t + 1) * P], wout[:, k, ns], start=(k == 0), stop=(k == CT - 1))
                        m.then_inc(*PE_.tick(f"O{t}{n}r"))
                        b = bank(f"O{t}{n}g")
                        pe.wait_ge(*A_.at(f"e:YT{t}", g))
                        for k in range(CT):
                            m = nc.tensor.matmul(b[:], qk[:, k, t * P:(t + 1) * P], wout[:, CT + k, ns], start=(k == 0), stop=(k == CT - 1))
                        m.then_inc(*PE_.tick(f"O{t}{n}g"))

                def router(t):
                    for q in range(2):
                        b = bank(f"H{t}{q}")
                        pe.wait_ge(*V_.at(f"hn{t}", g))
                        for k in range(4):
                            kk = 4 * q + k
                            m = nc.tensor.transpose(b[:, k * P:(k + 1) * P], hn2[t % 2][:, kk * P:(kk + 1) * P], ident[:])
                        m.then_inc(*PE_.tick(f"H{t}{q}"))
                    b = bank(f"R{t}")
                    pe.wait_ge(*A_.at(f"e:H{t}0", g))
                    pe.wait_ge(*V_.at(f"e:H{t}1", g))
                    for k in range(KT):
                        m = nc.tensor.matmul(b[:, 0:NR], hn2T[:, k], wrt[:, k], start=(k == 0), stop=(k == KT - 1))
                    m.then_inc(*PE_.tick(f"R{t}"))

                pe.wait_ge(wout_scaled, KT)
                for t in range(TT + 1):
                    if t < TT:
                        out(t)
                    if t:
                        router(t - 1)
                tables["P"] = PE_.table()


def route(nc, slot_dram, ident, ones, logits, dest, wts, btab, sem):
    with ExitStack() as ctx:
        def sb(name, shape, dt=F32):
            return ctx.enter_context(nc.sbuf_tensor(name, shape, dt))

        earlier = sb("earlier", [P, P])
        gdesc = sb("gdesc", [P, NG])
        edesc = sb("edesc", [P, EPG])
        blk = sb("blk", [P, BLOCKS + 1])
        rows = sb("rows", [P, TILES, 2, 2], I32)
        no_rows = sb("no_rows", [P, SLOTS // P, 2], I32)
        gval = sb("gval", [P, TILES, NG])
        goh = sb("goh", [P, TILES, NG])
        gm = sb("gm", [P, TILES])
        gx = sb("gx", [P, TILES, NG])
        gw = sb("gw", [P, TILES])
        le4 = sb("le4", [P, TILES, NG, EPG])
        le = sb("le", [P, TILES, EPG])
        eval_ = sb("eval", [P, TILES, EPG])
        oh = sb("oh", [P, 2, TILES, EPG])
        m12 = sb("m12", [P, 2, TILES])
        mx = sb("mx", [P, TILES])
        big_oh = sb("big_oh", [P, 2, TILES, NG, EPG])
        both = sb("both", [P, TILES, NE])
        carry = sb("carry", [P, TILES + 1, NE])
        rank = sb("rank", [P, TILES, NE])
        padded = sb("padded", [P, NE])
        padded_i = sb("padded_i", [P, NE], I32)
        pend = sb("pend", [P, NE])
        pstart = sb("pstart", [P, NE])
        prod = sb("prod", [P, TILES, NE])
        destf = sb("destf", [P, TILES, 2])
        cmp = sb("cmp", [P, BLOCKS + 1, NE])
        bef = sb("bef", [P, BLOCKS + 2])
        btf = sb("btf", [P, 2 * (BLOCKS + 1) + 1])
        rk = ctx.enter_context(nc.psum_tensor("rk", [P, TILES * NE], F32))
        tot = ctx.enter_context(nc.psum_tensor("tot", [P, TILES * NE], F32))

        tables_made = sem("r_tables_made")
        ohs_ready = sem("r_ohs_ready")
        counted = sem("r_counted")
        dve_steps = sem("r_dve_steps")
        exps = sem("r_exps")
        exp_in = sem("r_exp_in")
        dest_ready = sem("r_dest_ready")
        slots_zeroed = sem("r_slots_zeroed")
        slots_written = sem("r_slots_written")

        block = ctx.enter_context(nc.Block())

        @block.gpsimd
        def _(pool):
            nc.gpsimd.memset(earlier[:], 1.0).then_inc(tables_made, 1)
            nc.gpsimd.iota(no_rows[:, :, 0], [[0, SLOTS // P]], base=0, channel_multiplier=0).then_inc(tables_made, 1)
            nc.gpsimd.iota(no_rows[:, :, 1], [[1, SLOTS // P]], base=2 * SEQ, channel_multiplier=SLOTS // P).then_inc(tables_made, 1)
            nc.gpsimd.iota(gdesc[:], [[-1, NG]], base=NG, channel_multiplier=0,
                           allow_small_or_imprecise_dtypes=True).then_inc(tables_made, 1)
            nc.gpsimd.iota(edesc[:], [[-1, EPG]], base=EPG, channel_multiplier=0,
                           allow_small_or_imprecise_dtypes=True).then_inc(tables_made, 1)
            nc.gpsimd.iota(blk[:], [[1, BLOCKS + 1]], base=0, channel_multiplier=0,
                           allow_small_or_imprecise_dtypes=True).then_inc(tables_made, 1)
            nc.gpsimd.iota(rows[:, :, :, 0], [[P, TILES], [0, 2]], base=0, channel_multiplier=1).then_inc(tables_made, 1)
            nc.gpsimd.iota(rows[:, :, :, 1], [[2 * P, TILES], [1, 2]], base=0, channel_multiplier=2).then_inc(tables_made, 1)
            pool.wait_ge(tables_made, 8)
            nc.gpsimd.affine_select(out=earlier[:], in_=earlier[:], compare_op=ALU.is_gt, fill=0.0, base=0,
                                    pattern=[[1, P]], channel_multiplier=-1).then_inc(tables_made, 1)
            pool.wait_ge(dest_ready, 1)
            pool.wait_ge(slots_zeroed, 16)
            for t in range(TILES):
                for k in range(2):
                    nc.gpsimd.indirect_dma_start(slot_dram, bass.IndirectOffsetOnAxis(dest[:, t, k:k + 1], 0),
                                                 rows[:, t, k], None).then_inc(slots_written, 16)
            pool.wait_ge(slots_written, 16 * 2 * TILES)

        @block.sync
        def _(sync):
            sync.wait_ge(tables_made, 8)
            sync.dma_start(slot_dram.rearrange("(p a) o -> p (a o)", p=P), no_rows[:].rearrange("p a o -> p (a o)")).then_inc(slots_zeroed, 16)
            sync.wait_ge(slots_zeroed, 16)

        @block.scalar
        def _(act):
            act.wait_ge(exp_in, 1)
            nc.scalar.activation(gx[:], gx[:], ACT.Exp).then_inc(exps, 1)
            act.wait_ge(exp_in, 2)
            nc.scalar.activation(mx[:], mx[:], ACT.Exp).then_inc(exps, 1)

        @block.vector
        def _(dve):
            n = [0]

            def step(ins, signal=None):
                if signal is not None:
                    ins.then_inc(signal, 1)
                else:
                    n[0] += 1
                    ins.then_inc(dve_steps, 1)
                    dve.wait_ge(dve_steps, n[0])

            def bc(ap, shape):
                return ap.to_broadcast(shape)

            v = nc.vector
            dve.wait_ge(tables_made, 9)
            gl = logits[:, :, 0:NG]
            g4 = [P, TILES, NG]
            e8 = [P, TILES, EPG]
            step(v.tensor_reduce(gm[:], gl, AX, ALU.max))
            step(v.tensor_tensor(gx[:], gl, bc(gm[:].unsqueeze(2), g4), ALU.subtract))
            step(v.tensor_scalar(gval[:], gx[:], 0.0, None, ALU.is_equal))
            step(v.tensor_tensor(gval[:], gval[:], bc(gdesc[:].unsqueeze(1), g4), ALU.mult))
            v.tensor_reduce(gw[:], gval[:], AX, ALU.max).then_inc(exp_in, 1)
            dve.wait_ge(exp_in, 1)
            step(v.tensor_tensor(goh[:], gval[:], bc(gw[:].unsqueeze(2), g4), ALU.is_equal))
            dve.wait_ge(exps, 1)
            step(v.tensor_reduce(gw[:], gx[:], AX, ALU.add))
            step(v.reciprocal(gw[:], gw[:]))
            lg = logits[:, :, NG:NR].rearrange("p t (g e) -> p t g e", g=NG)
            for g in range(NG):
                step(v.tensor_tensor(le4[:, :, g], lg[:, :, g], bc(goh[:, :, g:g + 1], e8), ALU.mult))
            step(v.tensor_reduce(le[:], le4[:].rearrange("p t g e -> p t e g"), AX, ALU.add))
            for k in range(2):
                step(v.tensor_reduce(m12[:, k], le[:], AX, ALU.max))
                step(v.tensor_tensor(eval_[:], le[:], bc(m12[:, k].unsqueeze(2), e8), ALU.is_equal))
                step(v.tensor_tensor(eval_[:], eval_[:], bc(edesc[:].unsqueeze(1), e8), ALU.mult))
                step(v.tensor_reduce(mx[:], eval_[:], AX, ALU.max))
                step(v.tensor_tensor(oh[:, k], eval_[:], bc(mx[:].unsqueeze(2), e8), ALU.is_equal))
                if k == 0:
                    step(v.scalar_tensor_tensor(le[:], oh[:, 0], -3.0e38, le[:], ALU.mult, ALU.add))
            v.tensor_tensor(mx[:], m12[:, 1], m12[:, 0], ALU.subtract).then_inc(exp_in, 1)
            dve.wait_ge(exps, 2)
            step(v.tensor_scalar(m12[:, 0], mx[:], 1.0, None, ALU.add))
            step(v.reciprocal(m12[:, 0], m12[:, 0]))
            step(v.tensor_tensor(wts[:, :, 0], m12[:, 0], gw[:], ALU.mult))
            step(v.tensor_tensor(wts[:, :, 1], wts[:, :, 0], mx[:], ALU.mult))
            for k in range(2):
                for g in range(NG):
                    step(v.tensor_tensor(big_oh[:, k, :, g], oh[:, k], bc(goh[:, :, g:g + 1], e8), ALU.mult))
            b0 = big_oh[:, 0].rearrange("p t g e -> p t (g e)")
            b1 = big_oh[:, 1].rearrange("p t g e -> p t (g e)")
            v.tensor_tensor(both[:], b0, b1, ALU.add).then_inc(ohs_ready, 1)
            step(v.memset(carry[:, 0], 0.0))
            dve.wait_ge(counted, 2)
            tt = tot[:].rearrange("p (t e) -> p t e", e=NE)
            for t in range(TILES):
                step(v.tensor_tensor(carry[:, t + 1], tt[:, t], carry[:, t], ALU.add))
            step(v.tensor_tensor(rank[:], rk[:].rearrange("p (t e) -> p t e", e=NE), carry[:, 0:TILES], ALU.add))
            step(v.tensor_scalar(padded_i[:], carry[:, TILES], float(P - 1), None, ALU.add))
            step(v.tensor_scalar(padded_i[:], padded_i[:], 7, None, ALU.logical_shift_right))
            step(v.tensor_copy(padded[:], padded_i[:]))
            step(v.tensor_tensor_scan(pend[:], ones[:, 0:NE], padded[:], 0.0, ALU.mult, ALU.add))
            step(v.tensor_tensor(pstart[:], pend[:], padded[:], ALU.subtract))
            step(v.tensor_scalar(pstart[:], pstart[:], float(P), None, ALU.mult))
            step(v.tensor_tensor(rank[:], rank[:], bc(pstart[:].unsqueeze(1), [P, TILES, NE]), ALU.add))
            for k, b in enumerate((b0, b1)):
                step(v.tensor_tensor(prod[:], rank[:], b, ALU.mult))
                step(v.tensor_reduce(destf[:, :, k], prod[:], AX, ALU.add))
            v.tensor_copy(dest[:], destf[:]).then_inc(dest_ready, 1)
            step(v.tensor_tensor(cmp[:], bc(pend[:].unsqueeze(1), [P, BLOCKS + 1, NE]),
                                 bc(blk[:].unsqueeze(2), [P, BLOCKS + 1, NE]), ALU.is_le))
            step(v.memset(bef[:, 0:1], -1.0))
            step(v.tensor_reduce(bef[:, 1:], cmp[:], AX, ALU.add))
            step(v.tensor_scalar(btf[:, 0:BLOCKS + 1], bef[:, 1:], float(NE - 1), None, ALU.min))
            step(v.tensor_tensor(btf[:, BLOCKS + 1:2 * (BLOCKS + 1)], bef[:, 1:], bef[:, 0:BLOCKS + 1], ALU.not_equal))
            step(v.tensor_copy(btf[:, 2 * (BLOCKS + 1):], pend[:, NE - 1:NE]))
            step(v.tensor_copy(btab[:], btf[:]))

        @block.tensor
        def _(pe):
            pe.wait_ge(tables_made, 9)
            pe.wait_ge(ohs_ready, 1)
            b = both[:].rearrange("p t e -> p (t e)")
            nc.tensor.matmul(rk[:], earlier[:], b, start=True, stop=True).then_inc(counted, 1)
            nc.tensor.matmul(tot[:], ones[:], b, start=True, stop=True).then_inc(counted, 1)


def experts(nc, T, slot_dram, hn_dram, y_dram, ident, btab, sem):
    KU = 4
    UNITS = 12
    STAGE = 4
    UW = KU * 512
    with ExitStack() as ctx:
        def sb(name, shape, dt=F32):
            return ctx.enter_context(nc.sbuf_tensor(name, shape, dt))

        def ps(name, shape):
            return ctx.enter_context(nc.psum_tensor(name, shape, F32))

        raw = sb("raw", [P, UNITS, UW])
        whi = sb("whi", [P, STAGE, UW], F32R)
        wlo = sb("wlo", [P, STAGE, UW], F32R)
        xg = sb("xg", [P, D])
        idx = sb("idx", [P, 2], I32)
        place = sb("place", [P, 1], I32)
        xhi = sb("xhi", [P, KT, P], F32R)
        xlo = sb("xlo", [P, KT, P], F32R)
        hb = sb("hb", [P, D])
        hhi = sb("hhi", [P, KT, P], F32R)
        hlo = sb("hlo", [P, KT, P], F32R)
        ysb = sb("ysb", [P, D])
        gate = [ps(f"gate{n}", [P, 512]) for n in range(2)]
        up = [ps(f"up{n}", [P, 512]) for n in range(2)]
        yp = [ps(f"yp{n}", [P, 512]) for n in range(2)]
        tp = [ps(f"tp{n}", [P, 512]) for n in range(2)]

        w_in = [sem(f"e_w_in{u}") for u in range(UNITS)]
        hi_made = sem("e_hi_made")
        lo_made = sem("e_lo_made")
        stage_free = sem("e_stage_free")
        idx_in = sem("e_idx_in")
        place_kept = sem("e_place_kept")
        rows_in = sem("e_rows_in")
        x_turned = sem("e_x_turned")
        x_hi = sem("e_x_hi")
        x_lo = sem("e_x_lo")
        gelu_done = sem("e_gelu_done")
        h_done = sem("e_h_done")
        h_turned = sem("e_h_turned")
        h_hi = sem("e_h_hi")
        h_lo = sem("e_h_lo")
        y_out_a = sem("e_y_copied_act")
        y_out_v = sem("e_y_copied_dve")
        y_stored = sem("e_y_stored")
        passed_g = sem("e_passed_g")
        passed_s = sem("e_passed_s")

        def unit(u):
            if u < 8:
                n, r = divmod(u, 4)
                return ("gate", "up")[r % 2], n, r // 2
            return "down", None, u - 8

        def unit_rows(u, e):
            kind, n, q = unit(u)
            if kind == "down":
                w = T["w_exp_down"][0].rearrange("e (k p) n -> e p k n", p=P)
                return w[bass.ds(e, 1), :, 2 * q:2 * q + 2, :].rearrange("e p k n -> p (e k) n")
            w = T["w_exp_" + kind][0].rearrange("e (k p) n -> e p k n", p=P)
            return w[bass.ds(e, 1), :, KU * q:KU * q + KU, n * 512:(n + 1) * 512].rearrange("e p k n -> p (e k) n")

        def count_of_blocks(eng):
            return eng.value_load(btab[0:1, 2 * (BLOCKS + 1):], min_val=1, max_val=BLOCKS)

        block = ctx.enter_context(nc.Block())

        @block.sync
        def _(sync):
            n_blocks = count_of_blocks(sync)

            def dst(u):
                kind = unit(u)[0]
                k = 2 if kind == "down" else KU
                return raw[:, u].rearrange("p (k n) -> p k n", k=k)

            first = sync.value_load(btab[0:1, 0:1], min_val=0, max_val=NE - 1)
            for u in range(UNITS):
                sync.dma_start(dst(u), unit_rows(u, first)).then_inc(w_in[u], 16)
            with sync.Fori(0, n_blocks) as b:
                e = sync.value_load(btab[0:1, bass.ds(b + 1, 1)], min_val=0, max_val=NE - 1)
                new = sync.value_load(btab[0:1, bass.ds(b + BLOCKS + 2, 1)], min_val=0, max_val=1)
                srcs = [unit_rows(u, e) for u in range(UNITS)]
                for u in range(UNITS):
                    sync.wait_ge(hi_made, UNITS * b + u + 1)
                    sync.wait_ge(lo_made, UNITS * b + u + 1)
                    sync.dma_start(dst(u), srcs[u], cond=new > 0).then_inc(w_in[u], 16)
            for u in range(UNITS):
                sync.wait_ge(w_in[u], 16 * (n_blocks + 1))
            sync.sem_inc(passed_s, 1)

        @block.gpsimd
        def _(pool):
            n_blocks = count_of_blocks(pool)

            def gather(b):
                nc.gpsimd.dma_start(idx[:], slot_dram[bass.ds(b * P, P), :]).then_inc(idx_in, 16)
                pool.wait_ge(idx_in, 16 * (b + 1))
                if not isinstance(b, int) or b:
                    pool.wait_ge(x_turned, 2 * b)
                pool.sem_inc(passed_g, 1)
                nc.gpsimd.indirect_dma_start(xg[:], None, hn_dram, bass.IndirectOffsetOnAxis(idx[:, 0:1], 0)).then_inc(rows_in, 16)

            def keep_place(b):
                pool.wait_ge(rows_in, 16 * (b + 1))
                pool.sem_inc(passed_g, 1)
                nc.gpsimd.tensor_copy(place[:], idx[:, 1:2]).then_inc(place_kept, 1)
                pool.wait_ge(place_kept, b + 1)

            def scatter(b):
                pool.wait_ge(y_out_a, b + 1)
                pool.wait_ge(y_out_v, b + 1)
                pool.sem_inc(passed_g, 1)
                nc.gpsimd.indirect_dma_start(y_dram, bass.IndirectOffsetOnAxis(place[:, 0:1], 0), ysb[:], None).then_inc(y_stored, 16)
                pool.wait_ge(y_stored, 16 * (b + 1))

            gather(0)
            keep_place(0)
            gather(1)
            with pool.Fori(1, n_blocks) as b:
                scatter(b - 1)
                keep_place(b)
                gather(b + 1)
            scatter(n_blocks - 1)
            pool.wait_ge(rows_in, 16 * (n_blocks + 1))
            pool.sem_inc(passed_g, 1)

        @block.scalar
        def _(act):
            n_blocks = count_of_blocks(act)

            def split(u, b):
                act.wait_ge(w_in[u], 16 * (b + 1))
                act.wait_ge(stage_free, UNITS * b + u + 1)
                nc.scalar.activation(whi[:, u % STAGE], raw[:, u], ACT.Copy).then_inc(hi_made, 1)

            def x_part(q, b):
                act.wait_ge(x_turned, 2 * b + q + 1)
                nc.scalar.activation(xhi[:, 4 * q:4 * q + 4], tp[q][:].rearrange("p (k t) -> p k t", k=4), ACT.Copy).then_inc(x_hi, 1)

            def gelu(n, b):
                act.wait_ge(stage_free, STAGE + UNITS * b + 4 * (n + 1))
                act.wait_ge(h_turned, 2 * b + 2)
                nc.scalar.activation(hb[:, n * 512:(n + 1) * 512], gate[n][:], ACT.Gelu_apprx_tanh).then_inc(gelu_done, 1)

            def h_part(n, b):
                act.wait_ge(h_turned, 2 + 2 * b + n + 1)
                nc.scalar.activation(hhi[:, 4 * n:4 * n + 4], tp[n][:].rearrange("p (k t) -> p k t", k=4), ACT.Copy).then_inc(h_hi, 1)

            def y_half(b):
                act.wait_ge(stage_free, STAGE + UNITS * (b + 1))
                if not isinstance(b, int) or b:
                    act.wait_ge(place_kept, b + 1)
                nc.scalar.activation(ysb[:, 0:512], yp[0][:], ACT.Copy).then_inc(y_out_a, 1)

            def body(b, with_y):
                split(2, b)
                split(3, b)
                if with_y:
                    y_half(b - 1)
                for u in range(4, 8):
                    split(u, b)
                gelu(0, b)
                split(8, b)
                split(9, b)
                h_part(0, b)
                split(10, b)
                gelu(1, b)
                split(11, b)
                h_part(1, b)
                split(0, b + 1)
                x_part(0, b + 1)
                split(1, b + 1)
                x_part(1, b + 1)

            nc.scalar.preload_act_table(ACT.Gelu_apprx_tanh)
            split(0, 0)
            split(1, 0)
            x_part(0, 0)
            x_part(1, 0)
            body(0, False)
            with act.Fori(1, n_blocks) as b:
                body(b, True)
            y_half(n_blocks - 1)

        @block.vector
        def _(dve):
            n_blocks = count_of_blocks(dve)

            def split(u, b):
                dve.wait_ge(hi_made, UNITS * b + u + 1)
                nc.vector.tensor_tensor(wlo[:, u % STAGE], raw[:, u], whi[:, u % STAGE].bitcast(F32), ALU.subtract).then_inc(lo_made, 1)

            def x_part(q, b):
                dve.wait_ge(x_hi, 2 * b + q + 1)
                nc.vector.tensor_tensor(xlo[:, 4 * q:4 * q + 4], tp[q][:].rearrange("p (k t) -> p k t", k=4),
                                        xhi[:, 4 * q:4 * q + 4].bitcast(F32), ALU.subtract).then_inc(x_lo, 1)

            def h_half(n, b):
                dve.wait_ge(gelu_done, 2 * b + n + 1)
                hs = hb[:, n * 512:(n + 1) * 512]
                nc.vector.tensor_tensor(hs, up[n][:], hs, ALU.mult).then_inc(h_done, 1)

            def h_part(n, b):
                dve.wait_ge(h_hi, 2 * b + n + 1)
                nc.vector.tensor_tensor(hlo[:, 4 * n:4 * n + 4], tp[n][:].rearrange("p (k t) -> p k t", k=4),
                                        hhi[:, 4 * n:4 * n + 4].bitcast(F32), ALU.subtract).then_inc(h_lo, 1)

            def y_half(b):
                dve.wait_ge(stage_free, STAGE + UNITS * (b + 1))
                if not isinstance(b, int) or b:
                    dve.wait_ge(place_kept, b + 1)
                nc.vector.tensor_copy(ysb[:, 512:D], yp[1][:]).then_inc(y_out_v, 1)

            def body(b, with_y):
                split(2, b)
                split(3, b)
                if with_y:
                    y_half(b - 1)
                for u in range(4, 8):
                    split(u, b)
                h_half(0, b)
                split(8, b)
                split(9, b)
                h_part(0, b)
                split(10, b)
                h_half(1, b)
                split(11, b)
                h_part(1, b)
                split(0, b + 1)
                x_part(0, b + 1)
                split(1, b + 1)
                x_part(1, b + 1)

            split(0, 0)
            split(1, 0)
            x_part(0, 0)
            x_part(1, 0)
            body(0, False)
            with dve.Fori(1, n_blocks) as b:
                body(b, True)
            y_half(n_blocks - 1)

        @block.tensor
        def _(pe):
            n_blocks = count_of_blocks(pe)

            def turn_x(q, b):
                pe.wait_ge(rows_in, 16 * (b + 1))
                if not isinstance(b, int):
                    pe.wait_ge(h_lo, 2 * (b - 1) + q + 1)
                for k in range(4):
                    kk = 4 * q + k
                    m = nc.tensor.transpose(tp[q][:, k * P:(k + 1) * P], xg[:, kk * P:(kk + 1) * P], ident[:])
                m.then_inc(x_turned, 1)

            def turn_h(n, b):
                pe.wait_ge(h_done, 2 * b + n + 1)
                for k in range(4):
                    m = nc.tensor.transpose(tp[n][:, k * P:(k + 1) * P], hb[:, (4 * n + k) * P:(4 * n + k + 1) * P], ident[:])
                m.then_inc(h_turned, 1)

            def three(out, ahi, alo, u, col, first, last):
                s = slice(col * 512, (col + 1) * 512)
                nc.tensor.matmul(out, ahi, whi[:, u % STAGE, s], start=first, stop=False)
                nc.tensor.matmul(out, ahi, wlo[:, u % STAGE, s], start=False, stop=False)
                return nc.tensor.matmul(out, alo, whi[:, u % STAGE, s], start=False, stop=last)

            def run_unit(u, b):
                kind, n, q = unit(u)
                pe.wait_ge(lo_made, UNITS * b + u + 1)
                if kind == "down":
                    if u == 8:
                        pe.wait_ge(place_kept, b + 1)
                    for k in range(2):
                        kk = 2 * q + k
                        for nn in range(2):
                            m = three(yp[nn][:], hhi[:, kk], hlo[:, kk], u, 2 * k + nn, kk == 0, kk == KT - 1)
                else:
                    out = (gate if kind == "gate" else up)[n]
                    for k in range(KU):
                        kk = KU * q + k
                        m = three(out[:], xhi[:, kk], xlo[:, kk], u, k, kk == 0, kk == KT - 1)
                return m

            pe.sem_inc(stage_free, STAGE)
            pe.sem_inc(h_turned, 2)
            turn_x(0, 0)
            turn_x(1, 0)
            with pe.Fori(0, n_blocks) as b:
                pe.wait_ge(x_lo, 2 * b + 2)
                for u in range(UNITS):
                    if u == 8:
                        pe.wait_ge(h_lo, 2 * b + 1)
                    if u == 10:
                        pe.wait_ge(h_lo, 2 * b + 2)
                    run_unit(u, b).then_inc(stage_free, 1)
                    if u == 5:
                        turn_h(0, b)
                    if u == 8:
                        turn_h(1, b)
                    if u == 9:
                        turn_x(0, b + 1)
                    if u == 10:
                        turn_x(1, b + 1)


def combine(nc, T, h_dram, y_dram, out_rows, wts, sem):
    BUF = 4
    with ExitStack() as ctx:
        def sb(name, shape, dt=F32):
            return ctx.enter_context(nc.sbuf_tensor(name, shape, dt))

        h = sb("c_h", [P, BUF, D])
        y = sb("c_y", [P, BUF, 2, D])
        o = sb("c_o", [P, BUF, D])
        nf = sb("c_nf", [P, D])
        stt = sb("c_st", [P, 4 * TILES])
        nf_in = sem("c_nf_in")
        h_in = [sem(f"c_h_in{i}") for i in range(BUF)]
        y_in = [sem(f"c_y_in{i}") for i in range(BUF)]
        out_st = [sem(f"c_out{i}") for i in range(BUF)]
        dve_steps = sem("c_dve_steps")
        sq_done = sem("c_sq_done")
        rt_done = sem("c_rt_done")
        PER = 5

        block = ctx.enter_context(nc.Block())

        @block.sync
        def _(sync):
            sync.dma_start(nf[:], T["norm_final"].rearrange("(a d) -> a d", a=1).partition_broadcast(P)).then_inc(nf_in, 16)
            for t in range(TILES):
                if t >= BUF:
                    sync.wait_ge(dve_steps, PER * (t - BUF + 1))
                sync.dma_start(h[:, t % BUF], h_dram[t * P:(t + 1) * P, :]).then_inc(h_in[t % BUF], 16)
                sync.dma_start(y[:, t % BUF], y_dram[2 * t * P:2 * (t + 1) * P, :].rearrange("(p k) d -> p k d", k=2)).then_inc(y_in[t % BUF], 16)

        @block.scalar
        def _(act):
            for t in range(TILES):
                i = t % BUF
                act.wait_ge(dve_steps, PER * t + 2)
                nc.scalar.activation(y[:, i, 0], h[:, i], ACT.Square, accum_out=stt[:, t:t + 1]).then_inc(sq_done, 1)
                act.wait_ge(dve_steps, PER * t + 3)
                nc.scalar.activation(stt[:, 2 * TILES + t:2 * TILES + t + 1], stt[:, TILES + t:TILES + t + 1], ACT.Sqrt).then_inc(rt_done, 1)
                act.wait_ge(dve_steps, PER * t + PER)
                act.dma_start(out_rows[t * P:(t + 1) * P, :], o[:, i]).then_inc(out_st[i], 16)
            for i in range(BUF):
                act.wait_ge(out_st[i], 16 * (TILES // BUF))

        @block.vector
        def _(dve):
            dve.wait_ge(nf_in, 16)
            n = 0

            def step(ins):
                nonlocal n
                n += 1
                ins.then_inc(dve_steps, 1)
                dve.wait_ge(dve_steps, n)

            for t in range(TILES):
                i = t % BUF
                c = lambda q: stt[:, q * TILES + t:q * TILES + t + 1]
                dve.wait_ge(h_in[i], 16 * (t // BUF + 1))
                dve.wait_ge(y_in[i], 16 * (t // BUF + 1))
                for k in range(2):
                    step(nc.vector.scalar_tensor_tensor(h[:, i], y[:, i, k], wts[:, t, k:k + 1], h[:, i], ALU.mult, ALU.add))
                dve.wait_ge(sq_done, t + 1)
                step(nc.vector.tensor_scalar(c(1), c(0), 1.0 / D, EPS, ALU.mult, ALU.add))
                dve.wait_ge(rt_done, t + 1)
                step(nc.vector.reciprocal(c(3), c(2)))
                if t >= BUF:
                    dve.wait_ge(out_st[i], 16 * (t // BUF))
                step(nc.vector.scalar_tensor_tensor(o[:, i], h[:, i], c(3), nf[:], ALU.mult, ALU.mult))


_INS = ["x", "norm_mix", "w_in", "conv_w", "conv_b", "w_rg_a", "b_rg_a", "w_rg_x", "b_rg_x", "rg_lambda",
        "rg_norm", "w_alpha_up", "b_alpha", "gla_norm", "w_out", "norm_ffn", "w_router_group",
        "b_router_group", "w_router_expert", "b_router_expert", "w_exp_gate", "w_exp_up", "w_exp_down",
        "norm_final"]


def kernel(**inputs):
    import numpy as np
    import concourse.bacc as bacc
    from concourse.bass_utils import run_bass_kernel_spmd

    arrays = {n: np.ascontiguousarray(inputs[n]) for n in _INS}
    known = {}
    for _ in range(2):
        nc = bacc.Bacc("TRN2", target_bir_lowering=False, num_devices=1)
        T = {n: nc.dram_tensor(f"in_{n}", a.shape, mybir.dt.from_np(a.dtype), kind="ExternalInput").ap()
             for n, a in arrays.items()}
        T["out"] = nc.dram_tensor("out_0", (1, SEQ, D), F32, kind="ExternalOutput").ap()
        known = build(nc, T, known)
    r = run_bass_kernel_spmd(nc, [{f"in_{n}": a for n, a in arrays.items()}], core_ids=[0])
    return r.results[0]["out_0"]
```

```python
from contextlib import ExitStack

import concourse.bass as bass
from concourse import mybir

F32 = mybir.dt.float32
F32R = mybir.dt.float32r
I32 = mybir.dt.int32
U32 = mybir.dt.uint32
ALU = mybir.AluOpType
ACT = mybir.ActivationFunctionType
AX = mybir.AxisListType.X

P = 128
D = 1024
SEQ = 2048
KT = D // P
RG = 512
CT = RG // P
CONV = 4
HEADS = 4
DK = 64
DV = 128
HP = HEADS * DK // P
RANK = 16
CHUNK = 64
GT = 512
GROUPS = SEQ // GT
TT = GT // P
TILES = SEQ // P
NCH = GT // CHUNK
NG = 4
EPG = 8
NE = NG * EPG
NR = NG + NE
EPS = 1e-6
BLOCKS = (SEQ * 2 + NE * (P - 1) + P - 1) // P
SLOTS = (BLOCKS + 2) * P
UNITS = 12
N_EXP, N_BLOCKS, LAST_TURN, TURN = range(4)
EXPERT = TURN + BLOCKS + 1
SPLIT = EXPERT + NE + 1
TABLE = SPLIT + NE
PLACED_EARLY = 12
GATE_NORM = 16.0
C_RG = 8.0

COL_X, COL_Y, COL_Q, COL_K, COL_V, COL_G, COL_A = 0, 512, 1024, 1280, 1536, 2048, 2560
IN_W = 2576


class Steps:

    def __init__(self, sem, known):
        self.sem, self.known = sem, known
        self.n, self.base, self.per, self.g = 0, 0, None, None
        self.marks = {}

    def begin_loop(self, g):
        self.base, self.n, self.g = self.n, 0, g
        self.ahead, self.marks = self.marks, {}

    def tick(self, name=None):
        self.n += 1
        if name is not None:
            assert name not in self.marks, name
            self.marks[name] = self.n
        return self.sem, 1

    def now(self):
        if self.g is None:
            return self.sem, self.n
        return self.sem, self.base + self.known.get("per", 1) * self.g + self.n

    def at(self, name, g):
        return self.sem, self.known.get("base", 0) + self.known.get("per", 1) * g + self.known.get(name, 1)

    def before(self, name):
        return self.sem, self.known.get("ahead", {}).get(name, 1)

    def table(self):
        return {**self.marks, "base": self.base, "per": self.n, "ahead": self.ahead}


RESULTS = ([(f"T{k}", "AV"[k % 2]) for k in range(KT)]
           + [(f"X{c}", "A") for c in range(CT)] + [("AL", "A")]
           + [(f"V{t}", "A") for t in range(TT)] + [("L0", "V"), ("L1", "V")]
           + [("GA0", "A"), ("GX0", "A")] + [(n, "V") for n in ("Q0", "Q1", "K0", "K1")]
           + [("GA1", "A"), ("GX1", "A"), ("Y0", "A"), ("Y1", "A"), ("KE0", "V"), ("KE1", "V")]
           + [("GA2", "A"), ("GX2", "A"), ("Y2", "A"), ("Y3", "A"), ("GA3", "A"), ("GX3", "A")]
           + [("G0", "V"), ("G1", "V"), ("YT0", "A"), ("G2", "V"), ("SS", "V"), ("YT1", "A"), ("G3", "V"), ("YT2", "A")]
           + [r for t in range(TT) for r in
              ([(f"O{t}{n}", "V") for n in range(2)]
               + ([(f"H{t-1}{q}", "AV"[q]) for q in range(2)] + [(f"R{t-1}", "V")] if t else [("YT3", "A")]))]
           + [(f"H{TT-1}{q}", "AV"[q]) for q in range(2)] + [(f"R{TT-1}", "V")])
ORDER = [r for r, _ in RESULTS]
EMPTIED_BY = dict(RESULTS)


def build(nc, T, known):
    tables = {}
    x_rows = T["x"].rearrange("b s d -> (b s) d")
    out_rows = T["out"].rearrange("b s d -> (b s) d")
    w_in = T["w_in"][0].rearrange("(k p) n -> p k n", p=P)
    h_dram = nc.dram_tensor("h_rows", (SEQ, D), F32, kind="Internal").ap()
    hn_dram = nc.dram_tensor("hn_rows", (SEQ, D), F32, kind="Internal").ap()
    slot_dram = nc.dram_tensor("slot_rows", (SLOTS, 2), I32, kind="Internal").ap()
    y_dram = nc.dram_tensor("y_rows", (2 * SEQ + SLOTS, D), F32, kind="Internal").ap()

    with ExitStack() as ctx:
        def keep_sb(name, shape, dt=F32):
            return ctx.enter_context(nc.sbuf_tensor(name, shape, dt))

        def sem(name):
            return ctx.enter_context(nc.semaphore(name))

        ident = keep_sb("ident", [P, P])
        small = keep_sb("small", [P, TILES * 8 + TABLE], I32)
        rows = small[:, 0:TILES * 4].rearrange("p (t k o) -> p t k o", t=TILES, k=2)
        dest = small[:, TILES * 4:TILES * 6].rearrange("p (t k) -> p t k", t=TILES)
        wts = small[:, TILES * 6:TILES * 8].bitcast(F32).rearrange("p (t k) -> p t k", t=TILES)
        btab = small[:, TILES * 8:]
        squares = small[:, 0:2 * DV].bitcast(F32).rearrange("p (a d) -> p a d", a=2)
        slots_written = sem("slots_written")

        def place_slots(first, last):
            for i in range(first, last):
                t, k = divmod(i, 2)
                nc.gpsimd.indirect_dma_start(slot_dram, bass.IndirectOffsetOnAxis(dest[:, t, k:k + 1], 0),
                                             rows[:, t, k], None).then_inc(slots_written, 16)

        with ExitStack() as inner:
            ones = inner.enter_context(nc.sbuf_tensor("ones", [P, P], F32))
            logits = inner.enter_context(nc.sbuf_tensor("logits", [P, TILES, NR], F32))
            mixer(nc, T, known, tables, x_rows, w_in, h_dram, hn_dram, ident, ones, logits, squares, sem)
            route(nc, slot_dram, ident, ones, logits, dest, rows, wts, btab, place_slots, sem)
        experts(nc, T, slot_dram, hn_dram, y_dram, ident, btab, place_slots, slots_written, sem)
        combine(nc, T, h_dram, y_dram, out_rows, wts, sem)
    return tables


def mixer(nc, T, known, tables, x_rows, w_in, h_dram, hn_dram, ident, ones, logits, osq, sem):
    with ExitStack() as ctx:
        def sb(name, shape, dt=F32):
            return ctx.enter_context(nc.sbuf_tensor(name, shape, dt))

        def ps(name, shape, dt=F32):
            return ctx.enter_context(nc.psum_tensor(name, shape, dt))

        wout = sb("wout", [P, KT, D])
        wal = sb("wal", [P, KT, RANK])
        wup = sb("wup", [RANK, HP * P])
        wrt = sb("wrt", [P, KT, NR])
        bd = sb("bd", [P, 2, CT, P])
        nmix = sb("nmix", [P, KT])
        nffn = sb("nffn", [P, D])
        cw = sb("cw", [P, CT, CONV])
        cb = sb("cb", [P, CT])
        gb = sb("gb", [P, 2, CT])
        lam = sb("lam", [P, CT])
        sp = sb("sp", [P, 4, CT])
        rgn = sb("rgn", [P, CT])
        glan = sb("glan", [P, 1])
        bal = sb("bal", [P, HP])
        rbias = sb("rbias", [P, NR])
        keepm = sb("keepm", [P, HEADS * P], U32)
        restart = sb("restart", [P, GT])
        ring = sb("ring", [P, 4, KT, P])
        wvg = sb("wvg", [P, KT, RG])
        xs = sb("xs", [P, TT, D])
        hnT = sb("hnT", [P, KT, GT])
        xr = sb("xr", [P, CT, GT + CONV - 1])
        xc = sb("xc", [P, CT, GT])
        yr = sb("yr", [P, CT, GT])
        rg_tmp = sb("rg_tmp", [P, 5, GT])
        rt, it, at_, th, uu = (rg_tmp[:, i] for i in range(5))
        junk = rg_tmp[:, 0:2].rearrange("p a b -> p (a b)")
        hcar = sb("hcar", [P, CT])
        alow = uu[0:RANK]
        qk = sb("qk", [P, 4, GT])
        ks = sb("ks", [P, HP, GT])
        z_all = sb("z_all", [P, 2 * HP, GT])
        z1, z2 = z_all[:, 0:HP], z_all[:, HP:]
        attmask = z1[:, 0]
        bb = sb("bb", [P, HP, GT])
        dc = sb("dc", [P, HP, NCH])
        keT = sb("keT", [P, TT, HP * P])
        vt = sb("vt", [P, TT, RG])
        sg = sb("sg", [P, TT, RG])
        att = sb("att", [P, 2, HEADS * P])
        st = sb("st", [P, 2, HP, DV])
        ot = sb("ot", [P, TT, RG])
        yT = z_all[:, 0:CT]
        hres = [hnT[:, 6:8, :].rearrange("p a b -> p (a b)"), bb[:].rearrange("p a b -> p (a b)")]
        stat = sb("stat", [P, 64])
        hn2 = [hnT[:, 2 + 2 * i:4 + 2 * i, :].rearrange("p a b -> p (a b)") for i in range(2)]
        hn2T = hnT[:, 0:2, :].rearrange("p a (b t) -> p (a b) t", t=P)
        big = [ps(f"big{i}", [P, 512]) for i in range(4)]
        attp = [ps(f"attp{i}", [P, HEADS * P]) for i in range(2)]
        kvp = ps("kvp", [P, 2, HP, DV])
        op = ps("op", [P, HEADS * DV])

        consts_in = sem("m_consts_in")
        wout_in = sem("m_wout_in")
        consts_made = sem("m_consts_made")
        wout_scaled = sem("m_wout_scaled")
        wring_in = [sem(f"m_wring_in{i}") for i in range(4)]
        wvg_in = sem("m_wvg_in")
        x_in = sem("m_x_in")
        hres_in = [sem(f"m_hres_in{i}") for i in range(2)]
        h_out = [sem(f"m_h_out{i}") for i in range(2)]
        hn_ready = sem("m_hn_ready")
        hn_stat = sem("m_hn_stat")
        hn_rs = sem("m_hn_rs")
        group_done = sem("m_group_done")
        prep = sem("m_prep")
        passed_p = sem("m_passed_p")
        passed_s = sem("m_passed_s")
        passed_v = sem("m_passed_v")
        S = {k: Steps(sem(f"m_steps_{k}"), known.get(k, {})) for k in "PAV"}
        PE_, A_, V_ = S["P"], S["A"], S["V"]

        def now_in(E, g):
            return E.now()

        block = ctx.enter_context(nc.Block())
        tile_cols = ([COL_X + c * P for c in range(CT)] + [COL_Q + c * P for c in range(HP)]
                     + [COL_K + c * P for c in range(HP)] + [COL_Y + c * P for c in range(CT)])
        tile_names = [f"X{c}" for c in range(CT)] + ["Q0", "Q1", "K0", "K1"] + [f"Y{c}" for c in range(CT)]

        N_CONST = 15 + CONV + 4

        @block.sync
        def _(sync):
            def ring_load(i):
                c = tile_cols[i % 12]
                sync.dma_start(ring[:, i % 4], w_in[:, :, c:c + P]).then_inc(wring_in[i % 4], 16)

            def const(dst, src):
                sync.dma_start(dst, src, allow_slow_non_contiguous=True).then_inc(consts_in, 16)

            sync.dma_start(xs[:], x_rows[0:GT].rearrange("(t p) d -> p t d", p=P)).then_inc(x_in, 16)
            const(nmix[:], T["norm_mix"][0].rearrange("(k p) -> p k", p=P))
            const(nffn[:], T["norm_ffn"].partition_broadcast(P))
            const(wal[:], w_in[:, :, COL_A:COL_A + RANK])
            const(wup[:], T["w_alpha_up"][0])
            const(cb[:], T["conv_b"][0].rearrange("(c p) -> p c", p=P))
            const(gb[:, 0], T["b_rg_a"][0].rearrange("(c b) i -> (b i) c", b=2))
            const(gb[:, 1], T["b_rg_x"][0].rearrange("(c b) i -> (b i) c", b=2))
            const(lam[:], T["rg_lambda"][0].rearrange("(c p) -> p c", p=P))
            const(rgn[:], T["rg_norm"][0].rearrange("(c p) -> p c", p=P))
            const(glan[:], T["gla_norm"][0].rearrange("(p a) -> p a", a=1))
            const(bal[:], T["b_alpha"][0].rearrange("(c p) -> p c", p=P))
            const(wrt[:, :, 0:NG], T["w_router_group"][0].rearrange("(k p) n -> p k n", p=P))
            const(wrt[:, :, NG:NR], T["w_router_expert"][0].rearrange("(k p) n -> p k n", p=P))
            const(rbias[:, 0:NG], T["b_router_group"].partition_broadcast(P))
            const(rbias[:, NG:NR], T["b_router_expert"].partition_broadcast(P))
            for j in range(CONV):
                sync.dma_start(cw[:, :, j], T["conv_w"][0, j].rearrange("(c p) -> p c", p=P),
                               allow_slow_non_contiguous=True).then_inc(consts_in, 16)
            for i in range(4):
                ring_load(i)
            sync.dma_start(wvg[:], w_in[:, :, COL_V:COL_V + RG]).then_inc(wvg_in, 16)
            sync.wait_ge(prep, 1)
            for i, w in enumerate(("w_rg_a", "w_rg_x")):
                for b in range(2):
                    src = T[w][0].rearrange("(c b) i j -> b i c j", b=2)[b]
                    const(bd[b * 64:(b + 1) * 64, i, :, b * 64:(b + 1) * 64], src)
            sync.dma_start(wout[:], T["w_out"][0].rearrange("(k p) n -> p k n", p=P)).then_inc(wout_in, 16)

            with sync.Fori(0, GROUPS) as g:
                sync.wait_ge(*PE_.at("T7", g))
                nx = ((g + 1) % GROUPS) * GT
                sync.dma_start(xs[:], x_rows[bass.ds(nx, GT), :].rearrange("(t p) d -> p t d", p=P)).then_inc(x_in, 16)
                for i in range(4):
                    sync.wait_ge(*PE_.at(tile_names[i], g))
                    ring_load(i + 4)
                sync.wait_ge(*PE_.at("V3", g))
                sync.dma_start(wvg[:], w_in[:, :, COL_G:COL_G + RG]).then_inc(wvg_in, 16)
                for i in range(4, 12):
                    sync.wait_ge(*PE_.at(tile_names[i], g))
                    ring_load(i + 4)
                sync.wait_ge(*PE_.at("G3", g))
                sync.dma_start(wvg[:], w_in[:, :, COL_V:COL_V + RG]).then_inc(wvg_in, 16)
                sync.wait_ge(*V_.at("ke", g))
                for t in range(2):
                    sync.dma_start(hres[t], x_rows[bass.ds(g * GT + t * P, P), :]).then_inc(hres_in[t], 16)
                for t in range(TT):
                    sync.wait_ge(*V_.at(f"h{t}", g))
                    sync.dma_start(h_dram[bass.ds(g * GT + t * P, P), :], hres[t % 2]).then_inc(h_out[t % 2], 16)
                    sync.wait_ge(*V_.at(f"hn{t}", g))
                    sync.dma_start(hn_dram[bass.ds(g * GT + t * P, P), :], hn2[t % 2]).then_inc(h_out[t % 2], 16)
                    if t + 2 < TT:
                        sync.wait_ge(h_out[t % 2], 64 * g + 32)
                        sync.dma_start(hres[t % 2], x_rows[bass.ds(g * GT + (t + 2) * P, P), :]).then_inc(hres_in[t % 2], 16)
                for i in range(2):
                    sync.wait_ge(h_out[i], 64 * (g + 1))
                sync.sem_inc(passed_s, 1)
            sync.wait_ge(x_in, 16 * (GROUPS + 1))
            sync.wait_ge(wvg_in, 16 * (2 * GROUPS + 1))
            for i in range(4):
                sync.wait_ge(wring_in[i], 16 * (3 * GROUPS + 1))

        @block.gpsimd
        def _(pool):
            nc.gpsimd.memset(bd[:], 0.0).then_inc(prep, 1)
            nc.gpsimd.memset(ident[:], 0.0).then_inc(consts_made, 1)
            nc.gpsimd.memset(ones[:], 1.0).then_inc(consts_made, 1)
            nc.gpsimd.memset(attmask, 1.0).then_inc(consts_made, 1)
            nc.gpsimd.memset(restart[:], 1.0).then_inc(consts_made, 1)
            pool.wait_ge(consts_made, 4)
            nc.gpsimd.memset(restart[:].rearrange("p (n c) -> p n c", c=CHUNK)[:, :, 0:1], 0.0).then_inc(consts_made, 1)
            nc.gpsimd.affine_select(out=ident[:], in_=ident[:], compare_op=ALU.not_equal, fill=1.0, base=0,
                                    pattern=[[-1, P]], channel_multiplier=1).then_inc(consts_made, 1)
            am = attmask.rearrange("p (h i) -> p h i", h=HEADS)
            nc.gpsimd.affine_select(out=am, in_=am, compare_op=ALU.is_ge, fill=0.0, base=0,
                                    pattern=[[0, HEADS], [1, P]], channel_multiplier=-1).then_inc(consts_made, 1)
            pool.wait_ge(consts_made, 7)
            nc.gpsimd.memset(am[0:CHUNK, :, CHUNK:P], 0.0).then_inc(consts_made, 1)
            pool.wait_ge(consts_in, 16 * N_CONST)
            pool.wait_ge(wout_in, 16)
            for k in range(KT):
                s = rgn[:, k:k + 1] if k < CT else glan[:]
                nc.gpsimd.tensor_scalar(wout[:, k], wout[:, k], s, None, ALU.mult).then_inc(wout_scaled, 1)

        @block.scalar
        def _(act):
            A = A_

            def own():
                act.wait_ge(*A.now())

            def softplus():
                act.wait_ge(consts_in, 16 * N_CONST)
                nc.scalar.activation(sp[:, 0], lam[:], ACT.Abs).then_inc(*A.tick("p0"))
                own()
                nc.scalar.activation(sp[:, 1], sp[:, 0], ACT.Exp, scale=-1.0).then_inc(*A.tick("p1"))
                own()
                nc.scalar.activation(sp[:, 2], sp[:, 1], ACT.Ln, bias=1.0).then_inc(*A.tick("p2"))

            def norm_stats(n):
                act.wait_ge(x_in, 16 * (n + 1))
                for t in range(TT):
                    if t:
                        act.wait_ge(hn_stat, (TT + 1) * n + t)
                    nc.scalar.activation(junk, xs[:, t], ACT.Square, accum_out=stat[:, t:t + 1]).then_inc(hn_stat, 1)
                act.wait_ge(hn_rs, 2 * n + 1)
                nc.scalar.activation(stat[:, 8:12], stat[:, 4:8], ACT.Sqrt).then_inc(hn_stat, 1)

            norm_stats(0)
            softplus()

            act.wait_ge(*V_.before("sp"))
            with act.Fori(0, GROUPS) as g:
                A.begin_loop(g)

                def empty(name, dst, **kw):
                    i = ORDER.index(name)
                    func = kw.pop("func", ACT.Copy)
                    act.wait_ge(*PE_.at(name, g))
                    own()
                    nc.scalar.activation(dst, kw.pop("src", big[i % 4][:]), func, **kw).then_inc(*A.tick(kw_name(name)))

                def kw_name(name):
                    return "e:" + name if EMPTIED_BY[name] == "A" else "a:" + name

                for k in range(0, KT, 2):
                    empty(f"T{k}", hnT[:, k], scale=nmix[:, k:k + 1])
                for c in range(CT):
                    empty(f"X{c}", xr[:, c, CONV - 1:])
                empty("AL", alow, src=big[ORDER.index("AL") % 4][0:RANK, :])
                for t in range(TT):
                    empty(f"V{t}", vt[:, t])
                for c in range(HP):
                    empty(f"L{c}", z1[:, c], func=ACT.Abs, bias=bal[:, c:c + 1])
                own()
                nc.scalar.activation(z1, z1, ACT.Exp, scale=-1.0).then_inc(*A.tick())
                own()
                nc.scalar.activation(z1, z1, ACT.Ln, bias=1.0).then_inc(*A.tick("ln"))

                def gates(c):
                    if c:
                        act.wait_ge(*V_.at(f"scan{c-1}", g))
                    empty(f"GA{c}", rt, func=ACT.Sigmoid, bias=gb[:, 0, c:c + 1])
                    empty(f"GX{c}", it, func=ACT.Sigmoid, bias=gb[:, 1, c:c + 1])
                    own()
                    nc.scalar.activation(at_, rt, ACT.Exp, scale=sp[:, 0, c:c + 1]).then_inc(*A.tick())
                    nc.scalar.activation(th, rt, ACT.Tanh, scale=sp[:, 3, c:c + 1]).then_inc(*A.tick(f"th{c}"))
                    act.wait_ge(*V_.at(f"oma{c}", g))
                    own()
                    nc.scalar.activation(th, th, ACT.Sqrt).then_inc(*A.tick(f"sq{c}"))

                def attended(t):
                    act.wait_ge(*PE_.at(f"o{t}", g))
                    nc.scalar.activation(ot[:, t], op[:], ACT.Copy).then_inc(*A.tick(f"o{t}"))
                    for h in range(HEADS):
                        if h % 2 == 0:
                            own()
                        j = 32 + t * HEADS + h
                        nc.scalar.activation(osq[:, h % 2], ot[:, t, h * DV:(h + 1) * DV],
                                             ACT.Square, accum_out=stat[:, j:j + 1]).then_inc(*A.tick(f"os{t}" if h == HEADS - 1 else None))

                def root(name, cols):
                    act.wait_ge(*V_.at(name, g))
                    own()
                    nc.scalar.activation(cols, cols, ACT.Sqrt).then_inc(*A.tick("rt:" + name))

                def silu(t):
                    empty(f"G{t}", sg[:, t], func=ACT.Sigmoid)

                def turned(t):
                    empty(f"YT{t}", yT[:, :, t * P:(t + 1) * P], src=big[ORDER.index(f"YT{t}") % 4][:].rearrange("p (h t) -> p h t", h=HEADS))

                gates(0)
                act.wait_ge(*V_.at("b", g))
                own()
                nc.scalar.activation(z1, bb[:], ACT.Exp, scale=1.0 / GATE_NORM).then_inc(*A.tick("eb"))
                nc.scalar.activation(z2, bb[:], ACT.Exp, scale=-1.0 / GATE_NORM).then_inc(*A.tick("enb"))
                last = bb[:].rearrange("p a (n c) -> p a n c", c=CHUNK)[:, :, :, CHUNK - 1]
                nc.scalar.activation(dc[:], last, ACT.Exp, scale=1.0 / GATE_NORM).then_inc(*A.tick("dc"))
                act.wait_ge(*V_.at("bend", g))
                own()
                nc.scalar.activation(z1, z1, ACT.Exp, scale=1.0 / GATE_NORM).then_inc(*A.tick("eend"))
                gates(1)
                for c in range(2):
                    empty(f"Y{c}", yr[:, c], func=ACT.Gelu_apprx_tanh)
                gates(2)
                empty("Y2", yr[:, 2], func=ACT.Gelu_apprx_tanh)
                attended(0)
                empty("Y3", yr[:, 3], func=ACT.Gelu_apprx_tanh)
                gates(3)
                silu(0)
                root("oms0", stat[:, 48:52])
                attended(1)
                silu(1)
                for c in range(CT):
                    act.wait_ge(*V_.at(f"y{c}", g))
                    own()
                    nc.scalar.activation(xc[:, c], yr[:, c], ACT.Square).then_inc(*A.tick(f"ysq{c}"))
                turned(0)
                silu(2)
                root("oms1", stat[:, 52:56])
                attended(2)
                root("yms", uu)
                turned(1)
                silu(3)
                root("oms2", stat[:, 56:60])
                norm_stats(g + 1)
                attended(3)
                turned(2)
                root("oms3", stat[:, 60:64])
                turned(3)
                for t in range(TT + 1):
                    if t:
                        empty(f"H{t-1}0", hn2T[:, 0:4], src=big[ORDER.index(f"H{t-1}0") % 4][:].rearrange("p (k t) -> p k t", k=4))
                    if t < TT:
                        act.wait_ge(*V_.at(f"h{t}", g))
                        own()
                        nc.scalar.activation(junk, hres[t % 2], ACT.Square, accum_out=stat[:, 16 + t:17 + t]).then_inc(*A.tick(f"hsq{t}"))
                        root(f"hms{t}", stat[:, 20 + t:21 + t])
                for i in range(2):
                    act.wait_ge(h_out[i], 64 * (g + 1))
                tables["A"] = A.table()

        @block.vector
        def _(dve):
            V = V_

            def own():
                dve.wait_ge(*V.now())

            def op1(name, fn, *a, **k):
                own()
                fn(*a, **k).then_inc(*V.tick(name))

            nc.vector.memset(xr[:, :, 0:CONV - 1], 0.0).then_inc(*V.tick())
            nc.vector.memset(hcar[:], 0.0).then_inc(*V.tick())
            nc.vector.memset(att[:], 0.0).then_inc(*V.tick())
            nc.vector.memset(st[:], 0.0).then_inc(*V.tick("zeroed"))
            dve.wait_ge(consts_made, 8)
            nc.vector.tensor_copy(keepm[:], attmask).then_inc(*V.tick())
            def norm_rows(n):
                dve.wait_ge(hn_stat, (TT + 1) * n + TT)
                if not isinstance(n, int):
                    dve.wait_ge(hn_ready, TT * n)
                nc.vector.tensor_scalar(stat[:, 4:8], stat[:, 0:4], 1.0 / D, EPS, ALU.mult, ALU.add).then_inc(hn_rs, 1)
                dve.wait_ge(hn_stat, (TT + 1) * (n + 1))
                nc.vector.reciprocal(stat[:, 12:16], stat[:, 8:12]).then_inc(hn_rs, 1)
                dve.wait_ge(hn_rs, 2 * n + 2)
                for t in range(TT):
                    nc.vector.tensor_scalar(xs[:, t], xs[:, t], stat[:, 12 + t:13 + t], None, ALU.mult).then_inc(hn_ready, 1)

            norm_rows(0)
            dve.sem_inc(group_done, 1)
            dve.wait_ge(*A_.before("p2"))
            nc.vector.tensor_scalar(sp[:, 1], lam[:], -1.0, 0.0, ALU.mult, ALU.max).then_inc(*V.tick())
            own()
            nc.vector.tensor_tensor(sp[:, 1], sp[:, 1], sp[:, 2], ALU.add).then_inc(*V.tick())
            own()
            nc.vector.tensor_scalar(sp[:, 0], sp[:, 1], -C_RG, None, ALU.mult).then_inc(*V.tick())
            nc.vector.tensor_scalar(sp[:, 3], sp[:, 1], C_RG, None, ALU.mult).then_inc(*V.tick("sp"))
            with dve.Fori(0, GROUPS) as g:
                V.begin_loop(g)

                def result(name):
                    dve.wait_ge(*PE_.at(name, g))
                    own()
                    return big[ORDER.index(name) % 4]

                for k in range(1, KT, 2):
                    b = result(f"T{k}")
                    nc.vector.tensor_scalar(hnT[:, k], b[:], nmix[:, k:k + 1], None, ALU.mult).then_inc(*V.tick(f"e:T{k}"))
                for c in range(CT):
                    dve.wait_ge(*A_.at(f"e:X{c}", g))
                    own()
                    nc.vector.tensor_scalar(xc[:, c], xr[:, c, 0:GT], cw[:, c, 0:1], cb[:, c:c + 1], ALU.mult, ALU.add).then_inc(*V.tick())
                    for j in range(1, CONV):
                        own()
                        nc.vector.scalar_tensor_tensor(xc[:, c], xr[:, c, j:j + GT], cw[:, c, j:j + 1], xc[:, c],
                                                       ALU.mult, ALU.add).then_inc(*V.tick(f"xc{c}" if j == CONV - 1 else None))
                own()
                nc.vector.tensor_copy(xr[:, :, 0:CONV - 1], xr[:, :, GT:GT + CONV - 1]).then_inc(*V.tick("halo"))
                for c in range(HP):
                    b = result(f"L{c}")
                    dve.wait_ge(*A_.at(f"a:L{c}", g))
                    nc.vector.tensor_scalar(z2[:, c], b[:], bal[:, c:c + 1], 0.0, ALU.add, ALU.min).then_inc(*V.tick(f"e:L{c}"))
                dve.wait_ge(*A_.at("ln", g))
                own()
                nc.vector.tensor_tensor(z2, z2, z1, ALU.subtract).then_inc(*V.tick())
                for c in range(HP):
                    own()
                    nc.vector.tensor_tensor_scan(bb[:, c], restart[:], z2[:, c], 0.0, ALU.mult, ALU.add).then_inc(*V.tick("b" if c == HP - 1 else None))

                def rg(c):
                    dve.wait_ge(*A_.at(f"th{c}", g))
                    own()
                    nc.vector.tensor_scalar(uu, th, 1.0, None, ALU.add).then_inc(*V.tick())
                    own()
                    nc.vector.reciprocal(uu, uu).then_inc(*V.tick())
                    own()
                    nc.vector.scalar_tensor_tensor(th, th, 2.0, uu, ALU.mult, ALU.mult).then_inc(*V.tick(f"oma{c}"))
                    own()
                    nc.vector.tensor_tensor(it, it, xc[:, c], ALU.mult).then_inc(*V.tick())
                    dve.wait_ge(*A_.at(f"sq{c}", g))
                    own()
                    nc.vector.tensor_tensor(uu, th, it, ALU.mult).then_inc(*V.tick())
                    own()
                    nc.vector.tensor_tensor_scan(xc[:, c], at_, uu, hcar[:, c:c + 1], ALU.mult, ALU.add).then_inc(*V.tick(f"scan{c}"))
                    own()
                    nc.vector.tensor_copy(hcar[:, c:c + 1], xc[:, c, GT - 1:GT]).then_inc(*V.tick())

                def keep(t):
                    dve.wait_ge(*PE_.at(f"att{t}", g))
                    if t >= 2:
                        dve.wait_ge(*PE_.at(f"o{t-2}", g))
                    own()
                    dve.sem_inc(passed_v, 1)
                    nc.vector.copy_predicated(att[:, t % 2], keepm[:], attp[t % 2][:]).then_inc(*V.tick(f"keep{t}"))

                def state(j):
                    t, ch = divmod(j - 1, 2)
                    dve.wait_ge(*PE_.at(f"kv{t}", g))
                    if ch:
                        dve.wait_ge(*PE_.at(f"oc{t}", g))
                    elif t:
                        dve.wait_ge(*PE_.at(f"o{t-1}", g))
                    own()
                    for c in range(HP):
                        nc.vector.scalar_tensor_tensor(st[:, j % 2, c], st[:, (j + 1) % 2, c], dc[:, c, j - 1:j],
                                                       kvp[:, ch, c], ALU.mult, ALU.add).then_inc(*V.tick(f"st{j}" if c else None))

                def silu(t):
                    b = result(f"G{t}")
                    dve.wait_ge(*A_.at(f"a:G{t}", g))
                    nc.vector.tensor_tensor(sg[:, t], b[:], sg[:, t], ALU.mult).then_inc(*V.tick(f"e:G{t}"))

                def mean_sq(t):
                    dve.wait_ge(*A_.at(f"os{t}", g))
                    own()
                    nc.vector.tensor_scalar(stat[:, 48 + 4 * t:52 + 4 * t], stat[:, 32 + 4 * t:36 + 4 * t], 1.0 / DV, EPS,
                                            ALU.mult, ALU.add).then_inc(*V.tick(f"oms{t}"))

                def norm_heads(t):
                    dve.wait_ge(*A_.at(f"rt:oms{t}", g))
                    own()
                    nc.vector.reciprocal(stat[:, 48 + 4 * t:52 + 4 * t], stat[:, 48 + 4 * t:52 + 4 * t]).then_inc(*V.tick())
                    own()
                    for h in range(HEADS):
                        cs = slice(h * DV, (h + 1) * DV)
                        j = 48 + t * HEADS + h
                        nc.vector.scalar_tensor_tensor(ot[:, t, cs], ot[:, t, cs], stat[:, j:j + 1], sg[:, t, cs],
                                                       ALU.mult, ALU.mult).then_inc(*V.tick(f"on{t}" if h == HEADS - 1 else None))

                rg(0)
                for i, n in enumerate(("Q0", "Q1", "K0", "K1")):
                    b = result(n)
                    nc.vector.tensor_copy(qk[:, i], b[:]).then_inc(*V.tick("e:" + n))
                dve.wait_ge(*A_.at("enb", g))
                own()
                nc.vector.scalar_tensor_tensor(qk[:, 0:HP], qk[:, 0:HP], DK ** -0.5, z1, ALU.mult, ALU.mult).then_inc(*V.tick("qs"))
                nc.vector.tensor_tensor(ks[:], qk[:, HP:], z2, ALU.mult).then_inc(*V.tick("ks"))
                own()
                for c in range(HP):
                    bc = bb[:, c].rearrange("p (n c) -> p n c", c=CHUNK)
                    nc.vector.tensor_tensor(z1[:, c].rearrange("p (n c) -> p n c", c=CHUNK),
                                            bc[:, :, CHUNK - 1:CHUNK].to_broadcast([P, NCH, CHUNK]), bc,
                                            ALU.subtract).then_inc(*V.tick("bend" if c else None))
                dve.wait_ge(*A_.at("eend", g))
                own()
                nc.vector.tensor_tensor(qk[:, HP:], qk[:, HP:], z1, ALU.mult).then_inc(*V.tick("ke"))
                rg(1)
                for q in range(2):
                    b = result(f"KE{q}")
                    nc.vector.tensor_copy(keT[:, 2 * q:2 * q + 2], b[:].rearrange("p (t c) -> p t c", t=2)).then_inc(*V.tick(f"e:KE{q}"))
                keep(0)
                state(1)
                keep(1)
                rg(2)
                state(2)
                mean_sq(0)
                state(3)
                keep(2)
                rg(3)
                silu(0)
                norm_heads(0)
                state(4)
                mean_sq(1)
                for c in range(CT):
                    dve.wait_ge(*A_.at(f"e:Y{c}", g))
                    own()
                    nc.vector.tensor_tensor(yr[:, c], xc[:, c], yr[:, c], ALU.mult).then_inc(*V.tick(f"y{c}"))
                silu(1)
                state(5)
                keep(3)
                silu(2)
                norm_heads(1)
                state(6)
                mean_sq(2)
                b = result("SS")
                nc.vector.tensor_scalar(uu, b[:], 1.0 / RG, EPS, ALU.mult, ALU.add).then_inc(*V.tick("e:SS"))
                V.marks["yms"] = V.n
                silu(3)
                norm_heads(2)
                dve.wait_ge(*A_.at("rt:yms", g))
                own()
                nc.vector.reciprocal(uu, uu).then_inc(*V.tick())
                own()
                for c in range(CT):
                    nc.vector.tensor_tensor(yr[:, c], yr[:, c], uu, ALU.mult).then_inc(*V.tick("yn" if c == CT - 1 else None))
                norm_rows(g + 1)
                state(7)
                state(8)
                mean_sq(3)
                norm_heads(3)
                for t in range(TT + 1):
                    if t < TT:
                        for n in range(2):
                            hs = hres[t % 2][:, n * 512:(n + 1) * 512]
                            b = result(f"O{t}{n}")
                            dve.wait_ge(hres_in[t % 2], 32 * g + 16 * (t // 2 + 1))
                            nc.vector.tensor_tensor(hs, b[:], hs, ALU.add).then_inc(*V.tick(f"e:O{t}{n}"))
                        V.marks[f"h{t}"] = V.n
                    if t:
                        b = result(f"H{t-1}1")
                        nc.vector.tensor_copy(hn2T[:, 4:8], b[:].rearrange("p (k t) -> p k t", k=4)).then_inc(*V.tick(f"e:H{t-1}1"))
                    if t < TT:
                        dve.wait_ge(*A_.at(f"hsq{t}", g))
                        own()
                        nc.vector.tensor_scalar(stat[:, 20 + t:21 + t], stat[:, 16 + t:17 + t], 1.0 / D, EPS, ALU.mult, ALU.add).then_inc(*V.tick(f"hms{t}"))
                    if t:
                        b = result(f"R{t-1}")
                        nc.vector.tensor_tensor(logits[:, bass.ds(g * TT + t - 1, 1), :], b[:, 0:NR].rearrange("p (a n) -> p a n", a=1),
                                                rbias[:].rearrange("p (a n) -> p a n", a=1),
                                                ALU.add).then_inc(*(V.tick(f"e:R{t-1}") if t < TT else (group_done, 1)))
                    if t < TT:
                        dve.wait_ge(*A_.at(f"rt:hms{t}", g))
                        own()
                        nc.vector.reciprocal(stat[:, 24 + t:25 + t], stat[:, 20 + t:21 + t]).then_inc(*V.tick())
                        own()
                        if t >= 2:
                            dve.wait_ge(h_out[t % 2], 64 * g + 32)
                            dve.wait_ge(*PE_.at(f"H{t-2}1", g))
                        nc.vector.scalar_tensor_tensor(hn2[t % 2], hres[t % 2], stat[:, 24 + t:25 + t], nffn[:], ALU.mult, ALU.mult).then_inc(*V.tick(f"hn{t}"))
                for i in range(2):
                    dve.wait_ge(h_out[i], 64 * (g + 1))
                tables["V"] = V.table()

        @block.tensor
        def _(pe):
            pe.wait_ge(consts_made, 8)
            pe.wait_ge(consts_in, 16 * N_CONST)
            with pe.Fori(0, GROUPS) as g:
                PE_.begin_loop(g)

                def bank(name):
                    i = ORDER.index(name)
                    if i >= 4:
                        E = A_ if EMPTIED_BY[ORDER[i - 4]] == "A" else V_
                        pe.wait_ge(*E.at("e:" + ORDER[i - 4], g))
                    return big[i % 4]

                pe.wait_ge(group_done, g + 1)
                pe.wait_ge(hn_ready, TT * (g + 1))
                for k in range(KT):
                    b = bank(f"T{k}")
                    for t in range(TT):
                        m = nc.tensor.transpose(b[:, t * P:(t + 1) * P], xs[:, t, k * P:(k + 1) * P], ident[:])
                    m.then_inc(*PE_.tick(f"T{k}"))
                pe.wait_ge(*A_.at(f"e:T{KT-2}", g))
                pe.wait_ge(*V_.at(f"e:T{KT-1}", g))

                def channels(i):
                    n = tile_names[i]
                    b = bank(n)
                    pe.wait_ge(wring_in[i % 4], 48 * g + 16 * (i // 4 + 1))
                    for k in range(KT):
                        m = nc.tensor.matmul(b[:], ring[:, i % 4, k], hnT[:, k], start=(k == 0), stop=(k == KT - 1))
                    m.then_inc(*PE_.tick(n))

                def tokens(n, t):
                    b = bank(f"{n}{t}")
                    pe.wait_ge(wvg_in, 32 * g + (16 if n == "V" else 32))
                    for k in range(KT):
                        m = nc.tensor.matmul(b[:], hnT[:, k, t * P:(t + 1) * P], wvg[:, k], start=(k == 0), stop=(k == KT - 1))
                    m.then_inc(*PE_.tick(f"{n}{t}"))

                def gates(c):
                    for i, n in enumerate((f"GA{c}", f"GX{c}")):
                        b = bank(n)
                        pe.wait_ge(*V_.at(f"xc{c}", g))
                        nc.tensor.matmul(b[:], bd[:, i, c], xc[:, c], start=True, stop=True).then_inc(*PE_.tick(n))

                def decayed_keys(q):
                    b = bank(f"KE{q}")
                    pe.wait_ge(*V_.at("ke", g))
                    for t in range(2):
                        for c in range(HP):
                            tt = 2 * q + t
                            m = nc.tensor.transpose(b[:, (t * HP + c) * P:(t * HP + c + 1) * P],
                                                    qk[:, HP + c, tt * P:(tt + 1) * P], ident[:])
                    m.then_inc(*PE_.tick(f"KE{q}"))

                by_rows = [h for r in range(2) for h in range(r, HEADS, 2)]

                def rows_apart():
                    pe.wait_ge(*PE_.now())
                    pe.sem_inc(passed_p, 1)

                def scores(t):
                    if t >= 2:
                        pe.wait_ge(*V_.at(f"keep{t-2}", g))
                    else:
                        pe.wait_ge(*V_.at("ks", g))
                    for i, h in enumerate(by_rows):
                        if i == HP:
                            m.then_inc(*PE_.tick())
                            rows_apart()
                        r, c = slice(DK * (h % 2), DK * (h % 2) + DK), h // 2
                        m = nc.tensor.matmul(attp[t % 2][:, h * P:(h + 1) * P], ks[r, c, t * P:(t + 1) * P],
                                             qk[r, c, t * P:(t + 1) * P], start=True, stop=True)
                    m.then_inc(*PE_.tick(f"att{t}"))

                def outer(t):
                    pe.wait_ge(*V_.at(f"e:KE{t//2}", g))
                    if t:
                        pe.wait_ge(*V_.at(f"st{2*t}", g))
                    for ch in range(2):
                        for h in range(HEADS):
                            r, c = slice(DK * (h % 2), DK * (h % 2) + DK), h // 2
                            tk = slice(CHUNK * ch, CHUNK * ch + CHUNK)
                            if h == 0:
                                if ch:
                                    m.then_inc(*PE_.tick())
                                rows_apart()
                            m = nc.tensor.matmul(kvp[r, ch, c], keT[tk, t, h * DK:(h + 1) * DK], vt[tk, t, h * DV:(h + 1) * DV],
                                                 start=True, stop=True, skip_group_check=True)
                    m.then_inc(*PE_.tick(f"kv{t}"))

                def attend(t):
                    pe.wait_ge(*V_.at(f"keep{t}", g))
                    if t:
                        pe.wait_ge(*A_.at(f"o{t-1}", g))
                    for h in range(HEADS):
                        cs = slice(h * DV, (h + 1) * DV)
                        m = nc.tensor.matmul(op[:, cs], att[:, t % 2, h * P:(h + 1) * P], vt[:, t, cs],
                                             start=(h == 0), stop=False, skip_group_check=True)
                    for ch in range(2):
                        j = 2 * t + ch
                        if j:
                            pe.wait_ge(*V_.at(f"st{j}", g))
                        m.then_inc(*PE_.tick())
                        rows_apart()
                        for i, h in enumerate(by_rows):
                            if i == HP:
                                m.then_inc(*PE_.tick())
                                rows_apart()
                            r, c = slice(DK * (h % 2), DK * (h % 2) + DK), h // 2
                            tk = slice(CHUNK * ch, CHUNK * ch + CHUNK)
                            m = nc.tensor.matmul(op[tk, h * DV:(h + 1) * DV], qk[r, c, t * P + CHUNK * ch:t * P + CHUNK * (ch + 1)],
                                                 st[r, j % 2, c], start=False, stop=(ch == 1), skip_group_check=True)
                        PE_.marks[f"oc{t}" if ch == 0 else f"o{t}"] = PE_.n + 1
                        if ch == 1:
                            m.then_inc(*PE_.tick())

                def turn_o(t):
                    b = bank(f"YT{t}")
                    pe.wait_ge(*V_.at(f"on{t}", g))
                    for h in range(HEADS):
                        m = nc.tensor.transpose(b[:, h * P:(h + 1) * P], ot[:, t, h * DV:(h + 1) * DV], ident[:])
                    m.then_inc(*PE_.tick(f"YT{t}"))

                def out(t):
                    for n in range(2):
                        ns = slice(n * 512, (n + 1) * 512)
                        b = bank(f"O{t}{n}")
                        pe.wait_ge(*V_.at("yn", g))
                        pe.wait_ge(*A_.at(f"e:YT{t}", g))
                        for k in range(KT):
                            y = yr[:, k, t * P:(t + 1) * P] if k < CT else yT[:, k - CT, t * P:(t + 1) * P]
                            m = nc.tensor.matmul(b[:], y, wout[:, k, ns], start=(k == 0), stop=(k == KT - 1))
                        m.then_inc(*PE_.tick(f"O{t}{n}"))

                def router(t):
                    for q in range(2):
                        b = bank(f"H{t}{q}")
                        pe.wait_ge(*V_.at(f"hn{t}", g))
                        for k in range(4):
                            kk = 4 * q + k
                            m = nc.tensor.transpose(b[:, k * P:(k + 1) * P], hn2[t % 2][:, kk * P:(kk + 1) * P], ident[:])
                        m.then_inc(*PE_.tick(f"H{t}{q}"))
                    b = bank(f"R{t}")
                    pe.wait_ge(*A_.at(f"e:H{t}0", g))
                    pe.wait_ge(*V_.at(f"e:H{t}1", g))
                    for k in range(KT):
                        m = nc.tensor.matmul(b[:, 0:NR], hn2T[:, k], wrt[:, k], start=(k == 0), stop=(k == KT - 1))
                    m.then_inc(*PE_.tick(f"R{t}"))

                for i in range(4):
                    channels(i)
                b = bank("AL")
                for k in range(KT):
                    m = nc.tensor.matmul(b[0:RANK, :], wal[:, k], hnT[:, k], start=(k == 0), stop=(k == KT - 1))
                m.then_inc(*PE_.tick("AL"))
                for t in range(TT):
                    tokens("V", t)
                for c in range(HP):
                    b = bank(f"L{c}")
                    pe.wait_ge(*A_.at("e:AL", g))
                    nc.tensor.matmul(b[:], wup[:, c * P:(c + 1) * P], alow, start=True, stop=True).then_inc(*PE_.tick(f"L{c}"))
                gates(0)
                for i in range(4, 8):
                    channels(i)
                gates(1)
                channels(8)
                channels(9)
                decayed_keys(0)
                decayed_keys(1)
                gates(2)
                scores(0)
                outer(0)
                scores(1)
                channels(10)
                attend(0)
                channels(11)
                outer(1)
                scores(2)
                gates(3)
                tokens("G", 0)
                attend(1)
                tokens("G", 1)
                turn_o(0)
                outer(2)
                scores(3)
                tokens("G", 2)
                attend(2)
                b = bank("SS")
                for c in range(CT):
                    pe.wait_ge(*A_.at(f"ysq{c}", g))
                    m = nc.tensor.matmul(b[:], ones[:], xc[:, c], start=(c == 0), stop=(c == CT - 1))
                m.then_inc(*PE_.tick("SS"))
                turn_o(1)
                tokens("G", 3)
                outer(3)
                turn_o(2)
                attend(3)
                pe.wait_ge(wout_scaled, KT)
                for t in range(TT + 1):
                    if t < TT:
                        out(t)
                    if t:
                        router(t - 1)
                    else:
                        turn_o(3)
                tables["P"] = PE_.table()


def route(nc, slot_dram, ident, ones, logits, dest, rows, wts, btab, place_slots, sem):
    with ExitStack() as ctx:
        def sb(name, shape, dt=F32):
            return ctx.enter_context(nc.sbuf_tensor(name, shape, dt))

        earlier = sb("earlier", [P, P])
        gdesc = sb("gdesc", [P, NG])
        edesc = sb("edesc", [P, EPG])
        blk = sb("blk", [P, BLOCKS + 1])
        no_rows = sb("no_rows", [P, SLOTS // P, 2], I32)
        gval = sb("gval", [P, TILES, NG])
        goh = sb("goh", [P, TILES, NG])
        gm = sb("gm", [P, TILES])
        gx = sb("gx", [P, TILES, NG])
        gw = sb("gw", [P, TILES])
        le4 = sb("le4", [P, TILES, NG, EPG])
        le = sb("le", [P, TILES, EPG])
        eval_ = sb("eval", [P, TILES, EPG])
        oh = sb("oh", [P, 2, TILES, EPG])
        m12 = sb("m12", [P, 2, TILES])
        mx = sb("mx", [P, TILES])
        big_oh = sb("big_oh", [P, 2, TILES, NG, EPG])
        both = sb("both", [P, TILES, NE])
        carry = sb("carry", [P, TILES + 1, NE])
        rank = sb("rank", [P, TILES, NE])
        padded = sb("padded", [P, NE])
        padded_i = sb("padded_i", [P, NE], I32)
        pend = sb("pend", [P, NE])
        pstart = sb("pstart", [P, NE])
        prod = sb("prod", [P, TILES, NE])
        destf = sb("destf", [P, TILES, 2])
        cmp = sb("cmp", [P, BLOCKS + 1, NE])
        eno = sb("eno", [P, NE])
        some = sb("some", [P, NE])
        nth = sb("nth", [P, NE])
        pmark = sb("pmark", [P, NE])
        is_nth = sb("is_nth", [P, NE, NE])
        pick = sb("pick", [P, 2, NE, NE])
        picked = sb("picked", [P, 2, NE])
        btf = sb("btf", [P, TABLE])
        rk = ctx.enter_context(nc.psum_tensor("rk", [P, TILES * NE], F32))
        tot = ctx.enter_context(nc.psum_tensor("tot", [P, TILES * NE], F32))

        tables_made = sem("r_tables_made")
        ohs_ready = sem("r_ohs_ready")
        counted = sem("r_counted")
        dve_steps = sem("r_dve_steps")
        exps = sem("r_exps")
        exp_in = sem("r_exp_in")
        dest_ready = sem("r_dest_ready")
        slots_zeroed = sem("r_slots_zeroed")

        block = ctx.enter_context(nc.Block())

        @block.gpsimd
        def _(pool):
            nc.gpsimd.memset(earlier[:], 1.0).then_inc(tables_made, 1)
            nc.gpsimd.iota(no_rows[:, :, 0], [[0, SLOTS // P]], base=0, channel_multiplier=0).then_inc(tables_made, 1)
            nc.gpsimd.iota(no_rows[:, :, 1], [[1, SLOTS // P]], base=2 * SEQ, channel_multiplier=SLOTS // P).then_inc(tables_made, 1)
            nc.gpsimd.iota(gdesc[:], [[-1, NG]], base=NG, channel_multiplier=0,
                           allow_small_or_imprecise_dtypes=True).then_inc(tables_made, 1)
            nc.gpsimd.iota(edesc[:], [[-1, EPG]], base=EPG, channel_multiplier=0,
                           allow_small_or_imprecise_dtypes=True).then_inc(tables_made, 1)
            nc.gpsimd.iota(blk[:], [[1, BLOCKS + 1]], base=0, channel_multiplier=0,
                           allow_small_or_imprecise_dtypes=True).then_inc(tables_made, 1)
            nc.gpsimd.iota(rows[:, :, :, 0], [[P, TILES], [0, 2]], base=0, channel_multiplier=1).then_inc(tables_made, 1)
            nc.gpsimd.iota(rows[:, :, :, 1], [[2 * P, TILES], [1, 2]], base=0, channel_multiplier=2).then_inc(tables_made, 1)
            nc.gpsimd.iota(eno[:], [[1, NE]], base=0, channel_multiplier=0,
                           allow_small_or_imprecise_dtypes=True).then_inc(tables_made, 1)
            pool.wait_ge(tables_made, 9)
            nc.gpsimd.affine_select(out=earlier[:], in_=earlier[:], compare_op=ALU.is_gt, fill=0.0, base=0,
                                    pattern=[[1, P]], channel_multiplier=-1).then_inc(tables_made, 1)
            pool.wait_ge(dest_ready, 1)
            pool.wait_ge(slots_zeroed, 16)
            place_slots(0, PLACED_EARLY)

        @block.sync
        def _(sync):
            sync.wait_ge(tables_made, 9)
            sync.dma_start(slot_dram.rearrange("(p a) o -> p (a o)", p=P), no_rows[:].rearrange("p a o -> p (a o)")).then_inc(slots_zeroed, 16)
            sync.wait_ge(slots_zeroed, 16)

        @block.scalar
        def _(act):
            act.wait_ge(exp_in, 1)
            nc.scalar.activation(gx[:], gx[:], ACT.Exp).then_inc(exps, 1)
            act.wait_ge(exp_in, 2)
            nc.scalar.activation(mx[:], mx[:], ACT.Exp).then_inc(exps, 1)

        @block.vector
        def _(dve):
            n = [0]

            def step(ins, signal=None):
                if signal is not None:
                    ins.then_inc(signal, 1)
                else:
                    n[0] += 1
                    ins.then_inc(dve_steps, 1)
                    dve.wait_ge(dve_steps, n[0])

            def bc(ap, shape):
                return ap.to_broadcast(shape)

            v = nc.vector
            dve.wait_ge(tables_made, 10)
            gl = logits[:, :, 0:NG]
            g4 = [P, TILES, NG]
            e8 = [P, TILES, EPG]
            step(v.tensor_reduce(gm[:], gl, AX, ALU.max))
            step(v.tensor_tensor(gx[:], gl, bc(gm[:].unsqueeze(2), g4), ALU.subtract))
            step(v.tensor_scalar(gval[:], gx[:], 0.0, None, ALU.is_equal))
            step(v.tensor_tensor(gval[:], gval[:], bc(gdesc[:].unsqueeze(1), g4), ALU.mult))
            v.tensor_reduce(gw[:], gval[:], AX, ALU.max).then_inc(exp_in, 1)
            dve.wait_ge(exp_in, 1)
            step(v.tensor_tensor(goh[:], gval[:], bc(gw[:].unsqueeze(2), g4), ALU.is_equal))
            dve.wait_ge(exps, 1)
            step(v.tensor_reduce(gw[:], gx[:], AX, ALU.add))
            step(v.reciprocal(gw[:], gw[:]))
            lg = logits[:, :, NG:NR].rearrange("p t (g e) -> p t g e", g=NG)
            for g in range(NG):
                step(v.tensor_tensor(le4[:, :, g], lg[:, :, g], bc(goh[:, :, g:g + 1], e8), ALU.mult))
            step(v.tensor_reduce(le[:], le4[:].rearrange("p t g e -> p t e g"), AX, ALU.add))
            for k in range(2):
                step(v.tensor_reduce(m12[:, k], le[:], AX, ALU.max))
                step(v.tensor_tensor(eval_[:], le[:], bc(m12[:, k].unsqueeze(2), e8), ALU.is_equal))
                step(v.tensor_tensor(eval_[:], eval_[:], bc(edesc[:].unsqueeze(1), e8), ALU.mult))
                step(v.tensor_reduce(mx[:], eval_[:], AX, ALU.max))
                step(v.tensor_tensor(oh[:, k], eval_[:], bc(mx[:].unsqueeze(2), e8), ALU.is_equal))
                if k == 0:
                    step(v.scalar_tensor_tensor(le[:], oh[:, 0], -3.0e38, le[:], ALU.mult, ALU.add))
            v.tensor_tensor(mx[:], m12[:, 1], m12[:, 0], ALU.subtract).then_inc(exp_in, 1)
            dve.wait_ge(exps, 2)
            step(v.tensor_scalar(m12[:, 0], mx[:], 1.0, None, ALU.add))
            step(v.reciprocal(m12[:, 0], m12[:, 0]))
            step(v.tensor_tensor(wts[:, :, 0], m12[:, 0], gw[:], ALU.mult))
            step(v.tensor_tensor(wts[:, :, 1], wts[:, :, 0], mx[:], ALU.mult))
            for k in range(2):
                for g in range(NG):
                    step(v.tensor_tensor(big_oh[:, k, :, g], oh[:, k], bc(goh[:, :, g:g + 1], e8), ALU.mult))
            b0 = big_oh[:, 0].rearrange("p t g e -> p t (g e)")
            b1 = big_oh[:, 1].rearrange("p t g e -> p t (g e)")
            v.tensor_tensor(both[:], b0, b1, ALU.add).then_inc(ohs_ready, 1)
            step(v.memset(carry[:, 0], 0.0))
            dve.wait_ge(counted, 2)
            tt = tot[:].rearrange("p (t e) -> p t e", e=NE)
            for t in range(TILES):
                step(v.tensor_tensor(carry[:, t + 1], tt[:, t], carry[:, t], ALU.add))
            step(v.tensor_tensor(rank[:], rk[:].rearrange("p (t e) -> p t e", e=NE), carry[:, 0:TILES], ALU.add))
            step(v.tensor_scalar(padded_i[:], carry[:, TILES], float(P - 1), None, ALU.add))
            step(v.tensor_scalar(padded_i[:], padded_i[:], 7, None, ALU.logical_shift_right))
            step(v.tensor_copy(padded[:], padded_i[:]))
            step(v.tensor_tensor_scan(pend[:], ones[:, 0:NE], padded[:], 0.0, ALU.mult, ALU.add))
            step(v.tensor_tensor(pstart[:], pend[:], padded[:], ALU.subtract))
            step(v.tensor_scalar(pstart[:], pstart[:], float(P), None, ALU.mult))
            step(v.tensor_tensor(rank[:], rank[:], bc(pstart[:].unsqueeze(1), [P, TILES, NE]), ALU.add))
            for k, b in enumerate((b0, b1)):
                step(v.tensor_tensor(prod[:], rank[:], b, ALU.mult))
                step(v.tensor_reduce(destf[:, :, k], prod[:], AX, ALU.add))
            v.tensor_copy(dest, destf[:]).then_inc(dest_ready, 1)
            step(v.tensor_scalar(some[:], padded[:], 1.0, None, ALU.min))
            step(v.tensor_tensor_scan(nth[:], ones[:, 0:NE], some[:], 0.0, ALU.mult, ALU.add))
            step(v.tensor_copy(btf[:, N_EXP:N_EXP + 1], nth[:, NE - 1:NE]))
            step(v.tensor_copy(btf[:, N_BLOCKS:N_BLOCKS + 1], pend[:, NE - 1:NE]))
            step(v.tensor_scalar(btf[:, LAST_TURN:LAST_TURN + 1], nth[:, NE - 1:NE], -1.0, None, ALU.add))
            step(v.tensor_scalar(pmark[:], some[:], -2.0 * BLOCKS, 2.0 * BLOCKS, ALU.mult, ALU.add))
            step(v.tensor_tensor(pmark[:], pmark[:], pend[:], ALU.add))
            step(v.tensor_tensor(cmp[:], bc(pmark[:].unsqueeze(1), [P, BLOCKS + 1, NE]),
                                 bc(blk[:].unsqueeze(2), [P, BLOCKS + 1, NE]), ALU.is_le))
            step(v.tensor_reduce(btf[:, TURN:TURN + BLOCKS + 1], cmp[:], AX, ALU.add))
            step(v.tensor_scalar(btf[:, TURN:TURN + BLOCKS + 1], btf[:, TURN:TURN + BLOCKS + 1], btf[:, LAST_TURN:LAST_TURN + 1], None, ALU.min))
            step(v.tensor_tensor(nth[:], nth[:], some[:], ALU.mult))
            step(v.tensor_tensor(is_nth[:], bc(nth[:].unsqueeze(1), [P, NE, NE]),
                                 bc(blk[:, 1:NE + 1].unsqueeze(2), [P, NE, NE]), ALU.is_equal))
            for i, of in enumerate((eno, pend)):
                step(v.tensor_tensor(pick[:, i], is_nth[:], bc(of[:].unsqueeze(1), [P, NE, NE]), ALU.mult))
            step(v.tensor_reduce(picked[:], pick[:], AX, ALU.add))
            step(v.tensor_copy(btf[:, EXPERT:EXPERT + NE], picked[:, 0]))
            step(v.memset(btf[:, EXPERT + NE:EXPERT + NE + 1], 0.0))
            step(v.tensor_scalar(btf[:, SPLIT:SPLIT + NE], picked[:, 1], float(UNITS), -float(UNITS), ALU.mult, ALU.add))
            step(v.tensor_copy(btab, btf[:]))

        @block.tensor
        def _(pe):
            pe.wait_ge(tables_made, 10)
            pe.wait_ge(ohs_ready, 1)
            b = both[:].rearrange("p t e -> p (t e)")
            nc.tensor.matmul(rk[:], earlier[:], b, start=True, stop=True).then_inc(counted, 1)
            nc.tensor.matmul(tot[:], ones[:], b, start=True, stop=True).then_inc(counted, 1)


def experts(nc, T, slot_dram, hn_dram, y_dram, ident, btab, place_slots, slots_written, sem):
    KU = 4
    RING = 7
    AHEAD = 2 * RING - UNITS
    STAGE = 4
    UW = KU * 512
    with ExitStack() as ctx:
        def sb(name, shape, dt=F32):
            return ctx.enter_context(nc.sbuf_tensor(name, shape, dt))

        def ps(name, shape):
            return ctx.enter_context(nc.psum_tensor(name, shape, F32))

        raw = sb("raw", [P, RING, 2, UW])
        whi = sb("whi", [P, STAGE, UW], F32R)
        wlo = sb("wlo", [P, STAGE, UW], F32R)
        xg = sb("xg", [P, D])
        idx = sb("idx", [P, 2], I32)
        place = sb("place", [P, 1], I32)
        place_next = sb("place_next", [P, 1], I32)
        xhi = sb("xhi", [P, KT, P], F32R)
        xlo = sb("xlo", [P, KT, P], F32R)
        hb = sb("hb", [P, D])
        hhi = sb("hhi", [P, KT, P], F32R)
        hlo = sb("hlo", [P, KT, P], F32R)
        ysb = sb("ysb", [P, D])
        gate = [ps(f"gate{n}", [P, 512]) for n in range(2)]
        up = [ps(f"up{n}", [P, 512]) for n in range(2)]
        yp = [ps(f"yp{n}", [P, 512]) for n in range(2)]
        tp = [ps(f"tp{n}", [P, 512]) for n in range(2)]

        w_in = [sem(f"e_w_in{u}") for u in range(UNITS)]
        hi_made = sem("e_hi_made")
        lo_made = sem("e_lo_made")
        stage_free = sem("e_stage_free")
        idx_in = sem("e_idx_in")
        place_kept = sem("e_place_kept")
        next_kept = sem("e_next_kept")
        rows_in = sem("e_rows_in")
        x_turned = sem("e_x_turned")
        x_hi = sem("e_x_hi")
        x_lo = sem("e_x_lo")
        gelu_done = sem("e_gelu_done")
        h_done = sem("e_h_done")
        h_turned = sem("e_h_turned")
        h_hi = sem("e_h_hi")
        h_lo = sem("e_h_lo")
        y_out_a = sem("e_y_copied_act")
        y_out_v = sem("e_y_copied_dve")
        y_stored = sem("e_y_stored")
        passed_g = sem("e_passed_g")
        passed_s = sem("e_passed_s")

        def unit(u):
            if u < 8:
                n, r = divmod(u, 4)
                return ("gate", "up")[r % 2], n, r // 2
            return "down", None, u - 8

        def unit_rows(u, e):
            kind, n, q = unit(u)
            if kind == "down":
                w = T["w_exp_down"][0].rearrange("e (k p) n -> e p k n", p=P)
                return w[bass.ds(e, 1), :, 2 * q:2 * q + 2, :].rearrange("e p k n -> p (e k) n")
            w = T["w_exp_" + kind][0].rearrange("e (k p) n -> e p k n", p=P)
            return w[bass.ds(e, 1), :, KU * q:KU * q + KU, n * 512:(n + 1) * 512].rearrange("e p k n -> p (e k) n")

        def count_of_blocks(eng):
            return eng.value_load(btab[0:1, N_BLOCKS:N_BLOCKS + 1], min_val=1, max_val=BLOCKS)

        def turn_of(eng, b):
            at = slice(TURN + b, TURN + b + 1) if isinstance(b, int) else bass.ds(b + TURN, 1)
            return eng.value_load(btab[0:1, at], min_val=0, max_val=NE - 1)

        def raw_unit(u, turn):
            q = (turn * (UNITS // 2) + u // 2) % RING
            if isinstance(turn, int):
                return raw[:, q, u % 2]
            return raw[:, bass.ds(q, 1), u % 2, :].rearrange("p a f -> p (a f)")

        block = ctx.enter_context(nc.Block())

        @block.sync
        def _(sync):
            n_exp = sync.value_load(btab[0:1, N_EXP:N_EXP + 1], min_val=1, max_val=NE)

            def load(u, e, turn):
                k = 2 if unit(u)[0] == "down" else KU
                sync.dma_start(raw_unit(u, turn).rearrange("p (k n) -> p k n", k=k), unit_rows(u, e)).then_inc(w_in[u], 16)

            first = sync.value_load(btab[0:1, EXPERT:EXPERT + 1], min_val=0, max_val=NE - 1)
            for u in range(UNITS):
                if u >= 2:
                    sync.wait_ge(w_in[u - 2], 16)
                load(u, first, 0)
            second = sync.value_load(btab[0:1, EXPERT + 1:EXPERT + 2], min_val=0, max_val=NE - 1)
            for u in range(AHEAD):
                sync.wait_ge(w_in[u], 16)
                load(u, second, 1)
            with sync.Fori(1, n_exp) as j:
                e = sync.value_load(btab[0:1, bass.ds(j + EXPERT, 1)], min_val=0, max_val=NE - 1)
                after = sync.value_load(btab[0:1, bass.ds(j + (EXPERT + 1), 1)], min_val=0, max_val=NE - 1)
                split_before = sync.value_load(btab[0:1, bass.ds(j + (SPLIT - 1), 1)], min_val=0, max_val=UNITS * BLOCKS)
                for u in range(AHEAD, UNITS + AHEAD):
                    sync.wait_ge(lo_made, split_before + (u - AHEAD + 1))
                    sync.sem_inc(passed_s, 1)
                    sync.wait_ge(w_in[u % UNITS], 16 * j + 16 * (u // UNITS))
                    sync.sem_inc(passed_s, 1)
                    load(u % UNITS, after if u >= UNITS else e, j + u // UNITS)
            for u in range(UNITS):
                sync.wait_ge(w_in[u], 16 * n_exp + (16 if u < AHEAD else 0))
                sync.sem_inc(passed_s, 1)

        @block.gpsimd
        def _(pool):
            n_blocks = count_of_blocks(pool)

            def load_idx(b):
                nc.gpsimd.dma_start(idx[:], slot_dram[bass.ds(b * P, P), :]).then_inc(idx_in, 16)

            def gather(b):
                pool.wait_ge(idx_in, 16 * (b + 1))
                if not isinstance(b, int) or b:
                    pool.wait_ge(x_turned, 2 * b)
                pool.sem_inc(passed_g, 1)
                nc.gpsimd.indirect_dma_start(xg[:], None, hn_dram, bass.IndirectOffsetOnAxis(idx[:, 0:1], 0)).then_inc(rows_in, 16)

            def keep_next(b):
                pool.wait_ge(rows_in, 16 * (b + 1))
                if not isinstance(b, int) or b:
                    pool.wait_ge(place_kept, b)
                pool.sem_inc(passed_g, 1)
                nc.gpsimd.tensor_copy(place_next[:], idx[:, 1:2]).then_inc(next_kept, 1)
                pool.wait_ge(next_kept, b + 1)

            def keep_place(b):
                pool.sem_inc(passed_g, 1)
                nc.gpsimd.tensor_copy(place[:], place_next[:]).then_inc(place_kept, 1)
                pool.wait_ge(place_kept, b + 1)

            def scatter(b):
                pool.wait_ge(y_out_a, b + 1)
                pool.wait_ge(y_out_v, b + 1)
                pool.sem_inc(passed_g, 1)
                nc.gpsimd.indirect_dma_start(y_dram, bass.IndirectOffsetOnAxis(place[:, 0:1], 0), ysb[:], None).then_inc(y_stored, 16)
                pool.wait_ge(y_stored, 16 * (b + 1))

            place_slots(PLACED_EARLY, 2 * TILES)
            pool.wait_ge(slots_written, 16 * 2 * TILES)
            load_idx(0)
            gather(0)
            keep_next(0)
            keep_place(0)
            load_idx(1)
            gather(1)
            keep_next(1)
            load_idx(2)
            with pool.Fori(1, n_blocks) as b:
                gather(b + 1)
                scatter(b - 1)
                keep_place(b)
                keep_next(b + 1)
                load_idx(b + 2)
            scatter(n_blocks - 1)
            pool.wait_ge(idx_in, 16 * (n_blocks + 2))
            pool.sem_inc(passed_g, 1)

        @block.scalar
        def _(act):
            n_blocks = count_of_blocks(act)

            def split(u, b, turn):
                act.wait_ge(w_in[u], 16 * turn + 16)
                act.wait_ge(stage_free, UNITS * b + u + 1)
                nc.scalar.activation(whi[:, u % STAGE], raw_unit(u, turn), ACT.Copy).then_inc(hi_made, 1)

            def x_part(q, b):
                act.wait_ge(x_turned, 2 * b + q + 1)
                nc.scalar.activation(xhi[:, 4 * q:4 * q + 4], tp[q][:].rearrange("p (k t) -> p k t", k=4), ACT.Copy).then_inc(x_hi, 1)

            def gelu(n, b):
                act.wait_ge(stage_free, STAGE + UNITS * b + 4 * (n + 1))
                act.wait_ge(h_turned, 2 * b + 2)
                nc.scalar.activation(hb[:, n * 512:(n + 1) * 512], gate[n][:], ACT.Gelu_apprx_tanh).then_inc(gelu_done, 1)

            def h_part(n, b):
                act.wait_ge(h_turned, 2 + 2 * b + n + 1)
                nc.scalar.activation(hhi[:, 4 * n:4 * n + 4], tp[n][:].rearrange("p (k t) -> p k t", k=4), ACT.Copy).then_inc(h_hi, 1)

            def y_half(b):
                act.wait_ge(stage_free, STAGE + UNITS * (b + 1))
                if not isinstance(b, int) or b:
                    act.wait_ge(place_kept, b + 1)
                nc.scalar.activation(ysb[:, 0:512], yp[0][:], ACT.Copy).then_inc(y_out_a, 1)

            def body(b, with_y):
                turn = turn_of(act, b)
                split(2, b, turn)
                split(3, b, turn)
                if with_y:
                    y_half(b - 1)
                for u in range(4, 8):
                    split(u, b, turn)
                gelu(0, b)
                split(8, b, turn)
                split(9, b, turn)
                h_part(0, b)
                split(10, b, turn)
                gelu(1, b)
                split(11, b, turn)
                h_part(1, b)
                turn = turn_of(act, b + 1)
                split(0, b + 1, turn)
                x_part(0, b + 1)
                split(1, b + 1, turn)
                x_part(1, b + 1)

            nc.scalar.preload_act_table(ACT.Gelu_apprx_tanh)
            turn = turn_of(act, 0)
            split(0, 0, turn)
            split(1, 0, turn)
            x_part(0, 0)
            x_part(1, 0)
            body(0, False)
            with act.Fori(1, n_blocks) as b:
                body(b, True)
            y_half(n_blocks - 1)

        @block.vector
        def _(dve):
            n_blocks = count_of_blocks(dve)

            def split(u, b, turn):
                dve.wait_ge(hi_made, UNITS * b + u + 1)
                nc.vector.tensor_tensor(wlo[:, u % STAGE], raw_unit(u, turn), whi[:, u % STAGE].bitcast(F32), ALU.subtract).then_inc(lo_made, 1)

            def x_part(q, b):
                dve.wait_ge(x_hi, 2 * b + q + 1)
                nc.vector.tensor_tensor(xlo[:, 4 * q:4 * q + 4], tp[q][:].rearrange("p (k t) -> p k t", k=4),
                                        xhi[:, 4 * q:4 * q + 4].bitcast(F32), ALU.subtract).then_inc(x_lo, 1)

            def h_half(n, b):
                dve.wait_ge(gelu_done, 2 * b + n + 1)
                hs = hb[:, n * 512:(n + 1) * 512]
                nc.vector.tensor_tensor(hs, up[n][:], hs, ALU.mult).then_inc(h_done, 1)

            def h_part(n, b):
                dve.wait_ge(h_hi, 2 * b + n + 1)
                nc.vector.tensor_tensor(hlo[:, 4 * n:4 * n + 4], tp[n][:].rearrange("p (k t) -> p k t", k=4),
                                        hhi[:, 4 * n:4 * n + 4].bitcast(F32), ALU.subtract).then_inc(h_lo, 1)

            def y_half(b):
                dve.wait_ge(stage_free, STAGE + UNITS * (b + 1))
                if not isinstance(b, int) or b:
                    dve.wait_ge(place_kept, b + 1)
                nc.vector.tensor_copy(ysb[:, 512:D], yp[1][:]).then_inc(y_out_v, 1)

            def body(b, with_y):
                turn = turn_of(dve, b)
                split(2, b, turn)
                split(3, b, turn)
                if with_y:
                    y_half(b - 1)
                for u in range(4, 8):
                    split(u, b, turn)
                h_half(0, b)
                split(8, b, turn)
                split(9, b, turn)
                h_part(0, b)
                split(10, b, turn)
                h_half(1, b)
                split(11, b, turn)
                h_part(1, b)
                turn = turn_of(dve, b + 1)
                split(0, b + 1, turn)
                x_part(0, b + 1)
                split(1, b + 1, turn)
                x_part(1, b + 1)

            turn = turn_of(dve, 0)
            split(0, 0, turn)
            split(1, 0, turn)
            x_part(0, 0)
            x_part(1, 0)
            body(0, False)
            with dve.Fori(1, n_blocks) as b:
                body(b, True)
            y_half(n_blocks - 1)

        @block.tensor
        def _(pe):
            n_blocks = count_of_blocks(pe)

            def turn_x(q, b):
                pe.wait_ge(rows_in, 16 * (b + 1))
                if not isinstance(b, int):
                    pe.wait_ge(h_lo, 2 * (b - 1) + q + 1)
                for k in range(4):
                    kk = 4 * q + k
                    m = nc.tensor.transpose(tp[q][:, k * P:(k + 1) * P], xg[:, kk * P:(kk + 1) * P], ident[:])
                m.then_inc(x_turned, 1)

            def turn_h(n, b):
                pe.wait_ge(h_done, 2 * b + n + 1)
                for k in range(4):
                    m = nc.tensor.transpose(tp[n][:, k * P:(k + 1) * P], hb[:, (4 * n + k) * P:(4 * n + k + 1) * P], ident[:])
                m.then_inc(h_turned, 1)

            def three(out, ahi, alo, u, col, first, last):
                s = slice(col * 512, (col + 1) * 512)
                nc.tensor.matmul(out, ahi, whi[:, u % STAGE, s], start=first, stop=False)
                nc.tensor.matmul(out, ahi, wlo[:, u % STAGE, s], start=False, stop=False)
                return nc.tensor.matmul(out, alo, whi[:, u % STAGE, s], start=False, stop=last)

            def run_unit(u, b):
                kind, n, q = unit(u)
                pe.wait_ge(lo_made, UNITS * b + u + 1)
                if kind == "down":
                    if u == 8:
                        pe.wait_ge(place_kept, b + 1)
                    for k in range(2):
                        kk = 2 * q + k
                        for nn in range(2):
                            m = three(yp[nn][:], hhi[:, kk], hlo[:, kk], u, 2 * k + nn, kk == 0, kk == KT - 1)
                else:
                    out = (gate if kind == "gate" else up)[n]
                    for k in range(KU):
                        kk = KU * q + k
                        m = three(out[:], xhi[:, kk], xlo[:, kk], u, k, kk == 0, kk == KT - 1)
                return m

            pe.sem_inc(stage_free, STAGE)
            pe.sem_inc(h_turned, 2)
            turn_x(0, 0)
            turn_x(1, 0)
            with pe.Fori(0, n_blocks) as b:
                pe.wait_ge(x_lo, 2 * b + 2)
                for u in range(UNITS):
                    if u == 8:
                        pe.wait_ge(h_lo, 2 * b + 1)
                    if u == 10:
                        pe.wait_ge(h_lo, 2 * b + 2)
                    run_unit(u, b).then_inc(stage_free, 1)
                    if u == 5:
                        turn_h(0, b)
                    if u == 8:
                        turn_h(1, b)
                    if u == 9:
                        turn_x(0, b + 1)
                    if u == 10:
                        turn_x(1, b + 1)


def combine(nc, T, h_dram, y_dram, out_rows, wts, sem):
    BUF = 4
    with ExitStack() as ctx:
        def sb(name, shape, dt=F32):
            return ctx.enter_context(nc.sbuf_tensor(name, shape, dt))

        h = sb("c_h", [P, BUF, D])
        y = sb("c_y", [P, BUF, 2, D])
        o = sb("c_o", [P, BUF, D])
        nf = sb("c_nf", [P, D])
        stt = sb("c_st", [P, 4 * TILES])
        nf_in = sem("c_nf_in")
        h_in = [sem(f"c_h_in{i}") for i in range(BUF)]
        y_in = [sem(f"c_y_in{i}") for i in range(BUF)]
        out_st = [sem(f"c_out{i}") for i in range(BUF)]
        dve_steps = sem("c_dve_steps")
        sq_done = sem("c_sq_done")
        rt_done = sem("c_rt_done")
        PER = 5

        block = ctx.enter_context(nc.Block())

        @block.sync
        def _(sync):
            sync.dma_start(nf[:], T["norm_final"].rearrange("(a d) -> a d", a=1).partition_broadcast(P)).then_inc(nf_in, 16)
            for t in range(TILES):
                if t >= BUF:
                    sync.wait_ge(dve_steps, PER * (t - BUF + 1))
                sync.dma_start(h[:, t % BUF], h_dram[t * P:(t + 1) * P, :]).then_inc(h_in[t % BUF], 16)
                sync.dma_start(y[:, t % BUF], y_dram[2 * t * P:2 * (t + 1) * P, :].rearrange("(p k) d -> p k d", k=2)).then_inc(y_in[t % BUF], 16)

        @block.scalar
        def _(act):
            for t in range(TILES):
                i = t % BUF
                act.wait_ge(dve_steps, PER * t + 2)
                nc.scalar.activation(y[:, i, 0], h[:, i], ACT.Square, accum_out=stt[:, t:t + 1]).then_inc(sq_done, 1)
                act.wait_ge(dve_steps, PER * t + 3)
                nc.scalar.activation(stt[:, 2 * TILES + t:2 * TILES + t + 1], stt[:, TILES + t:TILES + t + 1], ACT.Sqrt).then_inc(rt_done, 1)
                act.wait_ge(dve_steps, PER * t + PER)
                act.dma_start(out_rows[t * P:(t + 1) * P, :], o[:, i]).then_inc(out_st[i], 16)
            for i in range(BUF):
                act.wait_ge(out_st[i], 16 * (TILES // BUF))

        @block.vector
        def _(dve):
            dve.wait_ge(nf_in, 16)
            n = 0

            def step(ins):
                nonlocal n
                n += 1
                ins.then_inc(dve_steps, 1)
                dve.wait_ge(dve_steps, n)

            for t in range(TILES):
                i = t % BUF
                c = lambda q: stt[:, q * TILES + t:q * TILES + t + 1]
                dve.wait_ge(h_in[i], 16 * (t // BUF + 1))
                dve.wait_ge(y_in[i], 16 * (t // BUF + 1))
                for k in range(2):
                    step(nc.vector.scalar_tensor_tensor(h[:, i], y[:, i, k], wts[:, t, k:k + 1], h[:, i], ALU.mult, ALU.add))
                dve.wait_ge(sq_done, t + 1)
                step(nc.vector.tensor_scalar(c(1), c(0), 1.0 / D, EPS, ALU.mult, ALU.add))
                dve.wait_ge(rt_done, t + 1)
                step(nc.vector.reciprocal(c(3), c(2)))
                if t >= BUF:
                    dve.wait_ge(out_st[i], 16 * (t // BUF))
                step(nc.vector.scalar_tensor_tensor(o[:, i], h[:, i], c(3), nf[:], ALU.mult, ALU.mult))


_INS = ["x", "norm_mix", "w_in", "conv_w", "conv_b", "w_rg_a", "b_rg_a", "w_rg_x", "b_rg_x", "rg_lambda",
        "rg_norm", "w_alpha_up", "b_alpha", "gla_norm", "w_out", "norm_ffn", "w_router_group",
        "b_router_group", "w_router_expert", "b_router_expert", "w_exp_gate", "w_exp_up", "w_exp_down",
        "norm_final"]


def kernel(**inputs):
    import numpy as np
    import concourse.bacc as bacc
    from concourse.bass_utils import run_bass_kernel_spmd

    arrays = {n: np.ascontiguousarray(inputs[n]) for n in _INS}
    known = {}
    for _ in range(2):
        nc = bacc.Bacc("TRN2", target_bir_lowering=False, num_devices=1)
        T = {n: nc.dram_tensor(f"in_{n}", a.shape, mybir.dt.from_np(a.dtype), kind="ExternalInput").ap()
             for n, a in arrays.items()}
        T["out"] = nc.dram_tensor("out_0", (1, SEQ, D), F32, kind="ExternalOutput").ap()
        known = build(nc, T, known)
    r = run_bass_kernel_spmd(nc, [{f"in_{n}": a for n, a in arrays.items()}], core_ids=[0])
    return r.results[0]["out_0"]
```

```python
from contextlib import ExitStack

import concourse.bass as bass
from concourse import mybir

F32 = mybir.dt.float32
F32R = mybir.dt.float32r
I32 = mybir.dt.int32
U32 = mybir.dt.uint32
ALU = mybir.AluOpType
ACT = mybir.ActivationFunctionType
AX = mybir.AxisListType.X

P = 128
D = 1024
SEQ = 2048
KT = D // P
RG = 512
CT = RG // P
CONV = 4
HEADS = 4
DK = 64
DV = 128
HP = HEADS * DK // P
RANK = 16
CHUNK = 64
GT = 512
GROUPS = SEQ // GT
TT = GT // P
TILES = SEQ // P
NCH = GT // CHUNK
NG = 4
EPG = 8
NE = NG * EPG
NR = NG + NE
EPS = 1e-6
BLOCKS = (SEQ * 2 + NE * (P - 1) + P - 1) // P
SLOTS = (BLOCKS + 2) * P
UNITS = 12
N_EXP, N_BLOCKS, LAST_TURN, TURN = range(4)
EXPERT = TURN + BLOCKS + 1
SPLIT = EXPERT + NE + 1
TABLE = SPLIT + NE
PLACED_EARLY = 12
W_BUF = 3
GATE_NORM = 16.0
C_RG = 8.0

COL_X, COL_Y, COL_Q, COL_K, COL_V, COL_G, COL_A = 0, 512, 1024, 1280, 1536, 2048, 2560
IN_W = 2576


class Steps:

    def __init__(self, sem, known):
        self.sem, self.known = sem, known
        self.n, self.base, self.per, self.g = 0, 0, None, None
        self.marks = {}

    def begin_loop(self, g):
        self.base, self.n, self.g = self.n, 0, g
        self.ahead, self.marks = self.marks, {}

    def tick(self, name=None):
        self.n += 1
        if name is not None:
            assert name not in self.marks, name
            self.marks[name] = self.n
        return self.sem, 1

    def now(self):
        if self.g is None:
            return self.sem, self.n
        return self.sem, self.base + self.known.get("per", 1) * self.g + self.n

    def at(self, name, g):
        return self.sem, self.known.get("base", 0) + self.known.get("per", 1) * g + self.known.get(name, 1)

    def before(self, name):
        return self.sem, self.known.get("ahead", {}).get(name, 1)

    def table(self):
        return {**self.marks, "base": self.base, "per": self.n, "ahead": self.ahead}


RESULTS = ([(f"T{k}", "V") for k in range(KT)]
           + [(f"X{c}", "A") for c in range(CT)] + [("AL", "A")]
           + [(f"V{t}", "A") for t in range(TT)] + [("L0", "V"), ("L1", "V")]
           + [("GA0", "A"), ("GX0", "A")] + [(n, "V") for n in ("Q0", "Q1", "K0", "K1")]
           + [("GA1", "A"), ("GX1", "A"), ("Y0", "A"), ("Y1", "A"), ("KE0", "V"), ("KE1", "V")]
           + [("GA2", "A"), ("GX2", "A"), ("Y2", "A"), ("Y3", "A"), ("GA3", "A"), ("GX3", "A")]
           + [(f"G{t}", "V") for t in range(TT)] + [("YT0", "A"), ("YT1", "A")]
           + [r for t in range(TT) for r in
              ([(f"O{t}0", "V")] + ([(f"H{t-1}{q}", "AV"[q]) for q in range(2)] if t else []) + [(f"O{t}1", "V")]
               + ([(f"YT{t+2}", "A")] if t < 2 else []) + ([(f"R{t-1}", "V")] if t else []))]
           + [(f"H{TT-1}{q}", "AV"[q]) for q in range(2)] + [(f"R{TT-1}", "V")])
ORDER = [r for r, _ in RESULTS]
EMPTIED_BY = dict(RESULTS)


def build(nc, T, known):
    tables = {}
    x_rows = T["x"].rearrange("b s d -> (b s) d")
    out_rows = T["out"].rearrange("b s d -> (b s) d")
    w_in = T["w_in"][0].rearrange("(k p) n -> p k n", p=P)
    h_dram = nc.dram_tensor("h_rows", (SEQ + P, D), F32, kind="Internal").ap()
    hn_dram = nc.dram_tensor("hn_rows", (SEQ + P, D), F32, kind="Internal").ap()
    slot_dram = nc.dram_tensor("slot_rows", (SLOTS, 2), I32, kind="Internal").ap()

    with ExitStack() as ctx:
        def keep_sb(name, shape, dt=F32):
            return ctx.enter_context(nc.sbuf_tensor(name, shape, dt))

        def sem(name):
            return ctx.enter_context(nc.semaphore(name))

        ident = keep_sb("ident", [P, P])
        small = keep_sb("small", [P, max(TILES * 6 + TABLE, 2 * DV)], I32)
        rows = small[:, 0:TILES * 4].rearrange("p (t k o) -> p t k o", t=TILES, k=2)
        dest = small[:, TILES * 4:TILES * 6].rearrange("p (t k) -> p t k", t=TILES)
        wts = small[:, 0:TILES * 4].bitcast(F32).rearrange("p (t k o) -> p t k o", t=TILES, k=2)[:, :, :, 1]
        btab = small[:, TILES * 6:TILES * 6 + TABLE]
        squares = small[:, 0:2 * DV].bitcast(F32).rearrange("p (a d) -> p a d", a=2)
        slots_written = sem("slots_written")

        def place_slots(first, last):
            for i in range(first, last):
                t, k = divmod(i, 2)
                nc.gpsimd.indirect_dma_start(slot_dram, bass.IndirectOffsetOnAxis(dest[:, t, k:k + 1], 0),
                                             rows[:, t, k], None).then_inc(slots_written, 16)

        with ExitStack() as inner:
            ones = inner.enter_context(nc.sbuf_tensor("ones", [P, P], F32))
            logits = inner.enter_context(nc.sbuf_tensor("logits", [P, TILES, NR], F32))
            mixer(nc, T, known, tables, x_rows, w_in, h_dram, hn_dram, ident, ones, logits, squares, sem)
            route(nc, slot_dram, ident, ones, logits, dest, rows, wts, btab, place_slots, sem)
        experts(nc, T, slot_dram, hn_dram, h_dram, ident, btab, place_slots, slots_written, sem)
        finish(nc, T, h_dram, out_rows, sem)
    return tables


def mixer(nc, T, known, tables, x_rows, w_in, h_dram, hn_dram, ident, ones, logits, osq, sem):
    with ExitStack() as ctx:
        def sb(name, shape, dt=F32):
            return ctx.enter_context(nc.sbuf_tensor(name, shape, dt))

        def ps(name, shape, dt=F32):
            return ctx.enter_context(nc.psum_tensor(name, shape, dt))

        wout = sb("wout", [P, KT, D])
        wup = sb("wup", [RANK, HP * P])
        wrt = sb("wrt", [P, KT, NR])
        bd = sb("bd", [P, 2, CT, P])
        nmix = sb("nmix", [P, KT])
        nffn = sb("nffn", [P, D])
        cw = sb("cw", [P, CT, CONV])
        cb = sb("cb", [P, CT])
        gb = sb("gb", [P, 2, CT])
        lam = sb("lam", [P, CT])
        sp = sb("sp", [P, 4, CT])
        rgn = sb("rgn", [P, CT])
        glan = sb("glan", [P, 1])
        bal = sb("bal", [P, HP])
        rbias = sb("rbias", [P, NR])
        keepm = sb("keepm", [P, HEADS * P], U32)
        restart = sb("restart", [P, GT])
        with nc.sbuf_tensor("hn_split", [P, 2, KT, GT], F32R) as hn_split:
            hhi, hlo = hn_split[:, 0], hn_split[:, 1]
        plain = sb("hn_plain", [P, 2, KT, GT])
        hnT, late = plain[:, 0], plain[:, 1]
        raw = sb("raw_in", [P, W_BUF, KT * P])
        whi = sb("whi_in", [P, W_BUF, KT * P], F32R)
        wlo = sb("wlo_in", [P, W_BUF, KT * P], F32R)
        xs = sb("xs", [P, TT, D])
        xr = sb("xr", [P, CT, GT + CONV - 1])
        xc = sb("xc", [P, CT, GT])
        yr = sb("yr", [P, CT, GT])
        rg_tmp = sb("rg_tmp", [P, 5, GT])
        rt, it, at_, th, uu = (rg_tmp[:, i] for i in range(5))
        junk = rg_tmp[:, 0:2].rearrange("p a b -> p (a b)")
        hcar = sb("hcar", [P, CT])
        alow = uu[0:RANK]
        qk = sb("qk", [P, 4, GT])
        ks = sb("ks", [P, HP, GT])
        z_all = sb("z_all", [P, 2 * HP, GT])
        z1, z2 = z_all[:, 0:HP], z_all[:, HP:]
        attmask = z1[:, 0]
        bb = sb("bb", [P, HP, GT])
        dc = sb("dc", [P, HP, NCH])
        keT = bb[:].rearrange("p a (b c) -> p (a b) c", c=HP * P)
        vt = sb("vt", [P, TT, RG])
        sg = late[:, 0:TT]
        att = sb("att", [P, 2, HEADS * P])
        st = sb("st", [P, 2, HP, DV])
        ot = xr[:, :, CONV - 1:]
        yT = z_all[:, 0:CT]
        hres = [hnT[:, 6:8, :].rearrange("p a b -> p (a b)"), late[:, 4:6, :].rearrange("p a b -> p (a b)")]
        stat = sb("stat", [P, 64])
        hn2 = [hnT[:, 2 + 2 * i:4 + 2 * i, :].rearrange("p a b -> p (a b)") for i in range(2)]
        hn2T = hnT[:, 0:2, :].rearrange("p a (b t) -> p (a b) t", t=P)
        big = [ps(f"big{i}", [P, 512]) for i in range(4)]
        attp = [ps(f"attp{i}", [P, HEADS * P]) for i in range(2)]
        kvp = ps("kvp", [P, 2, HP, DV])
        op = ps("op", [P, HEADS * DV])

        first_in = sem("m_first_consts_in")
        consts_in = sem("m_consts_in")
        late_in = sem("m_late_consts_in")
        wout_in = sem("m_wout_in")
        consts_made = sem("m_consts_made")
        wring_in = [sem(f"m_wring_in{i}") for i in range(W_BUF)]
        hi_made = sem("m_hi_made")
        lo_made = sem("m_lo_made")
        x_in = [sem(f"m_x_in{t}") for t in range(TT)]
        pad_in = sem("m_pad_in")
        rows_stored = sem("m_rows_stored")
        hres_in = [sem(f"m_hres_in{i}") for i in range(2)]
        h_out = [sem(f"m_h_out{i}") for i in range(2)]
        hn_ready = sem("m_hn_ready")
        hn_stat = sem("m_hn_stat")
        hn_rs = sem("m_hn_rs")
        group_done = sem("m_group_done")
        prep = sem("m_prep")
        passed_p = sem("m_passed_p")
        passed_g = sem("m_passed_g")
        passed_v = sem("m_passed_v")
        S = {k: Steps(sem(f"m_steps_{k}"), known.get(k, {})) for k in "PAV"}
        PE_, A_, V_ = S["P"], S["A"], S["V"]

        block = ctx.enter_context(nc.Block())
        units = ([("c", f"X{c}", COL_X + c * P) for c in range(CT)] + [("a", "AL", COL_A)]
                 + [("t", "V", COL_V, q) for q in range(4)]
                 + [("c", f"Q{c}", COL_Q + c * P) for c in range(HP)] + [("c", f"K{c}", COL_K + c * P) for c in range(HP)]
                 + [("c", f"Y{c}", COL_Y + c * P) for c in range(CT)]
                 + [("t", "G", COL_G, q) for q in range(4)])
        NU = len(units)
        PER_BUF = NU // W_BUF
        assert NU == PER_BUF * W_BUF

        def shaped(buf, i):
            kind = units[i % NU][0]
            if kind == "a":
                return buf[:, i % W_BUF, 0:KT * RANK].rearrange("p (k n) -> p k n", n=RANK)
            return buf[:, i % W_BUF, :].rearrange("p (k n) -> p k n", n=P if kind == "c" else RG)

        def flat(buf, i):
            return buf[:, i % W_BUF, 0:KT * (RANK if units[i % NU][0] == "a" else P)]

        N_CONST = 8 + CONV

        @block.sync
        def _(sync):
            def load(i):
                kind, _, col, *q = units[i % NU]
                if kind == "t":
                    src = w_in[:, 2 * q[0]:2 * q[0] + 2, col:col + RG]
                else:
                    src = w_in[:, :, col:col + (RANK if kind == "a" else P)]
                sync.dma_start(shaped(raw, i), src).then_inc(wring_in[i % W_BUF], 16)

            def const(dst, src):
                sync.dma_start(dst, src, allow_slow_non_contiguous=True).then_inc(consts_in, 16)

            for dst, src in ((lam[:], T["rg_lambda"][0].rearrange("(c p) -> p c", p=P)),
                             (nmix[:], T["norm_mix"][0].rearrange("(k p) -> p k", p=P))):
                sync.dma_start(dst, src, allow_slow_non_contiguous=True).then_inc(first_in, 16)
            for t in range(TT):
                sync.dma_start(xs[:, t], x_rows[t * P:(t + 1) * P, :]).then_inc(x_in[t], 16)
            for i in range(W_BUF):
                load(i)
            const(nffn[:], T["norm_ffn"].partition_broadcast(P))
            const(wup[:], T["w_alpha_up"][0])
            const(cb[:], T["conv_b"][0].rearrange("(c p) -> p c", p=P))
            const(gb[:, 0], T["b_rg_a"][0].rearrange("(c b) i -> (b i) c", b=2))
            const(gb[:, 1], T["b_rg_x"][0].rearrange("(c b) i -> (b i) c", b=2))
            const(rgn[:], T["rg_norm"][0].rearrange("(c p) -> p c", p=P))
            const(glan[:], T["gla_norm"][0].rearrange("(p a) -> p a", a=1))
            const(bal[:], T["b_alpha"][0].rearrange("(c p) -> p c", p=P))
            for j in range(CONV):
                sync.dma_start(cw[:, :, j], T["conv_w"][0, j].rearrange("(c p) -> p c", p=P),
                               allow_slow_non_contiguous=True).then_inc(consts_in, 16)
            sync.sem_inc(rows_stored, 1)
            with sync.Fori(0, GROUPS) as g:
                for i in range(NU):
                    sync.wait_ge(lo_made, NU * g + i + 1)
                    load(i + W_BUF)
                    if i == W_BUF:
                        sync.wait_ge(*PE_.at("T7", g))
                        nx = ((g + 1) % GROUPS) * GT
                        for t in range(TT):
                            sync.dma_start(xs[:, t], x_rows[bass.ds(nx + t * P, P), :]).then_inc(x_in[t], 16)
                sync.wait_ge(*PE_.at("G3", g))
                for t in range(2):
                    sync.dma_start(hres[t], x_rows[bass.ds(g * GT + t * P, P), :]).then_inc(hres_in[t], 16)
                for t in range(TT):
                    sync.wait_ge(*V_.at(f"h{t}", g))
                    sync.dma_start(h_dram[bass.ds(g * GT + t * P, P), :], hres[t % 2]).then_inc(h_out[t % 2], 16)
                    sync.wait_ge(*V_.at(f"hn{t}", g))
                    sync.dma_start(hn_dram[bass.ds(g * GT + t * P, P), :], hn2[t % 2]).then_inc(h_out[t % 2], 16)
                    if t + 2 < TT:
                        sync.wait_ge(h_out[t % 2], 64 * g + 32)
                        sync.dma_start(hres[t % 2], x_rows[bass.ds(g * GT + (t + 2) * P, P), :]).then_inc(hres_in[t % 2], 16)
                for i in range(2):
                    sync.wait_ge(h_out[i], 64 * (g + 1))
                sync.sem_inc(rows_stored, 1)
            for t in range(TT):
                sync.wait_ge(x_in[t], 16 * (GROUPS + 1))
            for i in range(W_BUF):
                sync.wait_ge(wring_in[i], 16 * (PER_BUF * GROUPS + 1))

        @block.gpsimd
        def _(pool):
            nc.gpsimd.memset(bd[:], 0.0).then_inc(prep, 1)
            nc.gpsimd.memset(ident[:], 0.0).then_inc(consts_made, 1)
            nc.gpsimd.memset(ones[:], 1.0).then_inc(consts_made, 1)
            nc.gpsimd.memset(attmask, 1.0).then_inc(consts_made, 1)
            nc.gpsimd.memset(restart[:], 1.0).then_inc(consts_made, 1)
            pool.wait_ge(consts_made, 4)
            nc.gpsimd.memset(restart[:].rearrange("p (n c) -> p n c", c=CHUNK)[:, :, 0:1], 0.0).then_inc(consts_made, 1)
            nc.gpsimd.affine_select(out=ident[:], in_=ident[:], compare_op=ALU.not_equal, fill=1.0, base=0,
                                    pattern=[[-1, P]], channel_multiplier=1).then_inc(consts_made, 1)
            am = attmask.rearrange("p (h i) -> p h i", h=HEADS)
            nc.gpsimd.affine_select(out=am, in_=am, compare_op=ALU.is_ge, fill=0.0, base=0,
                                    pattern=[[0, HEADS], [1, P]], channel_multiplier=-1).then_inc(consts_made, 1)
            pool.wait_ge(consts_made, 7)
            nc.gpsimd.memset(am[0:CHUNK, :, CHUNK:P], 0.0).then_inc(consts_made, 1)
            def const(dst, src, signal=late_in):
                pool.dma_start(dst, src, allow_slow_non_contiguous=True).then_inc(signal, 16)

            pool.wait_ge(prep, 1)
            for i, w in enumerate(("w_rg_a", "w_rg_x")):
                for b in range(2):
                    src = T[w][0].rearrange("(c b) i j -> b i c j", b=2)[b]
                    const(bd[b * 64:(b + 1) * 64, i, :, b * 64:(b + 1) * 64], src)
            const(wrt[:, :, 0:NG], T["w_router_group"][0].rearrange("(k p) n -> p k n", p=P))
            const(wrt[:, :, NG:NR], T["w_router_expert"][0].rearrange("(k p) n -> p k n", p=P))
            const(rbias[:, 0:NG], T["b_router_group"].partition_broadcast(P))
            const(rbias[:, NG:NR], T["b_router_expert"].partition_broadcast(P))
            const(wout[:], T["w_out"][0].rearrange("(k p) n -> p k n", p=P), wout_in)
            for rows in (h_dram, hn_dram):
                const(rows[SEQ:SEQ + P, :], x_rows[0:P], pad_in)
            with pool.Fori(0, GROUPS) as g:
                for i in range(NU):
                    pool.wait_ge(hi_made, NU * g + i + 1)
                    pool.sem_inc(passed_g, 1)
                    nc.gpsimd.tensor_tensor(flat(wlo, i), flat(raw, i), flat(whi, i).bitcast(F32), ALU.subtract).then_inc(lo_made, 1)
            pool.wait_ge(pad_in, 32)

        @block.scalar
        def _(act):
            A = A_

            def own():
                act.wait_ge(*A.now())

            def softplus():
                act.wait_ge(first_in, 32)
                nc.scalar.activation(sp[:, 0], lam[:], ACT.Abs).then_inc(*A.tick("p0"))
                own()
                nc.scalar.activation(sp[:, 1], sp[:, 0], ACT.Exp, scale=-1.0).then_inc(*A.tick("p1"))
                own()
                nc.scalar.activation(sp[:, 2], sp[:, 1], ACT.Ln, bias=1.0).then_inc(*A.tick("p2"))

            def norm_stats(n):
                for t in range(TT):
                    act.wait_ge(x_in[t], 16 * (n + 1))
                    if t:
                        act.wait_ge(hn_stat, (TT + 1) * n + t)
                    nc.scalar.activation(junk, xs[:, t], ACT.Square, accum_out=stat[:, t:t + 1]).then_inc(hn_stat, 1)
                act.wait_ge(hn_rs, 2 * n + 1)
                nc.scalar.activation(stat[:, 8:12], stat[:, 4:8], ACT.Sqrt).then_inc(hn_stat, 1)

            def split(i, g=0):
                act.wait_ge(wring_in[i % W_BUF], 16 * (PER_BUF * g + i // W_BUF + 1))
                if i >= W_BUF:
                    act.wait_ge(*PE_.at(f"u{i-W_BUF}", g))
                nc.scalar.activation(flat(whi, i), flat(raw, i), ACT.Copy).then_inc(hi_made, 1)

            softplus()
            norm_stats(0)
            for i in range(W_BUF):
                split(i)

            act.wait_ge(*V_.before("sp"))
            with act.Fori(0, GROUPS) as g:
                A.begin_loop(g)

                def empty(name, dst, **kw):
                    i = ORDER.index(name)
                    func = kw.pop("func", ACT.Copy)
                    act.wait_ge(*PE_.at(name, g))
                    own()
                    nc.scalar.activation(dst, kw.pop("src", big[i % 4][:]), func, **kw).then_inc(*A.tick(kw_name(name)))

                def kw_name(name):
                    return "e:" + name if EMPTIED_BY[name] == "A" else "a:" + name

                for k in range(KT):
                    if k == 2:
                        act.wait_ge(rows_stored, g + 1)
                    empty(f"T{k}", hhi[:, k], scale=nmix[:, k:k + 1])
                for c in range(CT):
                    empty(f"X{c}", xr[:, c, CONV - 1:])
                    split(c + 3, g)
                act.wait_ge(consts_in, 16 * N_CONST)
                empty("AL", alow, src=big[ORDER.index("AL") % 4][0:RANK, :])
                for i in range(7, 11):
                    split(i, g)
                for t in range(TT):
                    empty(f"V{t}", vt[:, t])
                split(11, g)
                for c in range(HP):
                    empty(f"L{c}", z1[:, c], func=ACT.Abs, bias=bal[:, c:c + 1])
                own()
                nc.scalar.activation(z1, z1, ACT.Exp, scale=-1.0).then_inc(*A.tick())
                own()
                nc.scalar.activation(z1, z1, ACT.Ln, bias=1.0).then_inc(*A.tick("ln"))

                def gates(c):
                    if c:
                        act.wait_ge(*V_.at(f"scan{c-1}", g))
                    empty(f"GA{c}", rt, func=ACT.Sigmoid, bias=gb[:, 0, c:c + 1])
                    empty(f"GX{c}", it, func=ACT.Sigmoid, bias=gb[:, 1, c:c + 1])
                    own()
                    nc.scalar.activation(at_, rt, ACT.Exp, scale=sp[:, 0, c:c + 1]).then_inc(*A.tick())
                    nc.scalar.activation(th, rt, ACT.Tanh, scale=sp[:, 3, c:c + 1]).then_inc(*A.tick(f"th{c}"))

                def gates_root(c):
                    act.wait_ge(*V_.at(f"oma{c}", g))
                    own()
                    nc.scalar.activation(th, th, ACT.Sqrt).then_inc(*A.tick(f"sq{c}"))

                def attended(t):
                    act.wait_ge(*PE_.at(f"o{t}", g))
                    nc.scalar.activation(ot[:, t], op[:], ACT.Copy).then_inc(*A.tick(f"o{t}"))
                    for h in range(HEADS):
                        if h % 2 == 0:
                            own()
                        j = 32 + t * HEADS + h
                        nc.scalar.activation(osq[:, h % 2], ot[:, t, h * DV:(h + 1) * DV],
                                             ACT.Square, accum_out=stat[:, j:j + 1]).then_inc(*A.tick(f"os{t}" if h == HEADS - 1 else None))

                def root(name, cols):
                    act.wait_ge(*V_.at(name, g))
                    own()
                    nc.scalar.activation(cols, cols, ACT.Sqrt).then_inc(*A.tick("rt:" + name))

                def silu(t):
                    empty(f"G{t}", sg[:, t], func=ACT.Sigmoid)

                def turned(t):
                    empty(f"YT{t}", yT[:, :, t * P:(t + 1) * P], scale=glan[:], src=big[ORDER.index(f"YT{t}") % 4][:].rearrange("p (h t) -> p h t", h=HEADS))

                gates(0)
                split(12, g)
                gates_root(0)
                split(13, g)
                act.wait_ge(*V_.at("b", g))
                own()
                nc.scalar.activation(z1, bb[:], ACT.Exp, scale=1.0 / GATE_NORM).then_inc(*A.tick("eb"))
                nc.scalar.activation(z2, bb[:], ACT.Exp, scale=-1.0 / GATE_NORM).then_inc(*A.tick("enb"))
                last = bb[:].rearrange("p a (n c) -> p a n c", c=CHUNK)[:, :, :, CHUNK - 1]
                nc.scalar.activation(dc[:], last, ACT.Exp, scale=1.0 / GATE_NORM).then_inc(*A.tick("dc"))
                split(14, g)
                split(15, g)
                act.wait_ge(*V_.at("bend", g))
                own()
                nc.scalar.activation(z1, z1, ACT.Exp, scale=1.0 / GATE_NORM).then_inc(*A.tick("eend"))
                gates(1)
                for c in range(2):
                    empty(f"Y{c}", yr[:, c], func=ACT.Gelu_apprx_tanh)
                    split(16 + c, g)
                gates_root(1)
                gates(2)
                empty("Y2", yr[:, 2], func=ACT.Gelu_apprx_tanh)
                split(18, g)
                gates_root(2)
                attended(0)
                empty("Y3", yr[:, 3], func=ACT.Gelu_apprx_tanh)
                split(19, g)
                gates(3)
                split(20, g)
                gates_root(3)
                attended(1)
                split(21, g)
                for c in range(CT):
                    act.wait_ge(*V_.at(f"y{c}", g))
                    own()
                    nc.scalar.activation(xc[:, c], yr[:, c], ACT.Square).then_inc(*A.tick(f"ysq{c}"))
                root("yms", uu)
                split(22, g)
                attended(2)
                root("oms2", stat[:, 48:60])
                for t in range(TT):
                    silu(t)
                split(23, g)
                turned(0)
                attended(3)
                turned(1)
                root("oms3", stat[:, 60:64])
                norm_stats(g + 1)
                turned(2)
                for t in range(TT + 1):
                    if t:
                        empty(f"H{t-1}0", hn2T[:, 0:4], src=big[ORDER.index(f"H{t-1}0") % 4][:].rearrange("p (k t) -> p k t", k=4))
                    if t == 1:
                        turned(3)
                    if t < TT:
                        act.wait_ge(*V_.at(f"h{t}", g))
                        own()
                        nc.scalar.activation(junk, hres[t % 2], ACT.Square, accum_out=stat[:, 16 + t:17 + t]).then_inc(*A.tick(f"hsq{t}"))
                        root(f"hms{t}", stat[:, 20 + t:21 + t])
                tables["A"] = A.table()

        @block.vector
        def _(dve):
            V = V_

            def own():
                dve.wait_ge(*V.now())

            def op1(name, fn, *a, **k):
                own()
                fn(*a, **k).then_inc(*V.tick(name))

            nc.vector.memset(xr[:, :, 0:CONV - 1], 0.0).then_inc(*V.tick())
            nc.vector.memset(hcar[:], 0.0).then_inc(*V.tick())
            nc.vector.memset(att[:], 0.0).then_inc(*V.tick())
            nc.vector.memset(st[:], 0.0).then_inc(*V.tick("zeroed"))
            dve.wait_ge(consts_made, 8)
            nc.vector.tensor_copy(keepm[:], attmask).then_inc(*V.tick())
            def norm_rows(n):
                dve.wait_ge(hn_stat, (TT + 1) * n + TT)
                if not isinstance(n, int):
                    dve.wait_ge(hn_ready, TT * n)
                nc.vector.tensor_scalar(stat[:, 4:8], stat[:, 0:4], 1.0 / D, EPS, ALU.mult, ALU.add).then_inc(hn_rs, 1)
                dve.wait_ge(hn_stat, (TT + 1) * (n + 1))
                nc.vector.reciprocal(stat[:, 12:16], stat[:, 8:12]).then_inc(hn_rs, 1)
                dve.wait_ge(hn_rs, 2 * n + 2)
                for t in range(TT):
                    nc.vector.tensor_scalar(xs[:, t], xs[:, t], stat[:, 12 + t:13 + t], None, ALU.mult).then_inc(hn_ready, 1)

            norm_rows(0)
            dve.sem_inc(group_done, 1)
            dve.wait_ge(*A_.before("p2"))
            nc.vector.tensor_scalar(sp[:, 1], lam[:], -1.0, 0.0, ALU.mult, ALU.max).then_inc(*V.tick())
            own()
            nc.vector.tensor_tensor(sp[:, 1], sp[:, 1], sp[:, 2], ALU.add).then_inc(*V.tick())
            own()
            nc.vector.tensor_scalar(sp[:, 0], sp[:, 1], -C_RG, None, ALU.mult).then_inc(*V.tick())
            nc.vector.tensor_scalar(sp[:, 3], sp[:, 1], C_RG, None, ALU.mult).then_inc(*V.tick("sp"))
            with dve.Fori(0, GROUPS) as g:
                V.begin_loop(g)

                def result(name):
                    dve.wait_ge(*PE_.at(name, g))
                    own()
                    return big[ORDER.index(name) % 4]

                for k in range(KT):
                    if k == 2:
                        dve.wait_ge(rows_stored, g + 1)
                    dve.wait_ge(*A_.at(f"a:T{k}", g))
                    b = result(f"T{k}")
                    nc.vector.scalar_tensor_tensor(hlo[:, k], b[:], nmix[:, k:k + 1], hhi[:, k].bitcast(F32), ALU.mult, ALU.subtract).then_inc(*V.tick(f"e:T{k}"))
                dve.wait_ge(consts_in, 16 * N_CONST)
                for c in range(CT):
                    dve.wait_ge(*A_.at(f"e:X{c}", g))
                    own()
                    nc.vector.tensor_scalar(xc[:, c], xr[:, c, 0:GT], cw[:, c, 0:1], cb[:, c:c + 1], ALU.mult, ALU.add).then_inc(*V.tick())
                    for j in range(1, CONV):
                        own()
                        nc.vector.scalar_tensor_tensor(xc[:, c], xr[:, c, j:j + GT], cw[:, c, j:j + 1], xc[:, c],
                                                       ALU.mult, ALU.add).then_inc(*V.tick(f"xc{c}" if j == CONV - 1 else None))
                own()
                nc.vector.tensor_copy(xr[:, :, 0:CONV - 1], xr[:, :, GT:GT + CONV - 1]).then_inc(*V.tick("halo"))
                for c in range(HP):
                    b = result(f"L{c}")
                    dve.wait_ge(*A_.at(f"a:L{c}", g))
                    nc.vector.tensor_scalar(z2[:, c], b[:], bal[:, c:c + 1], 0.0, ALU.add, ALU.min).then_inc(*V.tick(f"e:L{c}"))
                dve.wait_ge(*A_.at("ln", g))
                own()
                nc.vector.tensor_tensor(z2, z2, z1, ALU.subtract).then_inc(*V.tick())
                for c in range(HP):
                    own()
                    nc.vector.tensor_tensor_scan(bb[:, c], restart[:], z2[:, c], 0.0, ALU.mult, ALU.add).then_inc(*V.tick("b" if c == HP - 1 else None))

                def rg_first(c):
                    dve.wait_ge(*A_.at(f"th{c}", g))
                    own()
                    nc.vector.tensor_scalar(uu, th, 1.0, None, ALU.add).then_inc(*V.tick())
                    own()
                    nc.vector.reciprocal(uu, uu).then_inc(*V.tick())
                    own()
                    nc.vector.scalar_tensor_tensor(th, th, 2.0, uu, ALU.mult, ALU.mult).then_inc(*V.tick(f"oma{c}"))
                    own()
                    nc.vector.tensor_tensor(it, it, xc[:, c], ALU.mult).then_inc(*V.tick())

                def rg(c):
                    dve.wait_ge(*A_.at(f"sq{c}", g))
                    own()
                    nc.vector.tensor_tensor(uu, th, it, ALU.mult).then_inc(*V.tick())
                    own()
                    nc.vector.tensor_tensor_scan(xc[:, c], at_, uu, hcar[:, c:c + 1], ALU.mult, ALU.add).then_inc(*V.tick(f"scan{c}"))
                    own()
                    nc.vector.tensor_copy(hcar[:, c:c + 1], xc[:, c, GT - 1:GT]).then_inc(*V.tick())

                def keep(t):
                    dve.wait_ge(*PE_.at(f"att{t}", g))
                    if t >= 2:
                        dve.wait_ge(*PE_.at(f"o{t-2}", g))
                    own()
                    dve.sem_inc(passed_v, 1)
                    nc.vector.copy_predicated(att[:, t % 2], keepm[:], attp[t % 2][:]).then_inc(*V.tick(f"keep{t}"))

                def state(j):
                    t, ch = divmod(j - 1, 2)
                    dve.wait_ge(*PE_.at(f"kv{t}", g))
                    if ch:
                        dve.wait_ge(*PE_.at(f"oc{t}", g))
                    elif t:
                        dve.wait_ge(*PE_.at(f"o{t-1}", g))
                    own()
                    for c in range(HP):
                        nc.vector.scalar_tensor_tensor(st[:, j % 2, c], st[:, (j + 1) % 2, c], dc[:, c, j - 1:j],
                                                       kvp[:, ch, c], ALU.mult, ALU.add).then_inc(*V.tick(f"st{j}" if c else None))

                def silu(t):
                    b = result(f"G{t}")
                    dve.wait_ge(*A_.at(f"a:G{t}", g))
                    nc.vector.tensor_tensor(sg[:, t], b[:], sg[:, t], ALU.mult).then_inc(*V.tick(f"e:G{t}"))

                def mean_sq(t):
                    dve.wait_ge(*A_.at(f"os{t}", g))
                    own()
                    nc.vector.tensor_scalar(stat[:, 48 + 4 * t:52 + 4 * t], stat[:, 32 + 4 * t:36 + 4 * t], 1.0 / DV, EPS,
                                            ALU.mult, ALU.add).then_inc(*V.tick(f"oms{t}"))

                def norm_heads(t):
                    dve.wait_ge(*A_.at(f"rt:oms{max(t, 2)}", g))
                    own()
                    nc.vector.reciprocal(stat[:, 48 + 4 * t:52 + 4 * t], stat[:, 48 + 4 * t:52 + 4 * t]).then_inc(*V.tick())
                    own()
                    for h in range(HEADS):
                        cs = slice(h * DV, (h + 1) * DV)
                        j = 48 + t * HEADS + h
                        nc.vector.scalar_tensor_tensor(ot[:, t, cs], ot[:, t, cs], stat[:, j:j + 1], sg[:, t, cs],
                                                       ALU.mult, ALU.mult).then_inc(*V.tick(f"on{t}" if h == HEADS - 1 else None))

                rg_first(0)
                rg(0)
                for i, n in enumerate(("Q0", "Q1", "K0", "K1")):
                    b = result(n)
                    nc.vector.tensor_copy(qk[:, i], b[:]).then_inc(*V.tick("e:" + n))
                dve.wait_ge(*A_.at("enb", g))
                own()
                nc.vector.scalar_tensor_tensor(qk[:, 0:HP], qk[:, 0:HP], DK ** -0.5, z1, ALU.mult, ALU.mult).then_inc(*V.tick("qs"))
                nc.vector.tensor_tensor(ks[:], qk[:, HP:], z2, ALU.mult).then_inc(*V.tick("ks"))
                own()
                for c in range(HP):
                    bc = bb[:, c].rearrange("p (n c) -> p n c", c=CHUNK)
                    nc.vector.tensor_tensor(z1[:, c].rearrange("p (n c) -> p n c", c=CHUNK),
                                            bc[:, :, CHUNK - 1:CHUNK].to_broadcast([P, NCH, CHUNK]), bc,
                                            ALU.subtract).then_inc(*V.tick("bend" if c else None))
                dve.wait_ge(*A_.at("eend", g))
                own()
                nc.vector.tensor_tensor(qk[:, HP:], qk[:, HP:], z1, ALU.mult).then_inc(*V.tick("ke"))
                rg_first(1)
                for q in range(2):
                    b = result(f"KE{q}")
                    nc.vector.tensor_copy(keT[:, 2 * q:2 * q + 2], b[:].rearrange("p (t c) -> p t c", t=2)).then_inc(*V.tick(f"e:KE{q}"))
                rg(1)
                keep(0)
                state(1)
                keep(1)
                rg_first(2)
                state(2)
                rg(2)
                mean_sq(0)
                state(3)
                keep(2)
                rg_first(3)
                rg(3)
                state(4)
                mean_sq(1)
                for c in range(CT):
                    dve.wait_ge(*A_.at(f"e:Y{c}", g))
                    own()
                    nc.vector.tensor_tensor(yr[:, c], xc[:, c], yr[:, c], ALU.mult).then_inc(*V.tick(f"y{c}"))
                state(5)
                keep(3)
                dve.wait_ge(*PE_.at("SS", g))
                own()
                nc.vector.tensor_scalar(uu, attp[0][:], 1.0 / RG, EPS, ALU.mult, ALU.add).then_inc(*V.tick("yms"))
                state(6)
                dve.wait_ge(*A_.at("rt:yms", g))
                own()
                nc.vector.reciprocal(uu, uu).then_inc(*V.tick())
                mean_sq(2)
                silu(0)
                norm_heads(0)
                silu(1)
                state(7)
                silu(2)
                silu(3)
                norm_heads(1)
                own()
                for c in range(CT):
                    nc.vector.scalar_tensor_tensor(yr[:, c], yr[:, c], rgn[:, c:c + 1], uu, ALU.mult, ALU.mult).then_inc(*V.tick("yn" if c == CT - 1 else None))
                state(8)
                norm_heads(2)
                mean_sq(3)
                norm_heads(3)
                norm_rows(g + 1)
                for t in range(TT + 1):
                    for n in range(2):
                        if t < TT:
                            hs = hres[t % 2][:, n * 512:(n + 1) * 512]
                            b = result(f"O{t}{n}")
                            dve.wait_ge(hres_in[t % 2], 32 * g + 16 * (t // 2 + 1))
                            nc.vector.tensor_tensor(hs, b[:], hs, ALU.add).then_inc(*V.tick(f"e:O{t}{n}"))
                            V.marks[f"h{t}"] = V.n
                        if t and n == 0:
                            b = result(f"H{t-1}1")
                            nc.vector.tensor_copy(hn2T[:, 4:8], b[:].rearrange("p (k t) -> p k t", k=4)).then_inc(*V.tick(f"e:H{t-1}1"))
                    if t < TT:
                        dve.wait_ge(*A_.at(f"hsq{t}", g))
                        own()
                        nc.vector.tensor_scalar(stat[:, 20 + t:21 + t], stat[:, 16 + t:17 + t], 1.0 / D, EPS, ALU.mult, ALU.add).then_inc(*V.tick(f"hms{t}"))
                    if t:
                        b = result(f"R{t-1}")
                        nc.vector.tensor_tensor(logits[:, bass.ds(g * TT + t - 1, 1), :], b[:, 0:NR].rearrange("p (a n) -> p a n", a=1),
                                                rbias[:].rearrange("p (a n) -> p a n", a=1),
                                                ALU.add).then_inc(*(V.tick(f"e:R{t-1}") if t < TT else (group_done, 1)))
                    if t < TT:
                        dve.wait_ge(*A_.at(f"rt:hms{t}", g))
                        own()
                        nc.vector.reciprocal(stat[:, 24 + t:25 + t], stat[:, 20 + t:21 + t]).then_inc(*V.tick())
                        own()
                        if t >= 2:
                            dve.wait_ge(h_out[t % 2], 64 * g + 32)
                            dve.wait_ge(*PE_.at(f"H{t-2}1", g))
                        nc.vector.scalar_tensor_tensor(hn2[t % 2], hres[t % 2], stat[:, 24 + t:25 + t], nffn[:], ALU.mult, ALU.mult).then_inc(*V.tick(f"hn{t}"))
                tables["V"] = V.table()

        @block.tensor
        def _(pe):
            pe.wait_ge(consts_made, 8)
            with pe.Fori(0, GROUPS) as g:
                PE_.begin_loop(g)

                def bank(name):
                    i = ORDER.index(name)
                    if i >= 4:
                        E = A_ if EMPTIED_BY[ORDER[i - 4]] == "A" else V_
                        pe.wait_ge(*E.at("e:" + ORDER[i - 4], g))
                    return big[i % 4]

                pe.wait_ge(group_done, g + 1)
                pe.wait_ge(hn_ready, TT * (g + 1))
                for k in range(KT):
                    b = bank(f"T{k}")
                    for t in range(TT):
                        m = nc.tensor.transpose(b[:, t * P:(t + 1) * P], xs[:, t, k * P:(k + 1) * P], ident[:])
                    m.then_inc(*PE_.tick(f"T{k}"))

                def three(out, ahi, alo, bhi, blo, first, last):
                    nc.tensor.matmul(out, ahi, bhi, start=first, stop=False)
                    nc.tensor.matmul(out, ahi, blo, start=False, stop=False)
                    return nc.tensor.matmul(out, alo, bhi, start=False, stop=last)

                def channels(name):
                    i = [u[1] for u in units].index(name)
                    b = bank(name)
                    out = b[0:RANK, :] if name == "AL" else b[:]
                    pe.wait_ge(lo_made, NU * g + i + 1)
                    wh, wl = shaped(whi, i), shaped(wlo, i)
                    for k in range(KT):
                        if name == "X0":
                            pe.wait_ge(*V_.at(f"e:T{k}", g))
                        m = three(out, wh[:, k], wl[:, k], hhi[:, k], hlo[:, k], k == 0, k == KT - 1)
                    m.then_inc(*PE_.tick(name))
                    PE_.marks[f"u{i}"] = PE_.n

                def tokens(n, q):
                    i = [u[1] for u in units].index(n) + q
                    pe.wait_ge(lo_made, NU * g + i + 1)
                    wh, wl = shaped(whi, i), shaped(wlo, i)
                    for t in range(TT):
                        name = f"{n}{t}"
                        b = bank(name) if q == 0 else big[ORDER.index(name) % 4]
                        for k in range(2):
                            kk, ts = 2 * q + k, slice(t * P, (t + 1) * P)
                            m = three(b[:], hhi[:, kk, ts], hlo[:, kk, ts], wh[:, k], wl[:, k], kk == 0, kk == KT - 1)
                        if kk == KT - 1 or t == TT - 1:
                            m.then_inc(*PE_.tick(name if kk == KT - 1 else None))
                    PE_.marks[f"u{i}"] = PE_.n

                def gates(c):
                    for i, n in enumerate((f"GA{c}", f"GX{c}")):
                        b = bank(n)
                        pe.wait_ge(*V_.at(f"xc{c}", g))
                        nc.tensor.matmul(b[:], bd[:, i, c], xc[:, c], start=True, stop=True).then_inc(*PE_.tick(n))

                def decayed_keys(q):
                    b = bank(f"KE{q}")
                    pe.wait_ge(*V_.at("ke", g))
                    for t in range(2):
                        for c in range(HP):
                            tt = 2 * q + t
                            m = nc.tensor.transpose(b[:, (t * HP + c) * P:(t * HP + c + 1) * P],
                                                    qk[:, HP + c, tt * P:(tt + 1) * P], ident[:])
                    m.then_inc(*PE_.tick(f"KE{q}"))

                by_rows = [h for r in range(2) for h in range(r, HEADS, 2)]

                def rows_apart():
                    pe.wait_ge(*PE_.now())
                    pe.sem_inc(passed_p, 1)

                def scores(t):
                    if t >= 2:
                        pe.wait_ge(*V_.at(f"keep{t-2}", g))
                    else:
                        pe.wait_ge(*V_.at("ks", g))
                    for i, h in enumerate(by_rows):
                        if i == HP:
                            m.then_inc(*PE_.tick())
                            rows_apart()
                        r, c = slice(DK * (h % 2), DK * (h % 2) + DK), h // 2
                        m = nc.tensor.matmul(attp[t % 2][:, h * P:(h + 1) * P], ks[r, c, t * P:(t + 1) * P],
                                             qk[r, c, t * P:(t + 1) * P], start=True, stop=True)
                    m.then_inc(*PE_.tick(f"att{t}"))

                def outer(t):
                    pe.wait_ge(*V_.at(f"e:KE{t//2}", g))
                    if t:
                        pe.wait_ge(*V_.at(f"st{2*t}", g))
                    for ch in range(2):
                        for h in range(HEADS):
                            r, c = slice(DK * (h % 2), DK * (h % 2) + DK), h // 2
                            tk = slice(CHUNK * ch, CHUNK * ch + CHUNK)
                            if h == 0:
                                if ch:
                                    m.then_inc(*PE_.tick())
                                rows_apart()
                            m = nc.tensor.matmul(kvp[r, ch, c], keT[tk, t, h * DK:(h + 1) * DK], vt[tk, t, h * DV:(h + 1) * DV],
                                                 start=True, stop=True, skip_group_check=True)
                    m.then_inc(*PE_.tick(f"kv{t}"))

                def attend(t):
                    pe.wait_ge(*V_.at(f"keep{t}", g))
                    if t:
                        pe.wait_ge(*A_.at(f"o{t-1}", g))
                    for h in range(HEADS):
                        cs = slice(h * DV, (h + 1) * DV)
                        m = nc.tensor.matmul(op[:, cs], att[:, t % 2, h * P:(h + 1) * P], vt[:, t, cs],
                                             start=(h == 0), stop=False, skip_group_check=True)
                    for ch in range(2):
                        j = 2 * t + ch
                        if j:
                            pe.wait_ge(*V_.at(f"st{j}", g))
                        m.then_inc(*PE_.tick())
                        rows_apart()
                        for i, h in enumerate(by_rows):
                            if i == HP:
                                m.then_inc(*PE_.tick())
                                rows_apart()
                            r, c = slice(DK * (h % 2), DK * (h % 2) + DK), h // 2
                            tk = slice(CHUNK * ch, CHUNK * ch + CHUNK)
                            m = nc.tensor.matmul(op[tk, h * DV:(h + 1) * DV], qk[r, c, t * P + CHUNK * ch:t * P + CHUNK * (ch + 1)],
                                                 st[r, j % 2, c], start=False, stop=(ch == 1), skip_group_check=True)
                        PE_.marks[f"oc{t}" if ch == 0 else f"o{t}"] = PE_.n + 1
                        if ch == 1:
                            m.then_inc(*PE_.tick())

                def turn_o(t):
                    b = bank(f"YT{t}")
                    pe.wait_ge(*V_.at(f"on{t}", g))
                    for h in range(HEADS):
                        m = nc.tensor.transpose(b[:, h * P:(h + 1) * P], ot[:, t, h * DV:(h + 1) * DV], ident[:])
                    m.then_inc(*PE_.tick(f"YT{t}"))

                def out(t, n):
                    b = bank(f"O{t}{n}")
                    pe.wait_ge(*A_.at(f"e:YT{t}", g))
                    for i, k in enumerate([*range(CT, KT), *range(CT)]):
                        if i == CT:
                            pe.wait_ge(*V_.at("yn", g))
                        y = yr[:, k, t * P:(t + 1) * P] if k < CT else yT[:, k - CT, t * P:(t + 1) * P]
                        m = nc.tensor.matmul(b[:], y, wout[:, k, n * 512:(n + 1) * 512], start=(i == 0), stop=(i == KT - 1))
                    m.then_inc(*PE_.tick(f"O{t}{n}"))

                def turn_rows(t):
                    for q in range(2):
                        b = bank(f"H{t}{q}")
                        pe.wait_ge(*V_.at(f"hn{t}", g))
                        for k in range(4):
                            kk = 4 * q + k
                            m = nc.tensor.transpose(b[:, k * P:(k + 1) * P], hn2[t % 2][:, kk * P:(kk + 1) * P], ident[:])
                        m.then_inc(*PE_.tick(f"H{t}{q}"))

                def router(t):
                    b = bank(f"R{t}")
                    pe.wait_ge(*A_.at(f"e:H{t}0", g))
                    pe.wait_ge(*V_.at(f"e:H{t}1", g))
                    for k in range(KT):
                        m = nc.tensor.matmul(b[:, 0:NR], hn2T[:, k], wrt[:, k], start=(k == 0), stop=(k == KT - 1))
                    m.then_inc(*PE_.tick(f"R{t}"))

                for c in range(CT):
                    channels(f"X{c}")
                channels("AL")
                for q in range(4):
                    tokens("V", q)
                pe.wait_ge(consts_in, 16 * N_CONST)
                pe.wait_ge(late_in, 16 * 8)
                for c in range(HP):
                    b = bank(f"L{c}")
                    pe.wait_ge(*A_.at("e:AL", g))
                    nc.tensor.matmul(b[:], wup[:, c * P:(c + 1) * P], alow, start=True, stop=True).then_inc(*PE_.tick(f"L{c}"))
                gates(0)
                for n in ("Q0", "Q1", "K0", "K1"):
                    channels(n)
                gates(1)
                channels("Y0")
                channels("Y1")
                decayed_keys(0)
                decayed_keys(1)
                gates(2)
                scores(0)
                outer(0)
                scores(1)
                channels("Y2")
                attend(0)
                channels("Y3")
                outer(1)
                scores(2)
                gates(3)
                tokens("G", 0)
                attend(1)
                tokens("G", 1)
                outer(2)
                scores(3)
                pe.wait_ge(*V_.at("keep2", g))
                for c in range(CT):
                    pe.wait_ge(*A_.at(f"ysq{c}", g))
                    m = nc.tensor.matmul(attp[0][:], ones[:], xc[:, c], start=(c == 0), stop=(c == CT - 1))
                m.then_inc(*PE_.tick("SS"))
                tokens("G", 2)
                attend(2)
                tokens("G", 3)
                outer(3)
                turn_o(0)
                attend(3)
                turn_o(1)
                pe.wait_ge(wout_in, 16)
                for t in range(TT + 1):
                    if t < TT:
                        out(t, 0)
                    if t:
                        turn_rows(t - 1)
                    if t < TT:
                        out(t, 1)
                    if t < 2:
                        turn_o(t + 2)
                    if t:
                        router(t - 1)
                tables["P"] = PE_.table()


def route(nc, slot_dram, ident, ones, logits, dest, rows, wts, btab, place_slots, sem):
    with ExitStack() as ctx:
        def sb(name, shape, dt=F32):
            return ctx.enter_context(nc.sbuf_tensor(name, shape, dt))

        earlier = sb("earlier", [P, P])
        gdesc = sb("gdesc", [P, NG])
        edesc = sb("edesc", [P, EPG])
        blk = sb("blk", [P, BLOCKS + 1])
        no_rows = sb("no_rows", [P, SLOTS // P, 2], I32)
        gval = sb("gval", [P, TILES, NG])
        goh = sb("goh", [P, TILES, NG])
        gm = sb("gm", [P, TILES])
        gx = sb("gx", [P, TILES, NG])
        gw = sb("gw", [P, TILES])
        le4 = sb("le4", [P, TILES, NG, EPG])
        le = sb("le", [P, TILES, EPG])
        eval_ = sb("eval", [P, TILES, EPG])
        oh = sb("oh", [P, 2, TILES, EPG])
        m12 = sb("m12", [P, 2, TILES])
        mx = sb("mx", [P, TILES])
        big_oh = sb("big_oh", [P, 2, TILES, NG, EPG])
        both = sb("both", [P, TILES, NE])
        carry = sb("carry", [P, TILES + 1, NE])
        rank = sb("rank", [P, TILES, NE])
        padded = sb("padded", [P, NE])
        padded_i = sb("padded_i", [P, NE], I32)
        pend = sb("pend", [P, NE])
        pstart = sb("pstart", [P, NE])
        prod = sb("prod", [P, TILES, NE])
        destf = sb("destf", [P, TILES, 2])
        cmp = sb("cmp", [P, BLOCKS + 1, NE])
        eno = sb("eno", [P, NE])
        some = sb("some", [P, NE])
        nth = sb("nth", [P, NE])
        pmark = sb("pmark", [P, NE])
        is_nth = sb("is_nth", [P, NE, NE])
        pick = sb("pick", [P, 2, NE, NE])
        picked = sb("picked", [P, 2, NE])
        btf = sb("btf", [P, TABLE])
        rk = ctx.enter_context(nc.psum_tensor("rk", [P, TILES * NE], F32))
        tot = ctx.enter_context(nc.psum_tensor("tot", [P, TILES * NE], F32))

        tables_made = sem("r_tables_made")
        ohs_ready = sem("r_ohs_ready")
        counted = sem("r_counted")
        dve_steps = sem("r_dve_steps")
        exps = sem("r_exps")
        exp_in = sem("r_exp_in")
        dest_ready = sem("r_dest_ready")
        slots_zeroed = sem("r_slots_zeroed")
        no_rows_made = sem("r_no_rows_made")

        block = ctx.enter_context(nc.Block())

        @block.gpsimd
        def _(pool):
            nc.gpsimd.memset(earlier[:], 1.0).then_inc(tables_made, 1)
            nc.gpsimd.iota(no_rows[:, :, 0], [[1, SLOTS // P]], base=0, channel_multiplier=SLOTS // P).then_inc(tables_made, 1)
            nc.gpsimd.iota(no_rows[:, :, 1], [[0, SLOTS // P]], base=0, channel_multiplier=0).then_inc(tables_made, 1)
            nc.gpsimd.iota(gdesc[:], [[-1, NG]], base=NG, channel_multiplier=0,
                           allow_small_or_imprecise_dtypes=True).then_inc(tables_made, 1)
            nc.gpsimd.iota(edesc[:], [[-1, EPG]], base=EPG, channel_multiplier=0,
                           allow_small_or_imprecise_dtypes=True).then_inc(tables_made, 1)
            nc.gpsimd.iota(blk[:], [[1, BLOCKS + 1]], base=0, channel_multiplier=0,
                           allow_small_or_imprecise_dtypes=True).then_inc(tables_made, 1)
            nc.gpsimd.iota(rows[:, :, :, 0], [[P, TILES], [0, 2]], base=0, channel_multiplier=1).then_inc(tables_made, 1)
            nc.gpsimd.iota(eno[:], [[1, NE]], base=0, channel_multiplier=0,
                           allow_small_or_imprecise_dtypes=True).then_inc(tables_made, 1)
            pool.wait_ge(tables_made, 8)
            nc.gpsimd.affine_select(out=earlier[:], in_=earlier[:], compare_op=ALU.is_gt, fill=0.0, base=0,
                                    pattern=[[1, P]], channel_multiplier=-1).then_inc(tables_made, 1)
            pool.wait_ge(dest_ready, 1)
            pool.wait_ge(slots_zeroed, 16)
            place_slots(0, PLACED_EARLY)

        @block.sync
        def _(sync):
            sync.wait_ge(no_rows_made, 1)
            sync.dma_start(slot_dram.rearrange("(p a) o -> p (a o)", p=P), no_rows[:].rearrange("p a o -> p (a o)")).then_inc(slots_zeroed, 16)
            sync.wait_ge(slots_zeroed, 16)

        @block.scalar
        def _(act):
            act.wait_ge(exp_in, 1)
            nc.scalar.activation(gx[:], gx[:], ACT.Exp).then_inc(exps, 1)
            act.wait_ge(exp_in, 2)
            nc.scalar.activation(mx[:], mx[:], ACT.Exp).then_inc(exps, 1)

        @block.vector
        def _(dve):
            n = [0]

            def step(ins, signal=None):
                if signal is not None:
                    ins.then_inc(signal, 1)
                else:
                    n[0] += 1
                    ins.then_inc(dve_steps, 1)
                    dve.wait_ge(dve_steps, n[0])

            def bc(ap, shape):
                return ap.to_broadcast(shape)

            v = nc.vector
            dve.wait_ge(tables_made, 9)
            v.tensor_scalar(no_rows[:, :, 0], no_rows[:, :, 0], P - 1, SEQ, ALU.bitwise_and, ALU.bitwise_or).then_inc(no_rows_made, 1)
            gl = logits[:, :, 0:NG]
            g4 = [P, TILES, NG]
            e8 = [P, TILES, EPG]
            step(v.tensor_reduce(gm[:], gl, AX, ALU.max))
            step(v.tensor_tensor(gx[:], gl, bc(gm[:].unsqueeze(2), g4), ALU.subtract))
            step(v.tensor_scalar(gval[:], gx[:], 0.0, None, ALU.is_equal))
            step(v.tensor_tensor(gval[:], gval[:], bc(gdesc[:].unsqueeze(1), g4), ALU.mult))
            v.tensor_reduce(gw[:], gval[:], AX, ALU.max).then_inc(exp_in, 1)
            dve.wait_ge(exp_in, 1)
            step(v.tensor_tensor(goh[:], gval[:], bc(gw[:].unsqueeze(2), g4), ALU.is_equal))
            dve.wait_ge(exps, 1)
            step(v.tensor_reduce(gw[:], gx[:], AX, ALU.add))
            step(v.reciprocal(gw[:], gw[:]))
            lg = logits[:, :, NG:NR].rearrange("p t (g e) -> p t g e", g=NG)
            for g in range(NG):
                step(v.tensor_tensor(le4[:, :, g], lg[:, :, g], bc(goh[:, :, g:g + 1], e8), ALU.mult))
            step(v.tensor_reduce(le[:], le4[:].rearrange("p t g e -> p t e g"), AX, ALU.add))
            for k in range(2):
                step(v.tensor_reduce(m12[:, k], le[:], AX, ALU.max))
                step(v.tensor_tensor(eval_[:], le[:], bc(m12[:, k].unsqueeze(2), e8), ALU.is_equal))
                step(v.tensor_tensor(eval_[:], eval_[:], bc(edesc[:].unsqueeze(1), e8), ALU.mult))
                step(v.tensor_reduce(mx[:], eval_[:], AX, ALU.max))
                step(v.tensor_tensor(oh[:, k], eval_[:], bc(mx[:].unsqueeze(2), e8), ALU.is_equal))
                if k == 0:
                    step(v.scalar_tensor_tensor(le[:], oh[:, 0], -3.0e38, le[:], ALU.mult, ALU.add))
            v.tensor_tensor(mx[:], m12[:, 1], m12[:, 0], ALU.subtract).then_inc(exp_in, 1)
            dve.wait_ge(exps, 2)
            step(v.tensor_scalar(m12[:, 0], mx[:], 1.0, None, ALU.add))
            step(v.reciprocal(m12[:, 0], m12[:, 0]))
            step(v.tensor_tensor(wts[:, :, 0], m12[:, 0], gw[:], ALU.mult))
            step(v.tensor_tensor(wts[:, :, 1], wts[:, :, 0], mx[:], ALU.mult))
            for k in range(2):
                for g in range(NG):
                    step(v.tensor_tensor(big_oh[:, k, :, g], oh[:, k], bc(goh[:, :, g:g + 1], e8), ALU.mult))
            b0 = big_oh[:, 0].rearrange("p t g e -> p t (g e)")
            b1 = big_oh[:, 1].rearrange("p t g e -> p t (g e)")
            v.tensor_tensor(both[:], b0, b1, ALU.add).then_inc(ohs_ready, 1)
            step(v.memset(carry[:, 0], 0.0))
            dve.wait_ge(counted, 2)
            tt = tot[:].rearrange("p (t e) -> p t e", e=NE)
            for t in range(TILES):
                step(v.tensor_tensor(carry[:, t + 1], tt[:, t], carry[:, t], ALU.add))
            step(v.tensor_tensor(rank[:], rk[:].rearrange("p (t e) -> p t e", e=NE), carry[:, 0:TILES], ALU.add))
            step(v.tensor_scalar(padded_i[:], carry[:, TILES], float(P - 1), None, ALU.add))
            step(v.tensor_scalar(padded_i[:], padded_i[:], 7, None, ALU.logical_shift_right))
            step(v.tensor_copy(padded[:], padded_i[:]))
            step(v.tensor_tensor_scan(pend[:], ones[:, 0:NE], padded[:], 0.0, ALU.mult, ALU.add))
            step(v.tensor_tensor(pstart[:], pend[:], padded[:], ALU.subtract))
            step(v.tensor_scalar(pstart[:], pstart[:], float(P), None, ALU.mult))
            step(v.tensor_tensor(rank[:], rank[:], bc(pstart[:].unsqueeze(1), [P, TILES, NE]), ALU.add))
            for k, b in enumerate((b0, b1)):
                step(v.tensor_tensor(prod[:], rank[:], b, ALU.mult))
                step(v.tensor_reduce(destf[:, :, k], prod[:], AX, ALU.add))
            v.tensor_copy(dest, destf[:]).then_inc(dest_ready, 1)
            step(v.tensor_scalar(some[:], padded[:], 1.0, None, ALU.min))
            step(v.tensor_tensor_scan(nth[:], ones[:, 0:NE], some[:], 0.0, ALU.mult, ALU.add))
            step(v.tensor_copy(btf[:, N_EXP:N_EXP + 1], nth[:, NE - 1:NE]))
            step(v.tensor_copy(btf[:, N_BLOCKS:N_BLOCKS + 1], pend[:, NE - 1:NE]))
            step(v.tensor_scalar(btf[:, LAST_TURN:LAST_TURN + 1], nth[:, NE - 1:NE], -1.0, None, ALU.add))
            step(v.tensor_scalar(pmark[:], some[:], -2.0 * BLOCKS, 2.0 * BLOCKS, ALU.mult, ALU.add))
            step(v.tensor_tensor(pmark[:], pmark[:], pend[:], ALU.add))
            step(v.tensor_tensor(cmp[:], bc(pmark[:].unsqueeze(1), [P, BLOCKS + 1, NE]),
                                 bc(blk[:].unsqueeze(2), [P, BLOCKS + 1, NE]), ALU.is_le))
            step(v.tensor_reduce(btf[:, TURN:TURN + BLOCKS + 1], cmp[:], AX, ALU.add))
            step(v.tensor_scalar(btf[:, TURN:TURN + BLOCKS + 1], btf[:, TURN:TURN + BLOCKS + 1], btf[:, LAST_TURN:LAST_TURN + 1], None, ALU.min))
            step(v.tensor_tensor(nth[:], nth[:], some[:], ALU.mult))
            step(v.tensor_tensor(is_nth[:], bc(nth[:].unsqueeze(1), [P, NE, NE]),
                                 bc(blk[:, 1:NE + 1].unsqueeze(2), [P, NE, NE]), ALU.is_equal))
            for i, of in enumerate((eno, pend)):
                step(v.tensor_tensor(pick[:, i], is_nth[:], bc(of[:].unsqueeze(1), [P, NE, NE]), ALU.mult))
            step(v.tensor_reduce(picked[:], pick[:], AX, ALU.add))
            step(v.tensor_copy(btf[:, EXPERT:EXPERT + NE], picked[:, 0]))
            step(v.memset(btf[:, EXPERT + NE:EXPERT + NE + 1], 0.0))
            step(v.tensor_scalar(btf[:, SPLIT:SPLIT + NE], picked[:, 1], float(UNITS), -float(UNITS), ALU.mult, ALU.add))
            step(v.tensor_copy(btab, btf[:]))

        @block.tensor
        def _(pe):
            pe.wait_ge(tables_made, 9)
            pe.wait_ge(ohs_ready, 1)
            b = both[:].rearrange("p t e -> p (t e)")
            nc.tensor.matmul(rk[:], earlier[:], b, start=True, stop=True).then_inc(counted, 1)
            nc.tensor.matmul(tot[:], ones[:], b, start=True, stop=True).then_inc(counted, 1)


def experts(nc, T, slot_dram, hn_dram, h_dram, ident, btab, place_slots, slots_written, sem):
    KU = 4
    RING = 7
    AHEAD = 2 * RING - UNITS
    STAGE = 4
    UW = KU * 512
    with ExitStack() as ctx:
        def sb(name, shape, dt=F32):
            return ctx.enter_context(nc.sbuf_tensor(name, shape, dt))

        def ps(name, shape):
            return ctx.enter_context(nc.psum_tensor(name, shape, F32))

        raw = sb("raw", [P, RING, 2, UW])
        whi = sb("whi", [P, STAGE, UW], F32R)
        wlo = sb("wlo", [P, STAGE, UW], F32R)
        xg = sb("xg", [P, D])
        idx = sb("idx", [P, 2], I32)
        place = sb("place", [P, 2], I32)
        place_next = sb("place_next", [P, 2], I32)
        weight = place[:, 1:2].bitcast(F32)
        xhi = sb("xhi", [P, KT, P], F32R)
        xlo = sb("xlo", [P, KT, P], F32R)
        hb = sb("hb", [P, D])
        hhi = sb("hhi", [P, KT, P], F32R)
        hlo = sb("hlo", [P, KT, P], F32R)
        ysb = sb("ysb", [P, D])
        gate = [ps(f"gate{n}", [P, 512]) for n in range(2)]
        up = [ps(f"up{n}", [P, 512]) for n in range(2)]
        yp = [ps(f"yp{n}", [P, 512]) for n in range(2)]
        tp = [ps(f"tp{n}", [P, 512]) for n in range(2)]

        w_in = [sem(f"e_w_in{u}") for u in range(UNITS)]
        hi_made = sem("e_hi_made")
        lo_made = sem("e_lo_made")
        stage_free = sem("e_stage_free")
        idx_in = sem("e_idx_in")
        place_kept = sem("e_place_kept")
        next_kept = sem("e_next_kept")
        rows_in = sem("e_rows_in")
        x_turned = sem("e_x_turned")
        x_hi = sem("e_x_hi")
        x_lo = sem("e_x_lo")
        gelu_done = sem("e_gelu_done")
        h_done = sem("e_h_done")
        h_turned = sem("e_h_turned")
        h_hi = sem("e_h_hi")
        h_lo = sem("e_h_lo")
        y_out_a = sem("e_y_copied_act")
        y_out_v = sem("e_y_copied_dve")
        y_stored = sem("e_y_stored")
        passed_g = sem("e_passed_g")
        passed_s = sem("e_passed_s")

        def unit(u):
            if u < 8:
                n, r = divmod(u, 4)
                return ("gate", "up")[r % 2], n, r // 2
            return "down", None, u - 8

        def unit_rows(u, e):
            kind, n, q = unit(u)
            if kind == "down":
                w = T["w_exp_down"][0].rearrange("e (k p) n -> e p k n", p=P)
                return w[bass.ds(e, 1), :, 2 * q:2 * q + 2, :].rearrange("e p k n -> p (e k) n")
            w = T["w_exp_" + kind][0].rearrange("e (k p) n -> e p k n", p=P)
            return w[bass.ds(e, 1), :, KU * q:KU * q + KU, n * 512:(n + 1) * 512].rearrange("e p k n -> p (e k) n")

        def count_of_blocks(eng):
            return eng.value_load(btab[0:1, N_BLOCKS:N_BLOCKS + 1], min_val=1, max_val=BLOCKS)

        def turn_of(eng, b):
            at = slice(TURN + b, TURN + b + 1) if isinstance(b, int) else bass.ds(b + TURN, 1)
            return eng.value_load(btab[0:1, at], min_val=0, max_val=NE - 1)

        def raw_unit(u, turn):
            q = (turn * (UNITS // 2) + u // 2) % RING
            if isinstance(turn, int):
                return raw[:, q, u % 2]
            return raw[:, bass.ds(q, 1), u % 2, :].rearrange("p a f -> p (a f)")

        block = ctx.enter_context(nc.Block())

        @block.sync
        def _(sync):
            n_exp = sync.value_load(btab[0:1, N_EXP:N_EXP + 1], min_val=1, max_val=NE)

            def load(u, e, turn):
                k = 2 if unit(u)[0] == "down" else KU
                sync.dma_start(raw_unit(u, turn).rearrange("p (k n) -> p k n", k=k), unit_rows(u, e)).then_inc(w_in[u], 16)

            first = sync.value_load(btab[0:1, EXPERT:EXPERT + 1], min_val=0, max_val=NE - 1)
            for u in range(UNITS):
                if u >= 2:
                    sync.wait_ge(w_in[u - 2], 16)
                load(u, first, 0)
            second = sync.value_load(btab[0:1, EXPERT + 1:EXPERT + 2], min_val=0, max_val=NE - 1)
            for u in range(AHEAD):
                sync.wait_ge(w_in[u], 16)
                load(u, second, 1)
            with sync.Fori(1, n_exp) as j:
                e = sync.value_load(btab[0:1, bass.ds(j + EXPERT, 1)], min_val=0, max_val=NE - 1)
                after = sync.value_load(btab[0:1, bass.ds(j + (EXPERT + 1), 1)], min_val=0, max_val=NE - 1)
                split_before = sync.value_load(btab[0:1, bass.ds(j + (SPLIT - 1), 1)], min_val=0, max_val=UNITS * BLOCKS)
                for u in range(AHEAD, UNITS + AHEAD):
                    sync.wait_ge(lo_made, split_before + (u - AHEAD + 1))
                    sync.sem_inc(passed_s, 1)
                    sync.wait_ge(w_in[u % UNITS], 16 * j + 16 * (u // UNITS))
                    sync.sem_inc(passed_s, 1)
                    load(u % UNITS, after if u >= UNITS else e, j + u // UNITS)
            for u in range(UNITS):
                sync.wait_ge(w_in[u], 16 * n_exp + (16 if u < AHEAD else 0))
                sync.sem_inc(passed_s, 1)

        @block.gpsimd
        def _(pool):
            n_blocks = count_of_blocks(pool)

            def load_idx(b):
                nc.gpsimd.dma_start(idx[:], slot_dram[bass.ds(b * P, P), :]).then_inc(idx_in, 16)

            def gather(b):
                pool.wait_ge(idx_in, 16 * (b + 1))
                if not isinstance(b, int) or b:
                    pool.wait_ge(x_turned, 2 * b)
                pool.sem_inc(passed_g, 1)
                nc.gpsimd.indirect_dma_start(xg[:], None, hn_dram, bass.IndirectOffsetOnAxis(idx[:, 0:1], 0)).then_inc(rows_in, 16)

            def keep_next(b):
                pool.wait_ge(rows_in, 16 * (b + 1))
                if not isinstance(b, int) or b:
                    pool.wait_ge(place_kept, b)
                pool.sem_inc(passed_g, 1)
                nc.gpsimd.tensor_copy(place_next[:], idx[:]).then_inc(next_kept, 1)
                pool.wait_ge(next_kept, b + 1)

            def keep_place(b):
                pool.sem_inc(passed_g, 1)
                nc.gpsimd.tensor_copy(place[:], place_next[:]).then_inc(place_kept, 1)
                pool.wait_ge(place_kept, b + 1)

            def scatter(b):
                pool.wait_ge(y_out_a, b + 1)
                pool.wait_ge(y_out_v, b + 1)
                pool.sem_inc(passed_g, 1)
                nc.gpsimd.indirect_dma_start(h_dram, bass.IndirectOffsetOnAxis(place[:, 0:1], 0), ysb[:], None, compute_op=ALU.add).then_inc(y_stored, 16)
                pool.wait_ge(y_stored, 16 * (b + 1))

            place_slots(PLACED_EARLY, 2 * TILES)
            pool.wait_ge(slots_written, 16 * 2 * TILES)
            load_idx(0)
            gather(0)
            keep_next(0)
            keep_place(0)
            load_idx(1)
            gather(1)
            keep_next(1)
            load_idx(2)
            with pool.Fori(1, n_blocks) as b:
                gather(b + 1)
                scatter(b - 1)
                keep_place(b)
                keep_next(b + 1)
                load_idx(b + 2)
            scatter(n_blocks - 1)
            pool.wait_ge(idx_in, 16 * (n_blocks + 2))
            pool.sem_inc(passed_g, 1)

        @block.scalar
        def _(act):
            n_blocks = count_of_blocks(act)

            def split(u, b, turn):
                act.wait_ge(w_in[u], 16 * turn + 16)
                act.wait_ge(stage_free, UNITS * b + u + 1)
                nc.scalar.activation(whi[:, u % STAGE], raw_unit(u, turn), ACT.Copy).then_inc(hi_made, 1)

            def x_part(q, b):
                act.wait_ge(x_turned, 2 * b + q + 1)
                nc.scalar.activation(xhi[:, 4 * q:4 * q + 4], tp[q][:].rearrange("p (k t) -> p k t", k=4), ACT.Copy).then_inc(x_hi, 1)

            def gelu(n, b):
                act.wait_ge(stage_free, STAGE + UNITS * b + 4 * (n + 1))
                act.wait_ge(h_turned, 2 * b + 2)
                nc.scalar.activation(hb[:, n * 512:(n + 1) * 512], gate[n][:], ACT.Gelu_apprx_tanh).then_inc(gelu_done, 1)

            def h_part(n, b):
                act.wait_ge(h_turned, 2 + 2 * b + n + 1)
                nc.scalar.activation(hhi[:, 4 * n:4 * n + 4], tp[n][:].rearrange("p (k t) -> p k t", k=4), ACT.Copy).then_inc(h_hi, 1)

            def y_half(b):
                act.wait_ge(stage_free, STAGE + UNITS * (b + 1))
                act.wait_ge(place_kept, b + 1)
                nc.scalar.activation(ysb[:, 0:512], yp[0][:], ACT.Copy, scale=weight).then_inc(y_out_a, 1)

            def body(b, with_y):
                turn = turn_of(act, b)
                split(2, b, turn)
                split(3, b, turn)
                if with_y:
                    y_half(b - 1)
                for u in range(4, 7):
                    split(u, b, turn)
                gelu(0, b)
                split(7, b, turn)
                split(8, b, turn)
                split(9, b, turn)
                h_part(0, b)
                split(10, b, turn)
                gelu(1, b)
                split(11, b, turn)
                h_part(1, b)
                turn = turn_of(act, b + 1)
                split(0, b + 1, turn)
                x_part(0, b + 1)
                split(1, b + 1, turn)
                x_part(1, b + 1)

            nc.scalar.preload_act_table(ACT.Gelu_apprx_tanh)
            turn = turn_of(act, 0)
            split(0, 0, turn)
            split(1, 0, turn)
            x_part(0, 0)
            x_part(1, 0)
            body(0, False)
            with act.Fori(1, n_blocks) as b:
                body(b, True)
            y_half(n_blocks - 1)

        @block.vector
        def _(dve):
            n_blocks = count_of_blocks(dve)

            def split(u, b, turn):
                dve.wait_ge(hi_made, UNITS * b + u + 1)
                nc.vector.tensor_tensor(wlo[:, u % STAGE], raw_unit(u, turn), whi[:, u % STAGE].bitcast(F32), ALU.subtract).then_inc(lo_made, 1)

            def x_part(q, b):
                dve.wait_ge(x_hi, 2 * b + q + 1)
                nc.vector.tensor_tensor(xlo[:, 4 * q:4 * q + 4], tp[q][:].rearrange("p (k t) -> p k t", k=4),
                                        xhi[:, 4 * q:4 * q + 4].bitcast(F32), ALU.subtract).then_inc(x_lo, 1)

            def h_half(n, b):
                dve.wait_ge(gelu_done, 2 * b + n + 1)
                hs = hb[:, n * 512:(n + 1) * 512]
                nc.vector.tensor_tensor(hs, up[n][:], hs, ALU.mult).then_inc(h_done, 1)

            def h_part(n, b):
                dve.wait_ge(h_hi, 2 * b + n + 1)
                nc.vector.tensor_tensor(hlo[:, 4 * n:4 * n + 4], tp[n][:].rearrange("p (k t) -> p k t", k=4),
                                        hhi[:, 4 * n:4 * n + 4].bitcast(F32), ALU.subtract).then_inc(h_lo, 1)

            def y_half(b):
                dve.wait_ge(stage_free, STAGE + UNITS * (b + 1))
                dve.wait_ge(place_kept, b + 1)
                nc.vector.tensor_scalar(ysb[:, 512:D], yp[1][:], weight, None, ALU.mult).then_inc(y_out_v, 1)

            def body(b, with_y):
                turn = turn_of(dve, b)
                split(2, b, turn)
                split(3, b, turn)
                if with_y:
                    y_half(b - 1)
                for u in range(4, 7):
                    split(u, b, turn)
                h_half(0, b)
                split(7, b, turn)
                split(8, b, turn)
                split(9, b, turn)
                h_part(0, b)
                split(10, b, turn)
                h_half(1, b)
                split(11, b, turn)
                h_part(1, b)
                turn = turn_of(dve, b + 1)
                split(0, b + 1, turn)
                x_part(0, b + 1)
                split(1, b + 1, turn)
                x_part(1, b + 1)

            turn = turn_of(dve, 0)
            split(0, 0, turn)
            split(1, 0, turn)
            x_part(0, 0)
            x_part(1, 0)
            body(0, False)
            with dve.Fori(1, n_blocks) as b:
                body(b, True)
            y_half(n_blocks - 1)

        @block.tensor
        def _(pe):
            n_blocks = count_of_blocks(pe)

            def turn_x(q, b):
                pe.wait_ge(rows_in, 16 * (b + 1))
                if not isinstance(b, int):
                    pe.wait_ge(h_lo, 2 * (b - 1) + q + 1)
                for k in range(4):
                    kk = 4 * q + k
                    m = nc.tensor.transpose(tp[q][:, k * P:(k + 1) * P], xg[:, kk * P:(kk + 1) * P], ident[:])
                m.then_inc(x_turned, 1)

            def turn_h(n, b):
                pe.wait_ge(h_done, 2 * b + n + 1)
                for k in range(4):
                    m = nc.tensor.transpose(tp[n][:, k * P:(k + 1) * P], hb[:, (4 * n + k) * P:(4 * n + k + 1) * P], ident[:])
                m.then_inc(h_turned, 1)

            def three(out, ahi, alo, u, col, first, last):
                s = slice(col * 512, (col + 1) * 512)
                nc.tensor.matmul(out, ahi, whi[:, u % STAGE, s], start=first, stop=False)
                nc.tensor.matmul(out, ahi, wlo[:, u % STAGE, s], start=False, stop=False)
                return nc.tensor.matmul(out, alo, whi[:, u % STAGE, s], start=False, stop=last)

            def run_unit(u, b):
                kind, n, q = unit(u)
                pe.wait_ge(lo_made, UNITS * b + u + 1)
                if kind == "down":
                    if u == 8:
                        pe.wait_ge(place_kept, b + 1)
                    for k in range(2):
                        kk = 2 * q + k
                        for nn in range(2):
                            m = three(yp[nn][:], hhi[:, kk], hlo[:, kk], u, 2 * k + nn, kk == 0, kk == KT - 1)
                else:
                    out = (gate if kind == "gate" else up)[n]
                    for k in range(KU):
                        kk = KU * q + k
                        m = three(out[:], xhi[:, kk], xlo[:, kk], u, k, kk == 0, kk == KT - 1)
                return m

            pe.sem_inc(stage_free, STAGE)
            pe.sem_inc(h_turned, 2)
            turn_x(0, 0)
            turn_x(1, 0)
            with pe.Fori(0, n_blocks) as b:
                for u in range(UNITS):
                    if u in (0, 2):
                        pe.wait_ge(x_lo, 2 * b + 1 + u // 2)
                    if u == 8:
                        pe.wait_ge(h_lo, 2 * b + 1)
                    if u == 10:
                        pe.wait_ge(h_lo, 2 * b + 2)
                    run_unit(u, b).then_inc(stage_free, 1)
                    if u == 5:
                        turn_h(0, b)
                    if u == 8:
                        turn_h(1, b)
                    if u == 9:
                        turn_x(0, b + 1)
                    if u == 10:
                        turn_x(1, b + 1)


def finish(nc, T, h_dram, out_rows, sem):
    BUF = 6
    with ExitStack() as ctx:
        def sb(name, shape, dt=F32):
            return ctx.enter_context(nc.sbuf_tensor(name, shape, dt))

        h = sb("c_h", [P, BUF, D])
        sq = sb("c_sq", [P, D])
        o = sb("c_o", [P, BUF, D])
        nf = sb("c_nf", [P, D])
        stt = sb("c_st", [P, 4 * TILES])
        nf_in = sem("c_nf_in")
        h_in = [sem(f"c_h_in{i}") for i in range(BUF)]
        out_st = [sem(f"c_out{i}") for i in range(BUF)]
        sq_done = sem("c_sq_done")
        mean_done = sem("c_mean_done")
        rt_done = sem("c_rt_done")
        inv_done = sem("c_inv_done")
        o_done = sem("c_o_done")

        block = ctx.enter_context(nc.Block())

        @block.sync
        def _(sync):
            for t in range(TILES):
                if t >= BUF:
                    sync.wait_ge(o_done, t - BUF + 1)
                sync.dma_start(h[:, t % BUF], h_dram[t * P:(t + 1) * P, :]).then_inc(h_in[t % BUF], 16)
                if t == 0:
                    sync.dma_start(nf[:], T["norm_final"].rearrange("(a d) -> a d", a=1).partition_broadcast(P)).then_inc(nf_in, 16)

        @block.gpsimd
        def _(pool):
            for t in range(TILES):
                i = t % BUF
                pool.wait_ge(o_done, t + 1)
                pool.dma_start(out_rows[t * P:(t + 1) * P, :], o[:, i]).then_inc(out_st[i], 16)
            for i in range(BUF):
                pool.wait_ge(out_st[i], 16 * len(range(i, TILES, BUF)))

        @block.scalar
        def _(act):
            for t in range(TILES):
                act.wait_ge(h_in[t % BUF], 16 * (t // BUF + 1))
                if t:
                    act.wait_ge(sq_done, t)
                nc.scalar.activation(sq[:], h[:, t % BUF], ACT.Square, accum_out=stt[:, t:t + 1]).then_inc(sq_done, 1)
                act.wait_ge(mean_done, t + 1)
                nc.scalar.activation(stt[:, 2 * TILES + t:2 * TILES + t + 1], stt[:, TILES + t:TILES + t + 1], ACT.Sqrt).then_inc(rt_done, 1)

        @block.vector
        def _(dve):
            dve.wait_ge(nf_in, 16)
            for t in range(TILES):
                i = t % BUF
                c = lambda q: stt[:, q * TILES + t:q * TILES + t + 1]
                dve.wait_ge(sq_done, t + 1)
                nc.vector.tensor_scalar(c(1), c(0), 1.0 / D, EPS, ALU.mult, ALU.add).then_inc(mean_done, 1)
                dve.wait_ge(rt_done, t + 1)
                nc.vector.reciprocal(c(3), c(2)).then_inc(inv_done, 1)
                dve.wait_ge(inv_done, t + 1)
                if t >= BUF:
                    dve.wait_ge(out_st[i], 16 * (t // BUF))
                nc.vector.scalar_tensor_tensor(o[:, i], h[:, i], c(3), nf[:], ALU.mult, ALU.mult).then_inc(o_done, 1)


_INS = ["x", "norm_mix", "w_in", "conv_w", "conv_b", "w_rg_a", "b_rg_a", "w_rg_x", "b_rg_x", "rg_lambda",
        "rg_norm", "w_alpha_up", "b_alpha", "gla_norm", "w_out", "norm_ffn", "w_router_group",
        "b_router_group", "w_router_expert", "b_router_expert", "w_exp_gate", "w_exp_up", "w_exp_down",
        "norm_final"]


def kernel(**inputs):
    import numpy as np
    import concourse.bacc as bacc
    from concourse.bass_utils import run_bass_kernel_spmd

    arrays = {n: np.ascontiguousarray(inputs[n]) for n in _INS}
    known = {}
    for _ in range(2):
        nc = bacc.Bacc("TRN2", target_bir_lowering=False, num_devices=1)
        T = {n: nc.dram_tensor(f"in_{n}", a.shape, mybir.dt.from_np(a.dtype), kind="ExternalInput").ap()
             for n, a in arrays.items()}
        T["out"] = nc.dram_tensor("out_0", (1, SEQ, D), F32, kind="ExternalOutput").ap()
        known = build(nc, T, known)
    r = run_bass_kernel_spmd(nc, [{f"in_{n}": a for n, a in arrays.items()}], core_ids=[0])
    return r.results[0]["out_0"]
```
